# Optimizing a Trainium2 kernel written in Bass

```python
import jax, jax.numpy as jnp
from jax import lax
import numpy as np

D_MODEL = 1024
BATCH = 1
SEQ = 512
DEPTH = 2

GRID_W = 64
CTX_LEN = 256
HEAD_DIM = 64
A_HEADS = 8
A_KV_HEADS = 2
A_WIDTH = A_HEADS * HEAD_DIM
A_KV_WIDTH = A_KV_HEADS * HEAD_DIM
Q_BLOCK = 128
ROPE_BASE = 10000.0
B_HEADS = 4
B_WIDTH = B_HEADS * HEAD_DIM
DECAY_LORA = 64
AAA_LORA = 64
GATE_LORA = 128
LNX_EPS = 64e-5
C_HEADS = 4
C_WIDTH = C_HEADS * HEAD_DIM
WIN_ROWS = 8
WIN_COLS = 16
D_MIX = A_WIDTH + B_WIDTH + C_WIDTH
IN_SIZES = (A_WIDTH, A_KV_WIDTH, A_KV_WIDTH,
            B_WIDTH, B_WIDTH, B_WIDTH, 2 * DECAY_LORA, 2 * AAA_LORA, GATE_LORA,
            C_WIDTH, C_WIDTH, C_WIDTH)
N_IN = A_WIDTH + 2 * A_KV_WIDTH + 3 * B_WIDTH + 2 * DECAY_LORA + 2 * AAA_LORA + GATE_LORA + 3 * C_WIDTH
N_EXPERTS = 16
CAPACITY_FACTOR = 2
D_EXPERT = 1024
NORM_EPS = 1e-6

kernel_name = "hybrid_flow_gqa_rwkv7_natten_ecmoe"

def rms_norm(x, g, eps=NORM_EPS):
    xf = x.astype(jnp.float32)
    y = xf * lax.rsqrt(jnp.mean(xf * xf, axis=-1, keepdims=True) + eps)
    return (y * g.astype(jnp.float32)).astype(x.dtype)

def modulate(h, shift, scale):
    return h * (1 + scale) + shift

def rope_1d(x, pos):
    half = x.shape[-1] // 2
    inv = ROPE_BASE ** (-jnp.arange(half, dtype=jnp.float32) / half)
    ang = pos.astype(jnp.float32)[:, None] * inv[None, :]
    cos, sin = jnp.cos(ang)[:, None, :], jnp.sin(ang)[:, None, :]
    xf = x.astype(jnp.float32)
    x1, x2 = xf[..., :half], xf[..., half:]
    return jnp.concatenate([x1 * cos - x2 * sin, x2 * cos + x1 * sin], axis=-1).astype(x.dtype)

def rope_2d(x, row, col):
    h = x.shape[-1] // 2
    return jnp.concatenate([rope_1d(x[..., :h], row), rope_1d(x[..., h:], col)], axis=-1)

def gqa_attend(q, k, v):
    s = jnp.einsum('bmkgd,bskd->bkgms', q, k).astype(jnp.float32) * (HEAD_DIM ** -0.5)
    p = jax.nn.softmax(s, axis=-1).astype(v.dtype)
    return jnp.einsum('bkgms,bskd->bmkgd', p, v)

def mixer_grid_attention(q, k, v, q_gain, k_gain, n_ctx, need_ctx):
    B_, T, _ = q.shape
    n = T - n_ctx
    G = A_HEADS // A_KV_HEADS
    q = rms_norm(q.reshape(B_, T, A_HEADS, HEAD_DIM), q_gain)
    k = rms_norm(k.reshape(B_, T, A_KV_HEADS, HEAD_DIM), k_gain)
    v = v.reshape(B_, T, A_KV_HEADS, HEAD_DIM)
    pos = jnp.arange(n)
    row, col = pos // GRID_W, pos % GRID_W
    q_l = rope_2d(q[:, n_ctx:], row, col)
    k_l = rope_2d(k[:, n_ctx:], row, col)
    q_c, k_c, v_c, v_l = q[:, :n_ctx], k[:, :n_ctx], v[:, :n_ctx], v[:, n_ctx:]
    keys = jnp.concatenate([k_l, k_c], axis=1)
    vals = jnp.concatenate([v_l, v_c], axis=1)
    nb = n // Q_BLOCK
    qb = q_l.reshape(B_, nb, Q_BLOCK, A_KV_HEADS, G, HEAD_DIM).swapaxes(0, 1)
    o_l = lax.map(lambda qq: gqa_attend(qq, keys, vals), qb)
    o_l = o_l.swapaxes(0, 1).reshape(B_, n, A_WIDTH)
    o_c = None
    if need_ctx:
        o_c = gqa_attend(q_c.reshape(B_, n_ctx, A_KV_HEADS, G, HEAD_DIM), k_c, v_c).reshape(B_, n_ctx, A_WIDTH)
    return o_c, o_l

def mixer_neighbourhood(q, k, v, rpb, n_ctx, need_ctx):
    B_, T, _ = q.shape
    n = T - n_ctx
    rows = n // GRID_W
    wr = min(WIN_ROWS, rows)
    heads = lambda t: t.reshape(B_, T, C_HEADS, HEAD_DIM)
    q, k, v = heads(q), heads(k), heads(v)
    q_c, k_c, v_c = q[:, :n_ctx], k[:, :n_ctx], v[:, :n_ctx]
    q_l, k_l, v_l = q[:, n_ctx:], k[:, n_ctx:], v[:, n_ctx:]
    r = jnp.arange(rows)
    col = jnp.arange(GRID_W)
    row_start = jnp.clip(r - wr // 2, 0, rows - wr)
    col_start = jnp.clip(col - WIN_COLS // 2, 0, GRID_W - WIN_COLS)
    w_idx = jnp.arange(wr * WIN_COLS)
    key_row = row_start[:, None] + (w_idx // WIN_COLS)[None, :]
    key_col = col_start[:, None] + (w_idx % WIN_COLS)[None, :]
    idx = key_row[:, None, :] * GRID_W + key_col[None, :, :]
    d_row = (key_row - r[:, None] + WIN_ROWS - 1)[:, None, :]
    d_col = (key_col - col[:, None] + WIN_COLS - 1)[None, :, :]
    bias = rpb[:, d_row, d_col].astype(jnp.float32).transpose(1, 0, 2, 3)
    q_rows = q_l.reshape(B_, rows, GRID_W, C_HEADS, HEAD_DIM).swapaxes(0, 1)
    scale = HEAD_DIM ** -0.5

    def row_block(args):
        q_r, idx_r, bias_r = args
        k_w, v_w = k_l[:, idx_r], v_l[:, idx_r]
        s_w = jnp.einsum('bqhd,bqwhd->bhqw', q_r, k_w).astype(jnp.float32) * scale + bias_r
        s_c = jnp.einsum('bqhd,bchd->bhqc', q_r, k_c).astype(jnp.float32) * scale
        p = jax.nn.softmax(jnp.concatenate([s_w, s_c], axis=-1), axis=-1).astype(v_l.dtype)
        W = idx_r.shape[-1]
        return (jnp.einsum('bhqw,bqwhd->bqhd', p[..., :W], v_w)
                + jnp.einsum('bhqc,bchd->bqhd', p[..., W:], v_c))

    o_l = lax.map(row_block, (q_rows, idx, bias)).swapaxes(0, 1).reshape(B_, n, C_WIDTH)
    o_c = None
    if need_ctx:
        o_c = gqa_attend(q_c[:, :, :, None, :], k_c, v_c).reshape(B_, n_ctx, C_WIDTH)
    return o_c, o_l

def flip_segments(t, n_ctx):
    return jnp.concatenate([t[:, :n_ctx][:, ::-1], t[:, n_ctx:][:, ::-1]], axis=1)

def wkv_scan(r, w, k, v, a, b):
    B_, _, H, N = r.shape
    xs = tuple(t.swapaxes(0, 1) for t in (r, w, k, v, a, b))

    def step(S, inp):
        r_t, w_t, k_t, v_t, a_t, b_t = inp
        sa = jnp.einsum('bhij,bhj->bhi', S, a_t)
        S = S * w_t[:, :, None, :] + sa[..., None] * b_t[:, :, None, :] + v_t[..., None] * k_t[:, :, None, :]
        return S, jnp.einsum('bhij,bhj->bhi', S, r_t)

    _, y = lax.scan(step, jnp.zeros((B_, H, N, N), jnp.float32), xs)
    return y.swapaxes(0, 1)

def mixer_rwkv7(r, k, v, w_low, a_low, g_low, w0, w_up, a0, a_up, g_up, k_k, k_a, r_k, lnx_w, lnx_b, n_ctx):
    f32 = jnp.float32
    B_, T, _ = r.shape
    heads = lambda t: t.reshape(B_, T, B_HEADS, HEAD_DIM)
    r, k, v = r.astype(f32), k.astype(f32), v.astype(f32)
    kk = heads(k * k_k.astype(f32))
    kk = kk / jnp.maximum(jnp.sqrt(jnp.sum(kk * kk, axis=-1, keepdims=True)), 1e-12)
    g = jax.nn.sigmoid(g_low.astype(f32)) @ g_up.astype(f32)
    ys, bonuses = [], []
    for d in range(2):
        wl = w_low[..., d * DECAY_LORA:(d + 1) * DECAY_LORA].astype(f32)
        al = a_low[..., d * AAA_LORA:(d + 1) * AAA_LORA].astype(f32)
        w = -jax.nn.softplus(-(w0[d].astype(f32) + jnp.tanh(wl) @ w_up[d].astype(f32))) - 0.5
        decay = jnp.exp(-jnp.exp(w))
        a = jax.nn.sigmoid(a0[d].astype(f32) + al @ a_up[d].astype(f32))
        kd = k * (1 + (a - 1) * k_a.astype(f32))
        seq = [heads(t) for t in (r, decay, kd, v)] + [-kk, kk * heads(a)]
        if d == 1:
            seq = [flip_segments(t, n_ctx) for t in seq]
        y = wkv_scan(*seq)
        if d == 1:
            y = flip_segments(y, n_ctx)
        ys.append(y)
        bonuses.append(jnp.sum(heads(r * kd * r_k.astype(f32)), axis=-1, keepdims=True) * heads(v))
    y = ys[0] + ys[1]
    mu = jnp.mean(y, axis=-1, keepdims=True)
    var = jnp.mean(jnp.square(y - mu), axis=-1, keepdims=True)
    y = ((y - mu) * lax.rsqrt(var + LNX_EPS)).reshape(B_, T, B_WIDTH) * lnx_w.astype(f32) + lnx_b.astype(f32)
    return (y + (bonuses[0] + bonuses[1]).reshape(B_, T, B_WIDTH)) * g

def ec_moe(h, w_router, w_gate, w_up, w_down):
    B_, n, _ = h.shape
    cap = CAPACITY_FACTOR * n // N_EXPERTS
    aff = jax.nn.softmax((h @ w_router).astype(jnp.float32), axis=-1)
    gate, idx = lax.top_k(aff.swapaxes(1, 2), cap)
    bidx = jnp.arange(B_)[:, None, None]
    xe = h[bidx, idx]
    hid = jax.nn.silu(jnp.einsum('becd,edf->becf', xe, w_gate)) * jnp.einsum('becd,edf->becf', xe, w_up)
    ye = jnp.einsum('becf,efd->becd', hid, w_down) * gate[..., None].astype(h.dtype)
    return jnp.zeros_like(h).at[bidx, idx].add(ye)

def setup_inputs(seed: int = 0) -> dict:
    key = jax.random.key(seed)
    ks = iter(jax.random.split(key, 40))
    nrm = lambda shape, s: jax.random.normal(next(ks), shape, jnp.float32) * s
    L, D = DEPTH, D_MODEL
    return {
        "x": nrm((BATCH, SEQ, D), 1.0),
        "c": nrm((BATCH, D), 1.0),
        "ctx": nrm((BATCH, CTX_LEN, D), 1.0),
        "c_ctx": nrm((D,), 1.0),
        "w_mod": nrm((L, D, 6 * D), 0.5 * D ** -0.5),
        "b_mod": nrm((L, 6 * D), 0.01),
        "g_pre_mix": 1.0 + nrm((L, D), 0.05),
        "g_post_mix": 1.0 + nrm((L, D), 0.05),
        "g_pre_ffn": 1.0 + nrm((L, D), 0.05),
        "g_post_ffn": 1.0 + nrm((L, D), 0.05),
        "w_in": nrm((L, D, N_IN), D ** -0.5),
        "w_out": nrm((L, D_MIX, D), D_MIX ** -0.5),
        "q_gain": 1.0 + nrm((L, HEAD_DIM), 0.05),
        "k_gain": 1.0 + nrm((L, HEAD_DIM), 0.05),
        "rpb": nrm((L, C_HEADS, 2 * WIN_ROWS - 1, 2 * WIN_COLS - 1), 0.1),
        "rk_w0": jax.random.uniform(next(ks), (L, 2, B_WIDTH), jnp.float32, -5.0, 0.0),
        "rk_w_up": nrm((L, 2, DECAY_LORA, B_WIDTH), 0.5 * DECAY_LORA ** -0.5),
        "rk_a0": nrm((L, 2, B_WIDTH), 0.1),
        "rk_a_up": nrm((L, 2, AAA_LORA, B_WIDTH), 0.5 * AAA_LORA ** -0.5),
        "rk_g_up": nrm((L, GATE_LORA, B_WIDTH), GATE_LORA ** -0.5),
        "rk_k_k": 0.85 + nrm((L, B_WIDTH), 0.05),
        "rk_k_a": 1.0 + nrm((L, B_WIDTH), 0.05),
        "rk_r_k": nrm((L, B_WIDTH), 0.1),
        "rk_lnx_w": 1.0 + nrm((L, B_WIDTH), 0.05),
        "rk_lnx_b": nrm((L, B_WIDTH), 0.01),
        "w_router": nrm((L, D, N_EXPERTS), D ** -0.5),
        "w_e_gate": nrm((L, N_EXPERTS, D, D_EXPERT), D ** -0.5),
        "w_e_up": nrm((L, N_EXPERTS, D, D_EXPERT), D ** -0.5),
        "w_e_down": nrm((L, N_EXPERTS, D_EXPERT, D), D_EXPERT ** -0.5),
    }

def reference(x, c, ctx, c_ctx, w_mod, b_mod, g_pre_mix, g_post_mix, g_pre_ffn, g_post_ffn,
              w_in, w_out, q_gain, k_gain, rpb, rk_w0, rk_w_up, rk_a0, rk_a_up, rk_g_up,
              rk_k_k, rk_k_a, rk_r_k, rk_lnx_w, rk_lnx_b, w_router, w_e_gate, w_e_up, w_e_down):
    x_l, x_c = x, ctx
    n_ctx = ctx.shape[1]
    in_splits = np.cumsum(IN_SIZES)[:-1].tolist()
    s_l, s_c = jax.nn.silu(c), jax.nn.silu(c_ctx)
    for i in range(DEPTH):
        need_ctx = i < DEPTH - 1
        m_l = jnp.split((s_l @ w_mod[i] + b_mod[i])[:, None, :], 6, axis=-1)
        m_c = jnp.split(s_c @ w_mod[i] + b_mod[i], 6, axis=-1)
        h = jnp.concatenate([modulate(rms_norm(x_c, g_pre_mix[i]), m_c[0], m_c[1]),
                             modulate(rms_norm(x_l, g_pre_mix[i]), m_l[0], m_l[1])], axis=1)
        proj = h @ w_in[i]
        (qa, ka, va, rb, kb, vb, wlb, alb, glb, qn, kn, vn) = jnp.split(proj, in_splits, axis=-1)
        oa_c, oa_l = mixer_grid_attention(qa, ka, va, q_gain[i], k_gain[i], n_ctx, need_ctx)
        ob = mixer_rwkv7(rb, kb, vb, wlb, alb, glb, rk_w0[i], rk_w_up[i], rk_a0[i], rk_a_up[i],
                         rk_g_up[i], rk_k_k[i], rk_k_a[i], rk_r_k[i], rk_lnx_w[i], rk_lnx_b[i],
                         n_ctx).astype(x.dtype)
        on_c, on_l = mixer_neighbourhood(qn, kn, vn, rpb[i], n_ctx, need_ctx)
        y_l = jnp.concatenate([oa_l, ob[:, n_ctx:], on_l], axis=-1) @ w_out[i]
        x_l = x_l + m_l[2] * rms_norm(y_l, g_post_mix[i])
        if need_ctx:
            y_c = jnp.concatenate([oa_c, ob[:, :n_ctx], on_c], axis=-1) @ w_out[i]
            x_c = x_c + m_c[2] * rms_norm(y_c, g_post_mix[i])
        h_l = modulate(rms_norm(x_l, g_pre_ffn[i]), m_l[3], m_l[4])
        f_l = ec_moe(h_l, w_router[i], w_e_gate[i], w_e_up[i], w_e_down[i])
        x_l = x_l + m_l[5] * rms_norm(f_l, g_post_ffn[i])
        if need_ctx:
            h_c = modulate(rms_norm(x_c, g_pre_ffn[i]), m_c[3], m_c[4])
            f_c = ec_moe(h_c, w_router[i], w_e_gate[i], w_e_up[i], w_e_down[i])
            x_c = x_c + m_c[5] * rms_norm(f_c, g_post_ffn[i])
    return x_l


_drawn_inputs = setup_inputs


def setup_inputs(seed=0):
    import zlib

    import numpy as np

    out = dict(_drawn_inputs(seed))
    spreads = {}
    factors = {'q_gain': 3.237, 'rk_lnx_b': 5.613, 'rpb': 4.482}
    for name, (base, spread) in spreads.items():
        noise = np.random.default_rng([zlib.crc32(name.encode()), seed]).standard_normal(out[name].shape)
        drawn = base * np.exp(spread * noise) if base else spread * noise
        out[name] = __import__('jax').numpy.asarray(drawn.astype(out[name].dtype))
    for name, factor in factors.items():
        out[name] = (out[name] * factor).astype(out[name].dtype)
    return out
```

```python
from contextlib import ExitStack, contextmanager

import numpy as np

import concourse.bass as bass
from concourse import mybir

F32 = mybir.dt.float32
ACT = mybir.ActivationFunctionType
ALU = mybir.AluOpType
AX_X = mybir.AxisListType.X
ds = bass.ds

P = 128
D = 1024
KD = D // P
SEQ, CTX = 512, 256
T = SEQ + CTX
NT, NTC = T // P, CTX // P
DEPTH = 2
HD = 64
A_HEADS, A_KV = 8, 2
A_GROUP = A_HEADS // A_KV
A_W, A_KVW = A_HEADS * HD, A_KV * HD
B_HEADS, B_W = 4, 256
C_HEADS, C_W = 4, 256
N_IN = A_W + 2 * A_KVW + 3 * B_W + 3 * P + 3 * C_W
GRID = 64
WIN_ROWS, WIN_COLS = 8, 16
RPB_M = 14
NE, DE = 16, 1024
CAP_L, CAP_C = 2 * SEQ // NE, 2 * CTX // NE
CAP = CAP_L + CAP_C
EPS, LNX_EPS = 1e-6, 64e-5
SCALE = HD ** -0.5
CH = 64
NCH = T // CH
NCC = CTX // CH
KAPPA = -float(np.exp(-0.5))
NEG = -1e30

O_ID, O_TRI, O_LM, O_HB, O_HS, O_IOTA, O_I64 = 0, 128, 384, 768, 896, 898, 962
N_CST = 1026
TRI_LT, TRI_LE, TRI_GT, TRI_GE = range(4)
C_W0, C_A0, C_KK, C_KA, C_RK, N_COL = 0, 4, 8, 10, 12, 14
R_GAIN, R_LNW, R_LNB, N_ROW = 0, 640, 896, 1152


class Scope:

    def __init__(self, nc, stack):
        self.nc, self.stack = nc, stack

    def sb(self, name, shape):
        return self.stack.enter_context(self.nc.sbuf_tensor(name, shape, F32))

    def ps(self, name, shape):
        return self.stack.enter_context(self.nc.psum_tensor(name, shape, F32))


class Link:

    def __init__(self, eng, sem, base=0):
        self.eng, self.sem, self.n, self.base = eng, sem, 0, base

    def __call__(self, ins):
        ins.then_inc(self.sem, 1)
        self.n += 1
        self.eng.wait_ge(self.sem, self.base + self.n)


def at(ap, i):
    return ap[ds(i, 1)].squeeze(0)


def spread(ap, axis, n):
    v = ap.unsqueeze(axis)
    shape = list(v.shape)
    shape[axis] = n
    return v.to_broadcast(shape)




def modulation(nc, g, layer):
    NCHUNK, SLOTS, W = 6 * D // 512, 4, 512
    with ExitStack() as stack:
        a = Scope(nc, stack)
        wm = a.sb("wm", [P, SLOTS, KD, W])
        bias = a.sb("mod_bias", [2, 6 * D])
        gains = a.sb("mod_gains", [2, 4, D])
        rows = a.sb("mod_acc", [2, 6, D])
        rowsf = rows[:, :, :].rearrange("s a b -> s (a b)")
        ps = a.ps("mod_ps", [2, SLOTS, W])
        w_loaded = [g.sem(f"mod_w_loaded{s}") for s in range(SLOTS)]
        w_free = g.sem("mod_w_free")
        rows_loaded = g.sem("mod_rows_loaded")
        prod = g.sem("mod_product")
        ps_free = g.sem("mod_ps_free")
        folded = g.sem("mod_folded")
        stored = g.sem("mod_stored")
        wv = at(g.w_mod, layer).rearrange("(k p) n -> p k n", p=P)
        with nc.Block(no_gpsimd_drain=True) as block:

            @block.sync
            def _(sync):
                sync.sem_inc(w_free, SLOTS)
                sync.dma_start(bias[:, :], at(g.b_mod, layer).partition_broadcast(2)).then_inc(rows_loaded, 16)
                sync.dma_start(gains[:, :, :].rearrange("s a b -> s (a b)"),
                               at(g.gains, layer).partition_broadcast(2)).then_inc(rows_loaded, 16)
                with sync.Fori(0, NCHUNK // SLOTS) as i:
                    for s in range(SLOTS):
                        sync.wait_ge(w_free, i * SLOTS + s + 1)
                        sync.dma_start(wm[:, s, :, :], wv[:, :, ds((i * SLOTS + s) * W, W)]).then_inc(w_loaded[s], 16)
                sync.wait_ge(folded, 4)
                sync.dma_start(g.mod_rows[:, :], rowsf).then_inc(stored, 16)
                sync.wait_ge(stored, 16)

            @block.tensor
            def _(pe):
                pe.sem_inc(ps_free, SLOTS)
                with pe.Fori(0, NCHUNK // SLOTS) as i:
                    for s in range(SLOTS):
                        pe.wait_ge(w_loaded[s], i * 16 + 16)
                        pe.wait_ge(ps_free, i * SLOTS + s + 1)
                        for k in range(KD):
                            mm = pe.matmul(ps[:, s, :], g.silu_c[:, k, :], wm[:, s, k, :],
                                           start=(k == 0), stop=(k == KD - 1))
                        mm.then_inc(prod, 1)
                        pe.wait_ge(prod, i * SLOTS + s + 1)
                        pe.sem_inc(w_free, 1)

            @block.vector
            def _(dve):
                dve.wait_ge(rows_loaded, 32)
                with dve.Fori(0, NCHUNK // SLOTS) as i:
                    for s in range(SLOTS):
                        dve.wait_ge(prod, i * SLOTS + s + 1)
                        c = (i * SLOTS + s) * W
                        dve.tensor_tensor(rowsf[:, ds(c, W)], ps[:, s, :], bias[:, ds(c, W)],
                                          ALU.add).then_inc(ps_free, 1)
                dve.wait_ge(ps_free, SLOTS + NCHUNK)
                for sec, gain, pre in ((1, 0, True), (2, 1, False), (4, 2, True), (5, 3, False)):
                    dve.scalar_tensor_tensor(rows[:, sec, :], rows[:, sec, :], 1.0 if pre else 0.0, gains[:, gain, :],
                                             ALU.add, ALU.mult).then_inc(folded, 1)




class PreNorm:

    def __init__(self, g, name, x, h, gain, shift, junk, stats):
        self.x, self.h, self.gain, self.shift, self.junk, self.st = x, h, gain, shift, junk, stats
        self.squares, self.var, self.root, self.inv, self.scaled, self.shifted = (
            g.sem(f"{name}_{n}") for n in ("squares", "var", "root", "inv", "scaled", "shifted"))

    def scalar(self, act, x_ready):
        for t in range(NT):
            x_ready(act, t)
            act.activation(self.junk[:, :], self.x[:, t, :], ACT.Square,
                           accum_out=self.st[:, t:t + 1]).then_inc(self.squares, 1)
            act.wait_ge(self.squares, t + 1)
        act.wait_ge(self.var, 1)
        act.activation(self.st[:, 8:8 + NT], self.st[:, 8:8 + NT], ACT.Sqrt).then_inc(self.root, 1)

    def vector(self, dve, rows_ready):
        dve.wait_ge(self.squares, NT)
        dve.tensor_scalar(self.st[:, 8:8 + NT], self.st[:, 0:NT], 1.0 / D, EPS, ALU.mult, ALU.add).then_inc(self.var, 1)
        dve.wait_ge(self.root, 1)
        dve.reciprocal(self.st[:, 16:16 + NT], self.st[:, 8:8 + NT]).then_inc(self.inv, 1)
        dve.wait_ge(self.inv, 1)
        rows_ready(dve)
        for t in range(NT):
            dve.scalar_tensor_tensor(self.h[:, t, :], self.x[:, t, :], self.st[:, 16 + t:17 + t],
                                     self.gain[:, int(t >= NTC), :], ALU.mult, ALU.mult).then_inc(self.scaled, 1)

    def gpsimd(self, pool):
        for t in range(NT):
            pool.wait_ge(self.scaled, t + 1)
            pool.tensor_tensor(self.h[:, t, :], self.h[:, t, :], self.shift[:, int(t >= NTC), :],
                               ALU.add).then_inc(self.shifted, 1)


def load_mod_rows(eng, g, dst, section, sem):
    for s in range(2):
        eng.dma_start(dst[:, s, :], g.mod_rows[s, section * D:(section + 1) * D].partition_broadcast(P)).then_inc(sem, 16)



FM_OF = {768: 0, 896: 1, 1024: 2, 1152: 3, 1536: 4, 1664: 5, 1792: 6, 1920: 7, 2048: 8, 2176: 9, 2304: 10}


def proj_jobs():
    jobs = []
    for c in range(11):
        base = c * 256
        if base < 768:
            jobs.append((c, "qkv", 0, 256, base))
        elif base == 1280:
            jobs.append((c, "vb", 0, 256, 0))
        else:
            for off in (0, 128):
                col = base + off
                if col in FM_OF:
                    jobs.append((c, "fm", off, 128, FM_OF[col]))
                elif col < N_IN:
                    jobs.append((c, "vn", off, 128, col - 2432))
    return jobs


def projection(nc, g, layer):
    SLOTS, W, BANKS = 4, 256, 6
    NC = (N_IN + W - 1) // W
    groups = []
    for job in proj_jobs():
        groups += [(job, i) for i in range(2 if job[1] == "fm" else NT)]
    with ExitStack() as stack:
        a = Scope(nc, stack)
        x = a.sb("pj_x", [P, NT, D])
        h = x
        hT = a.sb("pj_hT", [P, KD, T])
        gain = a.sb("pj_gain", [P, 2, D])
        shift = a.sb("pj_shift", [P, 2, D])
        junk = a.sb("pj_junk", [P, D])
        stats = a.sb("pj_stats", [P, 24])
        w = a.sb("pj_w", [P, SLOTS, KD, W])
        tp = a.ps("pj_tp", [P, 2, 4, P])
        ps = a.ps("pj_ps", [P, BANKS, 512])
        norm = PreNorm(g, "pj", x, h, gain, shift, junk, stats)
        x_loaded = [g.sem(f"pj_x_loaded{t}") for t in range(NT)]
        w_loaded = [g.sem(f"pj_w_loaded{s}") for s in range(SLOTS)]
        rows_loaded = g.sem("pj_rows_loaded")
        turned = g.sem("pj_turned")
        hT_ready = g.sem("pj_hT_ready")
        group_done = g.sem("pj_group_done")
        out_s = g.sem("pj_copied_scalar")
        out_v = g.sem("pj_copied_vector")
        last_group = {}
        for n, (job, _) in enumerate(groups):
            last_group[job[0]] = n

        def dest(n):
            (c, kind, off, width, place), i = groups[n]
            src = ps[:, n % BANKS, 0:(T // 2 if kind == "fm" else width)]
            if kind == "fm":
                return g.fm[:, place, i * (T // 2):(i + 1) * (T // 2)], src
            buf = {"qkv": g.qkv, "vb": g.vb, "vn": g.vn}[kind]
            return buf[:, i, place:place + width], src

        with nc.Block(no_gpsimd_drain=True) as block:

            @block.sync
            def _(sync):
                for t in range(NT):
                    sync.dma_start(x[:, t, :], g.stream[t * P:(t + 1) * P, :]).then_inc(x_loaded[t], 16)
                load_mod_rows(sync, g, gain, 1, rows_loaded)
                load_mod_rows(sync, g, shift, 0, rows_loaded)
                wv = at(g.w_in, layer).rearrange("(k p) n -> p k n", p=P)
                for c in range(NC):
                    width = min(W, N_IN - c * W)
                    if c >= SLOTS:
                        sync.wait_ge(group_done, last_group[c - SLOTS] + 1)
                    sync.dma_start(w[:, c % SLOTS, :, 0:width], wv[:, :, c * W:c * W + width]).then_inc(w_loaded[c % SLOTS], 16)

            @block.scalar
            def _(act):
                norm.scalar(act, lambda e, t: e.wait_ge(x_loaded[t], 16))
                for n in range(2 * NT):
                    act.wait_ge(turned, n + 1)
                    t, half = n // 2, n % 2
                    act.activation(hT[:, 4 * half:4 * half + 4, t * P:(t + 1) * P], tp[:, half, :, :],
                                   ACT.Copy).then_inc(hT_ready, 1)
                for n in range(0, len(groups), 2):
                    act.wait_ge(group_done, n + 1)
                    o, i = dest(n)
                    act.activation(o, i, ACT.Copy).then_inc(out_s, 1)

            @block.vector
            def _(dve):
                norm.vector(dve, lambda e: e.wait_ge(rows_loaded, 64))
                for n in range(1, len(groups), 2):
                    dve.wait_ge(group_done, n + 1)
                    o, i = dest(n)
                    dve.tensor_copy(o, i).then_inc(out_v, 1)

            @block.gpsimd
            def _(pool):
                norm.gpsimd(pool)

            @block.tensor
            def _(pe):
                for n in range(2 * NT):
                    t, half = n // 2, n % 2
                    pe.wait_ge(norm.shifted, t + 1)
                    if n >= 2:
                        pe.wait_ge(hT_ready, n - 1)
                    for j in range(4):
                        k = 4 * half + j
                        mm = pe.transpose(tp[:, half, j, :], h[:, t, k * P:(k + 1) * P], g.ident)
                    mm.then_inc(turned, 1)
                pe.wait_ge(hT_ready, 2 * NT)
                for n, ((c, kind, off, width, place), i) in enumerate(groups):
                    pe.wait_ge(w_loaded[c % SLOTS], 16 * (c // SLOTS + 1))
                    if n >= BANKS:
                        pe.wait_ge(out_s if n % 2 == 0 else out_v, (n - BANKS) // 2 + 1)
                    for k in range(KD):
                        wk = w[:, c % SLOTS, k, off:off + width]
                        if kind == "fm":
                            mm = pe.matmul(ps[:, n % BANKS, 0:T // 2], wk, hT[:, k, i * (T // 2):(i + 1) * (T // 2)],
                                           start=(k == 0), stop=(k == KD - 1))
                        else:
                            mm = pe.matmul(ps[:, n % BANKS, 0:width], hT[:, k, i * P:(i + 1) * P], wk,
                                           start=(k == 0), stop=(k == KD - 1))
                    mm.then_inc(group_done, 1)



N_ITEM = A_HEADS + C_HEADS
Q_BLOCKS = A_GROUP + 2


def attention_prepare(nc, g, a, b, layer):
    NH = A_HEADS + A_KV
    ss, tmp, tmp2 = a.sb("qk_ss", [P, 3, NT, NH]), a.sb("qk_tmp", [P, 2, NH, HD]), a.sb("qk_tmp2", [P, 2, NH, HD])
    rot = a.sb("qk_rot", [P, 2, NH, HD])
    ssf = ss[:, :, :, :].rearrange("p a t h -> p a (t h)")
    rope_loaded, bias_loaded = g.sem("rope_loaded"), g.sem("bias_loaded")
    squared, summed, var, root, inv = (g.sem(f"qk_{n}") for n in ("squared", "summed", "var", "root", "inv"))
    scaled, gained, cosed, sined, rotated = (g.sem(f"qk_{n}") for n in ("scaled", "gained", "cosed", "sined", "rotated"))
    turned, stored = g.sem("qk_turned"), g.sem("qk_stored")
    b.qk_ready, b.bias_ready = stored, bias_loaded

    def qk(t):
        return g.qkv[:, t, 0:NH * HD].rearrange("p (h d) -> p h d", h=NH)

    def parts(v):
        return v.rearrange("p h (r s e) -> p h r s e", r=2, s=2)

    def sync(sync):
        sync.dma_start(b.rope[:, :, :], g.rope_d).then_inc(rope_loaded, 16)
        sync.dma_start(b.rows[:, :], at(g.rows_d, layer)[R_GAIN:R_GAIN + NH * HD].partition_broadcast(P)).then_inc(rope_loaded, 16)
        sync.dma_start(b.bias[:, :, :].rearrange("p h n -> p (h n)"), at(g.bias_d, layer)).then_inc(bias_loaded, 16)

    def vector(dve):
        for t in range(NT):
            if t >= 2:
                dve.wait_ge(summed, t - 1)
            dve.tensor_tensor(tmp[:, t % 2, :, :], qk(t), qk(t), ALU.mult).then_inc(squared, 1)
            dve.wait_ge(squared, t + 1)
            dve.tensor_reduce(ss[:, 0, t, :], tmp[:, t % 2, :, :], AX_X, ALU.add).then_inc(summed, 1)
        dve.wait_ge(summed, NT)
        dve.tensor_scalar(ssf[:, 1, :], ssf[:, 0, :], 1.0 / HD, EPS, ALU.mult, ALU.add).then_inc(var, 1)
        dve.wait_ge(root, 1)
        dve.reciprocal(ssf[:, 0, :], ssf[:, 2, :]).then_inc(inv, 1)
        dve.wait_ge(inv, 1)
        for t in range(NT):
            dve.tensor_tensor(qk(t), qk(t), spread(ss[:, 0, t, :], 2, HD), ALU.mult).then_inc(scaled, 1)
            if t >= 1:
                finish(dve, t - 1)
        finish(dve, NT - 1)

    def finish(dve, t):
        i = t % 2
        dve.wait_ge(gained, t + 1)
        dve.wait_ge(rope_loaded, 32)
        dve.wait_ge(rotated, 2 * max(t - 1, 0))
        dve.tensor_tensor(tmp[:, i, :, :], qk(t), spread(b.rope[:, t, 0:HD], 1, NH), ALU.mult).then_inc(cosed, 1)
        dve.wait_ge(cosed, t + 1)
        dve.wait_ge(sined, 2 * t + 2)
        if t >= 2:
            dve.wait_ge(turned, t - 1)
        dve.tensor_tensor(rot[:, i, 0:A_HEADS, :].rearrange("p (g v) d -> p v g d", v=A_KV),
                          tmp[:, i, 0:A_HEADS, :].rearrange("p (v g) d -> p v g d", v=A_KV),
                          tmp2[:, i, 0:A_HEADS, :].rearrange("p (v g) d -> p v g d", v=A_KV), ALU.add).then_inc(rotated, 1)
        dve.tensor_tensor(rot[:, i, A_HEADS:NH, :], tmp[:, i, A_HEADS:NH, :], tmp2[:, i, A_HEADS:NH, :],
                          ALU.add).then_inc(rotated, 1)

    def gpsimd(pool):
        pool.wait_ge(rope_loaded, 32)
        for t in range(NT):
            i = t % 2
            pool.wait_ge(scaled, t + 1)
            pool.tensor_tensor(qk(t), qk(t), b.rows[:, :].rearrange("p (h d) -> p h d", h=NH), ALU.mult).then_inc(gained, 1)
            pool.wait_ge(gained, t + 1)
            if t >= 2:
                pool.wait_ge(rotated, 2 * t - 2)
            for s in range(2):
                pool.tensor_tensor(parts(tmp2[:, i, :, :])[:, :, :, s, :], parts(qk(t))[:, :, :, 1 - s, :],
                                   spread(b.rope[:, t, HD:2 * HD].rearrange("p (r s e) -> p r s e", r=2, s=2)[:, :, s, :],
                                          1, NH), ALU.mult).then_inc(sined, 1)

    def scalar(act):
        act.wait_ge(var, 1)
        act.activation(ssf[:, 2, :], ssf[:, 1, :], ACT.Sqrt).then_inc(root, 1)
        for t in range(NT):
            act.wait_ge(turned, t + 1)
            act.activation(b.qkT[:, :, t * P:(t + 1) * P], b.prep_ps[:, t % 2, :, :], ACT.Copy).then_inc(stored, 1)

    def tensor(pe):
        for t in range(NT):
            pe.wait_ge(rotated, 2 * t + 2)
            if t >= 2:
                pe.wait_ge(stored, t - 1)
            for j in range(5):
                mm = pe.transpose(b.prep_ps[:, t % 2, j, :],
                                  rot[:, t % 2, 2 * j:2 * j + 2, :].rearrange("p h d -> p (h d)"), g.ident)
            mm.then_inc(turned, 1)

    return sync, scalar, vector, gpsimd, tensor


def attend(nc, g, b, block, name, tiles, first, key_tiles, local_bias):
    n_local = C_HEADS if local_bias else 0
    n_plain = N_ITEM - n_local
    keys = key_tiles * P
    ka = (key_tiles + 1) // 2
    kb = key_tiles - ka
    staged, scored, maxed = g.sem(name + "_staged"), g.sem(name + "_scored"), g.sem(name + "_maxed")
    link_sem = g.sem(name + "_dve_chain")
    free_plain, free_local = g.sem(name + "_scores_read_scalar"), g.sem(name + "_scores_read_vector")
    exped, turned = g.sem(name + "_exped"), g.sem(name + "_turned")
    copied_a, copied_b = g.sem(name + "_copied_scalar"), g.sem(name + "_copied_vector")
    valued, normed = g.sem(name + "_valued"), g.sem(name + "_normed")
    uses = N_ITEM + 1

    def head(n):
        if n < A_HEADS:
            v = n // A_GROUP
            return n % A_GROUP, v * HD, None, lambda kt: g.qkv[:, kt, A_W + A_KVW + v * HD:A_W + A_KVW + (v + 1) * HD]
        h = n - A_HEADS
        return A_GROUP + h // 2, (h % 2) * HD, 9 + h // 2, lambda kt: g.vn[:, kt, h * HD:(h + 1) * HD]

    @block.gpsimd
    def _(pool):
        pool.wait_ge(b.qk_ready, NT)
        with pool.Fori(0, tiles) as i:
            pool.wait_ge(scored, i * N_ITEM)
            col = (i + first) * P
            pool.tensor_copy(b.q_now[:, 0:A_GROUP, :], b.qkT[:, 0:A_GROUP, ds(col, P)]).then_inc(staged, 1)
            pool.tensor_copy(b.q_now[:, A_GROUP:, :], g.fm[:, 7:9, ds(col, P)]).then_inc(staged, 1)

    @block.tensor
    def _(pe):
        if n_local:
            pe.sem_inc(free_local, n_local)
        else:
            pe.sem_inc(free_plain, 2)

        with pe.Fori(0, tiles) as i:
            def scores(n):
                if not n_local:
                    pe.wait_ge(free_plain, i * n_plain + n + 1)
                elif n < 2:
                    pe.wait_ge(free_local, i * n_local + n_local - 1 + n)
                elif n - 2 < n_plain:
                    pe.wait_ge(free_plain, i * n_plain + n - 1)
                else:
                    pe.wait_ge(free_local, i * n_local + n_local + (n - 2 - n_plain) + 1)
                q, part, kblk, _ = head(n)
                src = b.qkT[part:part + HD, A_GROUP, :] if kblk is None else g.fm[part:part + HD, kblk, :]
                for c in range(0, keys, 512):
                    w = min(512, keys - c)
                    mm = pe.matmul(b.sc_ps[:, n % 2, c:c + w], b.q_now[part:part + HD, q, :], src[:, c:c + w],
                                   start=True, stop=True)
                mm.then_inc(scored, 1)

            def turns(n):
                pe.wait_ge(exped, i * N_ITEM + n + 1)
                for kt in range(key_tiles):
                    if kt == 0 and n > 0:
                        pe.wait_ge(copied_a, i * uses + n)
                    if kt == ka and n > 0:
                        pe.wait_ge(copied_b, i * uses + n)
                    half, j = (0, kt) if kt < ka else (1, kt - ka)
                    mm = pe.transpose(b.pt_ps[:, half, j, :], b.e[:, n % 2, kt * P:(kt + 1) * P], g.ident)
                    if kt in (ka - 1, key_tiles - 1):
                        mm.then_inc(turned, 1)

            def values(n):
                pe.wait_ge(copied_a, i * uses + n + 1)
                pe.wait_ge(copied_b, i * uses + n + 1)
                v = head(n)[3]
                for kt in range(key_tiles):
                    mm = pe.matmul(b.o_ps[:, n * HD:(n + 1) * HD], b.pT[:, n % 2, kt, :], v(kt),
                                   start=(kt == 0), stop=(kt == key_tiles - 1))
                if n == N_ITEM - 1:
                    mm.then_inc(valued, 1)

            pe.wait_ge(staged, i * 2 + 2)
            pe.wait_ge(copied_a, i * uses)
            pe.wait_ge(copied_b, i * uses)
            scores(0)
            for n in range(N_ITEM):
                if n + 1 < N_ITEM:
                    scores(n + 1)
                turns(n)
                if n >= 1:
                    values(n - 1)
            values(N_ITEM - 1)
            pe.wait_ge(normed, i + 1)
            for j in range(6):
                mm = pe.transpose(b.pt_ps[:, j // 3, j % 3, :], b.o[:, j * P:(j + 1) * P], g.ident)
                if j % 3 == 2:
                    mm.then_inc(turned, 1)

    @block.scalar
    def _(act):
        with act.Fori(0, tiles) as i:
            def exp(n):
                act.wait_ge(maxed, i * N_ITEM + n + 1)
                if n >= 2:
                    act.wait_ge(turned, i * 2 * uses + 2 * (n - 1))
                else:
                    act.wait_ge(turned, i * 2 * uses)
                if n < n_plain:
                    src, scale = b.sc_ps[:, n % 2, 0:keys], SCALE
                else:
                    src, scale = b.s[:, n % 2, 0:keys], 1.0
                ins = act.activation(b.e[:, n % 2, 0:keys], src, ACT.Exp, bias=b.negmax[:, n:n + 1], scale=scale,
                                     accum_out=b.total[:, n:n + 1])
                ins.then_inc(exped, 1)
                if n < n_plain:
                    act.wait_ge(exped, i * N_ITEM + n + 1)
                    act.sem_inc(free_plain, 1)

            exp(0)
            for n in range(N_ITEM):
                if n + 1 < N_ITEM:
                    exp(n + 1)
                act.wait_ge(turned, i * 2 * uses + 2 * n + 1)
                act.activation(b.pT[:, n % 2, 0:ka, :], b.pt_ps[:, 0, 0:ka, :], ACT.Copy).then_inc(copied_a, 1)
            act.wait_ge(turned, i * 2 * uses + 2 * N_ITEM + 1)
            act.activation(g.mixT[:, 0:3, ds((i + first) * P, P)], b.pt_ps[:, 0, 0:3, :], ACT.Copy).then_inc(copied_a, 1)

    @block.vector
    def _(dve):
        per = 2 * n_plain + 4 * n_local + 1
        if local_bias:
            dve.wait_ge(b.bias_ready, 16)
        with dve.Fori(0, tiles) as i:
            link = Link(dve, link_sem, i * per)

            def maximum(n):
                dve.wait_ge(scored, i * N_ITEM + n + 1)
                if n < n_plain:
                    link(dve.tensor_reduce(b.mx[:, n:n + 1], b.sc_ps[:, n % 2, 0:keys], AX_X, ALU.max))
                    scale = -SCALE
                else:
                    if n >= n_plain + 2:
                        dve.wait_ge(exped, i * N_ITEM + n - 1)
                    h, ctx_keys = n - n_plain, CTX
                    dve.scalar_tensor_tensor(b.s[:, n % 2, ctx_keys:keys], b.sc_ps[:, n % 2, ctx_keys:keys], SCALE,
                                             b.bias[:, h, ds((RPB_M - WIN_ROWS) * GRID - i * 2 * GRID, WIN_ROWS * GRID)],
                                             ALU.mult, ALU.add).then_inc(link_sem, 1)
                    dve.tensor_scalar(b.s[:, n % 2, 0:ctx_keys], b.sc_ps[:, n % 2, 0:ctx_keys], SCALE, None,
                                      ALU.mult).then_inc(link_sem, 1)
                    link.n += 2
                    dve.wait_ge(link_sem, link.base + link.n)
                    dve.sem_inc(free_local, 1)
                    link(dve.tensor_reduce(b.mx[:, n:n + 1], b.s[:, n % 2, 0:keys], AX_X, ALU.max))
                    scale = -1.0
                dve.tensor_scalar(b.negmax[:, n:n + 1], b.mx[:, n:n + 1], scale, None, ALU.mult).then_inc(maxed, 1)
                dve.sem_inc(link_sem, 1)
                link.n += 1

            maximum(0)
            for n in range(N_ITEM):
                if n + 1 < N_ITEM:
                    maximum(n + 1)
                dve.wait_ge(turned, i * 2 * uses + 2 * n + 2)
                dve.tensor_copy(b.pT[:, n % 2, ka:key_tiles, :], b.pt_ps[:, 1, 0:kb, :]).then_inc(copied_b, 1)
            dve.wait_ge(exped, (i + 1) * N_ITEM)
            link(dve.reciprocal(b.inv[:, 0:N_ITEM], b.total[:, 0:N_ITEM]))
            dve.wait_ge(valued, i + 1)
            dve.tensor_tensor(b.o[:, :].rearrange("p (h d) -> p h d", d=HD),
                              b.o_ps[:, 0:N_ITEM * HD].rearrange("p (h d) -> p h d", d=HD),
                              spread(b.inv[:, 0:N_ITEM], 2, HD), ALU.mult).then_inc(normed, 1)
            dve.wait_ge(turned, i * 2 * uses + 2 * N_ITEM + 2)
            col = (i + first) * P
            dve.tensor_copy(g.mixT[:, 3, ds(col, P)], b.pt_ps[:, 1, 0, :])
            dve.tensor_copy(g.mixT[:, 6:8, ds(col, P)], b.pt_ps[:, 1, 1:3, :]).then_inc(copied_b, 1)
            assert link.n == per, (link.n, per)


class Buffers:
    pass


def attention(nc, g, layer):
    with ExitStack() as stack:
        a, b = Scope(nc, stack), Buffers()
        b.rope = a.sb("at_rope", [P, NT, 2 * HD])
        b.rows = a.sb("at_gain", [P, (A_HEADS + A_KV) * HD])
        b.bias = a.sb("at_bias", [P, C_HEADS, RPB_M * GRID])
        b.qkT = a.sb("at_qkT", [P, A_GROUP + 1, T])
        with ExitStack() as first:
            f = Scope(nc, first)
            b.prep_ps = f.ps("at_prep_ps", [P, 2, 8, P])[:, :, 0:5, :]
            sync, scalar, vector, gpsimd, tensor = attention_prepare(nc, g, f, b, layer)
            with nc.Block(no_gpsimd_drain=True) as block:
                block.sync(sync)
                block.scalar(scalar)
                block.vector(vector)
                block.gpsimd(gpsimd)
                block.tensor(tensor)
        b.q_now = a.sb("at_q_now", [P, Q_BLOCKS, P])
        b.e = a.sb("at_e", [P, 2, T])
        b.s = a.sb("at_s", [P, 2, T])
        b.pT = a.sb("at_pT", [P, 2, NT, P])
        b.o = a.sb("at_o", [P, N_ITEM * HD])
        b.mx, b.negmax, b.total, b.inv = (a.sb("at_" + n, [P, 16]) for n in ("mx", "negmax", "total", "inv"))
        b.sc_ps = a.ps("at_sc_ps", [P, 2, 1024])
        b.pt_ps = a.ps("at_pt_ps", [P, 2, 4, P])
        b.o_ps = a.ps("at_o_ps", [P, 1024])
        with nc.Block(no_gpsimd_drain=True) as block:
            attend(nc, g, b, block, "lat", NT - NTC, NTC, NT, True)
        with nc.Block(no_gpsimd_drain=True) as block:
            attend(nc, g, b, block, "ctx", NTC, 0, NTC, False)



HALF = T // 2


def rwkv_gates(nc, g, r, layer):
    fm = g.fm
    rT, kT, wl, al, gl = fm[:, 0:2, :], fm[:, 2:4, :], fm[:, 4, :], fm[:, 5, :], fm[:, 6, :]
    with ExitStack() as stack:
        a = Scope(nc, stack)
        tmp, tmp2 = a.sb("rg_tmp", [P, 2, T]), a.sb("rg_tmp2", [P, 2, T])
        restart = a.sb("rg_restart", [P, T])
        cols, wu, au = a.sb("rg_cols", [P, N_COL]), a.sb("rg_wu", [P, B_W]), a.sb("rg_au", [P, B_W])
        z = a.ps("rg_z", [P, 4, 512])
        ns = a.ps("rg_ns", [P, 2, 2, 512])
        bon = z[:, 0, 0:NT * B_HEADS].rearrange("p (t h) -> p t h", h=B_HEADS)
        loaded, acted, looked, gated = g.sem("rg_loaded"), g.sem("rg_acted"), g.sem("rg_looked"), g.sem("rg_gated")
        squared, summed, rooted, chain = g.sem("rg_squared"), g.sem("rg_summed"), g.sem("rg_rooted"), g.sem("rg_chain")
        bonus_in, bonus_out = g.sem("rg_bonus_in"), g.sem("rg_bonus_out")
        with nc.Block(no_gpsimd_drain=True) as block:

            @block.sync
            def _(sync):
                sync.dma_start(cols[:, :], at(g.cols_d, layer)).then_inc(loaded, 16)
                sync.dma_start(wu[:, :], at(g.w_up, layer)).then_inc(loaded, 16)
                sync.dma_start(au[:, :], at(g.a_up, layer)).then_inc(loaded, 16)

            @block.scalar
            def _(act):
                act.activation(wl, wl, ACT.Tanh).then_inc(acted, 1)
                act.activation(gl, gl, ACT.Sigmoid).then_inc(acted, 1)
                act.wait_ge(loaded, 48)
                for n in range(16):
                    d, blk, half = (n % 8) // 4, (n % 4) // 2, n % 2
                    dst, col = (r.xc, C_W0) if n < 8 else (r.b, C_A0)
                    act.wait_ge(looked, n + 1)
                    act.activation(dst[:, 2 * d + blk, half * HALF:(half + 1) * HALF], z[:, n % 4, 0:HALF], ACT.Sigmoid,
                                   bias=cols[:, col + 2 * d + blk:col + 2 * d + blk + 1]).then_inc(gated, 1)
                act.wait_ge(summed, 1)
                act.activation(tmp2[:, :, :].rearrange("p b (h n) -> p b h n", h=2), ns[:, :, :, 0:HALF],
                               ACT.Sqrt).then_inc(rooted, 1)

            @block.tensor
            def _(pe):
                pe.wait_ge(loaded, 48)
                pe.wait_ge(acted, 1)
                for n in range(16):
                    d, blk, half = (n % 8) // 4, (n % 4) // 2, n % 2
                    wt, src = (wu, wl) if n < 8 else (au, al)
                    if n >= 4:
                        pe.wait_ge(gated, n - 3)
                    pe.matmul(z[:, n % 4, 0:HALF], wt[d * 64:d * 64 + 64, blk * P:(blk + 1) * P],
                              src[d * 64:d * 64 + 64, half * HALF:(half + 1) * HALF], start=True, stop=True).then_inc(looked, 1)
                pe.wait_ge(squared, 1)
                for blk in range(2):
                    for half in range(2):
                        mm = pe.matmul(ns[:, blk, half, 0:HALF], g.cst[:, O_HB:O_HB + P],
                                       tmp[:, blk, half * HALF:(half + 1) * HALF], start=True, stop=True)
                mm.then_inc(summed, 1)
                pe.wait_ge(bonus_in, 2)
                for t in range(NT):
                    for blk in range(2):
                        mm = pe.matmul(bon[:, t, 2 * blk:2 * blk + 2], tmp[:, blk, t * P:(t + 1) * P],
                                       g.cst[:, O_HS:O_HS + 2], start=True, stop=True)
                mm.then_inc(bonus_out, 1)

            @block.vector
            def _(dve):
                link = Link(dve, chain)
                dve.wait_ge(loaded, 48)
                for blk in range(2):
                    link(dve.tensor_scalar(r.nkk[:, blk, :], kT[:, blk, :], cols[:, C_KK + blk:C_KK + blk + 1], None, ALU.mult))
                dve.tensor_tensor(tmp[:, :, :], r.nkk[:, :, :], r.nkk[:, :, :], ALU.mult).then_inc(squared, 1)
                link(dve.memset(restart[:, :], 1.0))
                link(dve.memset(restart[:, 0:T:CH], 0.0))
                dve.wait_ge(gated, 8)
                for db in range(4):
                    way = slice(None) if db < 2 else slice(None, None, -1)
                    link(dve.tensor_tensor_scan(r.cs[:, db, way], restart[:, :], r.xc[:, db, way], 0.0, ALU.mult, ALU.add))
                link(dve.tensor_tensor(r.xc[:, :, :], r.cs[:, :, :], r.xc[:, :, :], ALU.subtract))
                dve.wait_ge(rooted, 1)
                link(dve.tensor_scalar(tmp2[:, :, :], tmp2[:, :, :], 1e-12, None, ALU.max))
                link(dve.reciprocal(tmp2[:, :, :], tmp2[:, :, :]))
                link(dve.scalar_tensor_tensor(r.nkk[:, :, :], r.nkk[:, :, :], -1.0, tmp2[:, :, :], ALU.mult, ALU.mult))
                dve.wait_ge(gated, 16)
                for db in range(4):
                    blk = db % 2
                    link(dve.tensor_scalar(r.kd[:, db, :], r.b[:, db, :], 1.0, cols[:, C_KA + blk:C_KA + blk + 1],
                                           ALU.subtract, ALU.mult))
                for d in range(2):
                    link(dve.scalar_tensor_tensor(r.kd[:, 2 * d:2 * d + 2, :], r.kd[:, 2 * d:2 * d + 2, :], 1.0, kT,
                                                  ALU.add, ALU.mult))
                for d in range(2):
                    link(dve.scalar_tensor_tensor(r.b[:, 2 * d:2 * d + 2, :], r.b[:, 2 * d:2 * d + 2, :], -1.0, r.nkk[:, :, :],
                                                  ALU.mult, ALU.mult))
                link(dve.tensor_tensor(tmp[:, :, :], r.kd[:, 0:2, :], r.kd[:, 2:4, :], ALU.add))
                for blk in range(2):
                    dve.scalar_tensor_tensor(tmp[:, blk, :], tmp[:, blk, :], cols[:, C_RK + blk:C_RK + blk + 1],
                                             rT[:, blk, :], ALU.mult, ALU.mult).then_inc(bonus_in, 1)
                dve.wait_ge(bonus_out, 1)
                dve.tensor_copy(r.bonus[:, :, :], bon)


def rwkv_chunks(nc, g, r, layer):
    with ExitStack() as stack:
        a = Scope(nc, stack)
        e = a.sb("rc_e", [P, 3, 4, P])
        bh, kh = e[:, 0, :, :], e[:, 1, :, :]
        dg = e[:, 2, :, :].rearrange("p db (c n) -> p (db c) n", c=2)
        wend = a.sb("rc_wend", [P, 8])
        ar = a.sb("rc_ar", [P, 2, 4, P])
        bt, kt = a.sb("rc_bt", [P, 4, P]), a.sb("rc_kt", [P, 4, P])
        vt = a.sb("rc_vt", [P, B_W])
        ag = a.sb("rc_ag", [P, 8, 2, CH])
        bht, kht = a.sb("rc_bht", [P, 8, CH]), a.sb("rc_kht", [P, 8, CH])
        lb, lk = a.sb("rc_lb", [P, 8, 2 * CH]), a.sb("rc_lk", [P, 8, 2 * CH])
        nl = a.sb("rc_nl", [P, 5, 8, CH])
        tu = a.sb("rc_tu", [P, 2, 2, 4, CH])
        y = a.sb("rc_y", [P, 8, CH])
        tag = a.sb("rc_tag", [P, 8, 2 * CH])
        mk = a.sb("rc_mk", [P, 2, 2 * CH])
        m0 = a.sb("rc_m0", [P, 2, CH])
        ps = a.ps("rc_ps", [P, 8, 512])
        names = ("masks", "decays", "tildes", "hats", "v_staged", "products", "turned", "turned_kept", "masked",
                 "levels", "y_made", "y_kept", "step_made", "inverse", "g0_made", "g0_kept", "tag_made",
                 "tag_kept_v", "tag_kept_s", "results", "kept_v", "kept_s", "passed")
        s = Buffers()
        (s.masks, s.decays, s.tildes, s.hats, s.v_staged, s.products, s.turned, s.turned_kept, s.masked,
         s.levels, s.y_made, s.y_kept, s.step_made, s.inverse, s.g0_made, s.g0_kept, s.tag_made,
         s.tag_kept_v, s.tag_kept_s, s.results, s.kept_v, s.kept_s, s.passed) = (g.sem("rc_" + n) for n in names)
        lm = [g.cst[:, O_LM + 64 * lv:O_LM + 64 * lv + 64] for lv in range(6)]
        tri = [g.cst[:, O_TRI + 64 * i:O_TRI + 64 * i + 64] for i in range(4)]
        i64 = g.cst[:, O_I64:O_I64 + CH]
        units = [(par, db, ck) for par in range(2) for db in range(4) for ck in range(2)]
        half = [slice(0, 64), slice(64, 128)]

        def value(par, db):
            h = (db % 2) * 2 + par
            return slice(h * HD, h * HD + HD)

        def by_ck(v, col):
            return v[:, :, ds(col, P)].rearrange("p b (c n) -> p b c n", c=2)

        def from_ck(bank, c):
            return ps[:, bank:bank + 2, c:c + 256].rearrange("p c (b n) -> p b c n", b=4)

        def by_db(v, groups=4):
            return v.rearrange("p (b n) -> p b n", b=groups)

        with nc.Block(no_gpsimd_drain=True) as block:

            @block.scalar
            def _(act):
                with act.Fori(0, NT) as i:
                    col = i * P
                    act.wait_ge(s.results, i * 4)
                    act.wait_ge(s.kept_v, i * 2)
                    for n, (src, scale) in enumerate(((r.cs, KAPPA), (r.xc, KAPPA), (r.cs, -KAPPA))):
                        act.activation(e[:, n, :, :], src[:, :, ds(col, P)], ACT.Exp, scale=scale).then_inc(s.decays, 1)
                    for n, (dst, bank) in enumerate(((ag[:, :, 0, :], 6), (bht[:, :, :], 7), (kht[:, :, :], 6))):
                        act.wait_ge(s.turned, i * 3 + n + 1)
                        act.activation(dst, by_db(ps[:, bank, :], 8), ACT.Copy).then_inc(s.turned_kept, 1)
                    act.wait_ge(s.g0_made, i + 1)
                    act.activation(ag[:, :, 1, :], ps[:, 7, :].rearrange("p (u n) -> p u n", u=8), ACT.Copy).then_inc(s.g0_kept, 1)
                    for lv in range(5):
                        for d in range(2):
                            act.wait_ge(s.y_made, i * 10 + lv * 2 + d + 1)
                            act.activation(y[:, d:8:2, :], by_db(ps[:, 4 + d, 0:256]),
                                           ACT.Copy).then_inc(s.y_kept, 1)
                    act.wait_ge(s.tag_made, i * 2 + 2)
                    act.activation(tag[:, 1:8:2, :], by_db(ps[:, 3, :]), ACT.Copy).then_inc(s.tag_kept_s, 1)
                    act.wait_ge(s.results, i * 4 + 3)
                    act.activation(r.yl[:, ds(i, 1), :].squeeze(1), ps[:, 2, 0:256], ACT.Copy).then_inc(s.kept_s, 1)
                    act.wait_ge(s.results, i * 4 + 4)
                    act.activation(by_ck(r.hh, col), from_ck(5, 0), ACT.Copy).then_inc(s.kept_s, 1)

            @block.vector
            def _(dve):
                for d in range(2):
                    strict, incl, other = (TRI_LT, TRI_LE, TRI_GT) if d == 0 else (TRI_GT, TRI_GE, TRI_LT)
                    dve.tensor_copy(mk[:, d, 0:CH], tri[strict]).then_inc(s.masks, 1)
                    dve.tensor_copy(mk[:, d, CH:], tri[incl]).then_inc(s.masks, 1)
                    dve.tensor_tensor(m0[:, d, :], tri[other], lm[0], ALU.mult).then_inc(s.masks, 1)
                dve.wait_ge(s.masks, 6)
                with dve.Fori(0, NT) as i:
                    col = i * P
                    dve.wait_ge(s.decays, i * 3 + 3)
                    dve.tensor_copy(wend[:, 0:4].rearrange("p (b c) -> p b c", b=2), e[:, 0, 0:2, CH - 1:P:CH]).then_inc(s.tildes, 1)
                    dve.tensor_copy(wend[:, 4:8].rearrange("p (b c) -> p b c", b=2), e[:, 0, 2:4, 0:P:CH]).then_inc(s.tildes, 1)
                    for d in range(2):
                        for n, (decay, src) in enumerate(((1, r.nkk), (0, g.fm[:, 0:2, :]))):
                            dve.tensor_tensor(ar[:, n, 2 * d:2 * d + 2, :], e[:, decay, 2 * d:2 * d + 2, :],
                                              src[:, :, ds(col, P)], ALU.mult).then_inc(s.tildes, 1)
                    dve.tensor_tensor(bt[:, :, :], e[:, 2, :, :], r.b[:, :, ds(col, P)], ALU.mult).then_inc(s.tildes, 1)
                    dve.tensor_tensor(kt[:, :, :], e[:, 2, :, :], r.kd[:, :, ds(col, P)], ALU.mult).then_inc(s.tildes, 1)
                    for par in range(2):
                        dve.wait_ge(s.products, i * 2 + par + 1)

                        def by_d(v):
                            return v.rearrange("p (d b) n -> p d b n", d=2)

                        for dst, bank in ((lb, par), (lk, 2 + par)):
                            dve.tensor_tensor(by_d(dst[:, par:8:2, :]), by_d(by_db(ps[:, bank, :])),
                                              spread(mk[:, :, :], 2, 2), ALU.mult).then_inc(s.masked, 1)
                        dve.tensor_tensor(by_d(tu[:, par, 0, :, :]), by_d(by_db(ps[:, 4 + par, 0:256])),
                                          spread(m0[:, :, :], 2, 2), ALU.mult).then_inc(s.masked, 1)
                        dve.wait_ge(s.masked, i * 8 + par * 4 + 3)
                        dve.tensor_tensor(tu[:, par, 1, :, :], lb[:, par:8:2, 0:CH], spread(lm[0], 1, 4), ALU.mult).then_inc(s.masked, 1)
                        dve.wait_ge(s.masked, i * 8 + par * 4 + 4)
                        tud = tu[:, par, :, :, :].rearrange("p a h n -> p (a h) n")
                        dve.tensor_tensor(tud, tud, spread(i64, 1, 8), ALU.add).then_inc(s.inverse, 1)
                    for lv in range(5):
                        for d in range(2):
                            n = lv * 2 + d
                            dve.wait_ge(s.step_made, i * 10 + n + 1)
                            dve.wait_ge(s.inverse, i * 12 + n + 1)
                            if lv < 4:
                                dst, src = tu[:, d, :, :, :].rearrange("p a h n -> p (a h n)"), ps[:, d, :]
                            else:
                                dst, src = tu[:, d, 1, :, :].rearrange("p h n -> p (h n)"), ps[:, d, 256:512]
                            dve.tensor_tensor(dst, dst, src, ALU.add).then_inc(s.inverse, 1)
                    dve.wait_ge(s.tag_made, i * 2 + 1)
                    dve.tensor_copy(tag[:, 0:8:2, :], by_db(ps[:, 2, :])).then_inc(s.tag_kept_v, 1)
                    dve.wait_ge(s.results, i * 4 + 2)
                    dve.tensor_tensor(by_ck(r.pt, col), from_ck(0, 0), ar[:, 1, :, :].rearrange("p b (c n) -> p b c n", c=2),
                                      ALU.add).then_inc(s.kept_v, 1)
                    dve.wait_ge(s.hats, i * 3 + 3)
                    dve.tensor_tensor(by_ck(r.mt, col), from_ck(0, 256), e[:, 2, :, :].rearrange("p b (c n) -> p b c n", c=2),
                                      ALU.add).then_inc(s.kept_v, 1)

            @block.gpsimd
            def _(pool):
                with pool.Fori(0, NT) as i:
                    pool.wait_ge(s.results, i * 4)
                    pool.tensor_copy(vt[:, :], g.vb[:, ds(i, 1), :].squeeze(1)).then_inc(s.v_staged, 1)
                    pool.wait_ge(s.tildes, i * 8 + 8)
                    w8 = spread(wend[:, :], 2, CH)
                    for dst, src in ((bh, bt), (kh, kt)):
                        pool.tensor_tensor(dst.rearrange("p b (c n) -> p (b c) n", c=2),
                                           src[:, :, :].rearrange("p b (c n) -> p (b c) n", c=2), w8, ALU.mult).then_inc(s.hats, 1)
                    pool.tensor_tensor(dg, spread(i64, 1, 8), w8, ALU.mult).then_inc(s.hats, 1)
                    for d in range(2):
                        pool.wait_ge(s.masked, i * 8 + d * 4 + 1)
                        for lv in range(5):
                            pool.tensor_tensor(nl[:, lv, d:8:2, :], lb[:, d:8:2, 0:CH],
                                               spread(lm[lv + 1], 1, 4), ALU.mult).then_inc(s.levels, 1)

            @block.tensor
            def _(pe):
                def pe_wait(sem, value):
                    pe.wait_ge(sem, value)
                    pe.sem_inc(s.passed, 1)

                with pe.Fori(0, NT) as i:
                    pe_wait(s.tildes, i * 8 + 8)
                    pe_wait(s.kept_v, i * 2)
                    pe_wait(s.kept_s, i * 2)
                    pe_wait(s.tag_kept_s, i)
                    for par in range(2):
                        ch = half[par]
                        for db in range(4):
                            for ck in range(2):
                                st, steps = half[ck], slice(ck * CH, ck * CH + CH)
                                for bank, lhs in ((par, bt), (2 + par, kt)):
                                    pe.matmul(ps[st, bank, db * 128:db * 128 + 128].rearrange("p (a n) -> p a n", a=2),
                                              lhs[ch, db, steps], ar[ch, :, db, steps], start=True, stop=True)
                                mm = pe.matmul(ps[st, 4 + par, db * CH:db * CH + CH], ar[ch, 0, db, steps], bt[ch, db, steps],
                                               start=True, stop=True)
                        mm.then_inc(s.products, 1)
                    for n, (src, bank) in enumerate(((ar[:, 0, :, :], 6), (bh, 7), (kh, 6))):
                        if n:
                            pe_wait(s.hats, i * 3 + n)
                        if n == 2:
                            pe_wait(s.turned_kept, i * 3 + 1)
                        for db in range(4):
                            mm = pe.transpose(ps[:, bank, db * P:db * P + P], src[:, db, :], g.ident)
                        mm.then_inc(s.turned, 1)
                    pe_wait(s.turned_kept, i * 3 + 3)
                    pe_wait(s.masked, i * 8 + 7)
                    pe_wait(s.v_staged, i + 1)
                    for par, db, ck in units:
                        st, u = half[ck], 2 * db + par
                        mm = pe.matmul(ps[st, 7, u * CH:u * CH + CH], lk[st, u, 0:CH], vt[st, value(par, db)], start=True, stop=True)
                    mm.then_inc(s.g0_made, 1)
                    for lv in range(5):
                        for par in range(2):
                            pe_wait(s.levels, i * 10 + par * 5 + lv + 1)
                            pe_wait(s.inverse, i * 12 + lv * 2 + par + 1)
                            for db in range(4):
                                for st in half:
                                    mm = pe.matmul(ps[st, 4 + par, db * CH:db * CH + CH], nl[st, lv, 2 * db + par, :],
                                                   tu[st, par, 0, db, :], start=True, stop=True)
                            mm.then_inc(s.y_made, 1)
                        for par in range(2):
                            pe_wait(s.y_kept, i * 10 + lv * 2 + par + 1)
                            for db in range(4):
                                for st in half:
                                    t_, y_, c = tu[st, par, 1, db, :], y[st, 2 * db + par, :], db * CH
                                    if lv < 4:
                                        pe.matmul(ps[st, par, c:c + CH], t_, y_, start=True, stop=True)
                                    mm = pe.matmul(ps[st, par, 256 + c:256 + c + CH], y_, t_, start=True, stop=True)
                            mm.then_inc(s.step_made, 1)
                    pe_wait(s.g0_kept, i + 1)
                    for par in range(2):
                        pe_wait(s.inverse, i * 12 + 11 + par)
                        for db in range(4):
                            for st in half:
                                mm = pe.matmul(ps[st, 2 + par, db * 128:db * 128 + 128], tu[st, par, 1, db, :],
                                               ag[st, 2 * db + par, :, :].rearrange("p a n -> p (a n)"), start=True, stop=True)
                        mm.then_inc(s.tag_made, 1)
                    pe_wait(s.tag_kept_v, i + 1)
                    pe_wait(s.tag_kept_s, i + 1)
                    for base, rhs in ((0, lambda st, u: lb[st, u, CH:]), (256, lambda st, u: bht[st, u, :])):
                        for par, db, ck in units:
                            u, st, ch, c = 2 * db + par, half[ck], half[par], base + db * CH
                            mm = pe.matmul(ps[ch, ck, c:c + CH], tag[st, u, 0:CH], rhs(st, u), start=True, stop=True)
                        mm.then_inc(s.results, 1)
                    for h in range(4):
                        for st in half:
                            for d in range(2):
                                u, o = d * 4 + h, ps[st, 2, h * HD:h * HD + HD]
                                pe.matmul(o, lb[st, u, CH:], tag[st, u, CH:], start=(d == 0), stop=False)
                                mm = pe.matmul(o, lk[st, u, CH:], vt[st, h * HD:h * HD + HD], start=False, stop=(d == 1))
                    mm.then_inc(s.results, 1)
                    for par, db, ck in units:
                        u, st, ch = 2 * db + par, half[ck], half[par]
                        o = ps[ch, 5 + ck, db * CH:db * CH + CH]
                        pe.matmul(o, bht[st, u, :], tag[st, u, CH:], start=True, stop=False)
                        mm = pe.matmul(o, kht[st, u, :], vt[st, value(par, db)], start=False, stop=True)
                    mm.then_inc(s.results, 1)


def rwkv_readout(nc, g, r, layer):
    order = [list(range(NCH)), list(range(NCC - 1, -1, -1)) + list(range(NCH - 1, NCC - 1, -1))]
    with ExitStack() as stack:
        a = Scope(nc, stack)
        xs = a.sb("ro_xs", [P, 4, NCH, CH])
        gate = a.sb("ro_gate", [P, NT, B_W])
        gup, ln = a.sb("ro_gup", [P, B_W]), a.sb("ro_ln", [P, 2, B_W])
        tmp = a.sb("ro_tmp", [P, NT * B_HEADS, HD])
        st = a.sb("ro_st", [P, 4, NT * B_HEADS])
        sps = a.ps("ro_sps", [P, 2, B_W])
        yps = a.ps("ro_yps", [P, 2, 2, 512])
        gps = a.ps("ro_gps", [P, 2, 512])
        tps = gps
        loaded, zeroed, moved, stepped = g.sem("ro_loaded"), g.sem("ro_zeroed"), g.sem("ro_moved"), g.sem("ro_stepped")
        read, added, gated, gate_kept = g.sem("ro_read"), g.sem("ro_added"), g.sem("ro_gated"), g.sem("ro_gate_kept")
        chain, var, root, done = g.sem("ro_chain"), g.sem("ro_var"), g.sem("ro_root"), g.sem("ro_done")
        vbon, turned, kept = g.sem("ro_vbonus"), g.sem("ro_turned"), g.sem("ro_kept")
        yh = r.yl[:, :, :].rearrange("p t (h n) -> p (t h) n", h=B_HEADS)
        yf = r.yl[:, :, :]
        with nc.Block(no_gpsimd_drain=True) as block:

            @block.sync
            def _(sync):
                sync.dma_start(gup[:, :], at(g.g_up, layer)).then_inc(loaded, 16)
                sync.dma_start(ln[:, :, :].rearrange("p a n -> p (a n)"),
                               at(g.rows_d, layer)[R_LNW:R_LNW + 2 * B_W].partition_broadcast(P)).then_inc(loaded, 16)

            @block.tensor
            def _(pe):
                pe.wait_ge(zeroed, 2)
                for n in range(NCH - 1):
                    if n:
                        pe.wait_ge(stepped, 2 * n)
                    for d in range(2):
                        c = order[d][n]
                        for blk in range(2):
                            for par in (0, 64):
                                ch, db = slice(par, par + 64), 2 * d + blk
                                mm = pe.matmul(sps[ch, n % 2, db * CH:db * CH + CH], r.mt[ch, db, c * CH:c * CH + CH],
                                               xs[ch, db, c, :], start=True, stop=True)
                    mm.then_inc(moved, 1)
                    if n < NT:
                        if n == 0:
                            pe.wait_ge(loaded, 32)
                        if n >= 2:
                            pe.wait_ge(gate_kept, n - 1)
                        pe.matmul(gps[:, n % 2, 0:B_W], g.fm[:, 6, n * P:(n + 1) * P], gup[:, :], start=True, stop=True).then_inc(gated, 1)
                pe.wait_ge(stepped, 2 * (NCH - 1))
                for t in range(NT):
                    if t >= 2:
                        pe.wait_ge(added, t - 1)
                    for h in range(B_HEADS):
                        for ck in range(2):
                            for d in range(2):
                                ch, db, c = slice((h % 2) * 64, (h % 2) * 64 + 64), 2 * d + h // 2, 2 * t + ck
                                mm = pe.matmul(yps[ck * 64:ck * 64 + 64, t % 2, h % 2, (h // 2) * HD:(h // 2) * HD + HD],
                                               r.pt[ch, db, c * CH:c * CH + CH], xs[ch, db, c, :], start=(d == 0), stop=(d == 1))
                    mm.then_inc(read, 1)
                for t in range(NT):
                    pe.wait_ge(done, 1)
                    if t >= 2:
                        pe.wait_ge(kept, t - 1)
                    for j in range(2):
                        mm = pe.transpose(tps[:, t % 2, j * P:(j + 1) * P], r.yl[:, t, j * P:(j + 1) * P], g.ident)
                    mm.then_inc(turned, 1)

            @block.gpsimd
            def _(pool):
                pool.tensor_tensor(g.vb[:, :, :].rearrange("p t (h n) -> p (t h) n", h=B_HEADS),
                                   g.vb[:, :, :].rearrange("p t (h n) -> p (t h) n", h=B_HEADS),
                                   spread(r.bonus[:, :, :].rearrange("p t h -> p (t h)"), 2, HD), ALU.mult).then_inc(vbon, 1)

            @block.scalar
            def _(act):
                for t in range(NT):
                    act.wait_ge(gated, t + 1)
                    act.activation(gate[:, t, :], gps[:, t % 2, 0:B_W], ACT.Copy).then_inc(gate_kept, 1)
                act.wait_ge(var, 1)
                act.activation(st[:, 2, :], st[:, 1, :], ACT.Sqrt).then_inc(root, 1)
                for t in range(NT):
                    act.wait_ge(turned, t + 1)
                    act.activation(g.mixT[:, 4:6, t * P:(t + 1) * P], tps[:, t % 2, 0:2 * P].rearrange("p (j n) -> p j n", j=2),
                                   ACT.Copy).then_inc(kept, 1)

            @block.vector
            def _(dve):
                link = Link(dve, chain)
                for d in range(2):
                    dve.memset(xs[:, 2 * d:2 * d + 2, order[d][0], :], 0.0).then_inc(zeroed, 1)
                for n in range(NCH - 1):
                    dve.wait_ge(moved, n + 1)
                    for d in range(2):
                        c, nxt, q = order[d][n], order[d][n + 1], slice(2 * d, 2 * d + 2)
                        dve.tensor_tensor(xs[:, q, nxt, :], sps[:, n % 2, 128 * d:128 * d + 128].rearrange("p (b n) -> p b n", b=2),
                                          r.hh[:, q, c * CH:c * CH + CH], ALU.add).then_inc(stepped, 1)
                for t in range(NT):
                    dve.wait_ge(read, t + 1)
                    yt = r.yl[:, t, :].rearrange("p (b a n) -> p a b n", b=2, a=2)
                    dve.tensor_tensor(yt, yt, yps[:, t % 2, :, 0:P].rearrange("p a (b n) -> p a b n", b=2),
                                      ALU.add).then_inc(added, 1)
                dve.wait_ge(added, NT)
                link(dve.tensor_reduce(st[:, 0, :], yh, AX_X, ALU.add))
                link(dve.tensor_scalar(st[:, 0, :], st[:, 0, :], 1.0 / HD, None, ALU.mult))
                link(dve.tensor_tensor(yh, yh, spread(st[:, 0, :], 2, HD), ALU.subtract))
                link(dve.tensor_tensor(tmp[:, :, :], yh, yh, ALU.mult))
                link(dve.tensor_reduce(st[:, 1, :], tmp[:, :, :], AX_X, ALU.add))
                dve.tensor_scalar(st[:, 1, :], st[:, 1, :], 1.0 / HD, LNX_EPS, ALU.mult, ALU.add).then_inc(var, 1)
                dve.wait_ge(root, 1)
                link(dve.reciprocal(st[:, 3, :], st[:, 2, :]))
                link(dve.tensor_tensor(yh, yh, spread(st[:, 3, :], 2, HD), ALU.mult))
                dve.wait_ge(loaded, 32)
                link(dve.tensor_tensor(yf, yf, spread(ln[:, 0, :], 1, NT), ALU.mult))
                link(dve.tensor_tensor(yf, yf, spread(ln[:, 1, :], 1, NT), ALU.add))
                dve.wait_ge(vbon, 1)
                link(dve.tensor_tensor(yf, yf, g.vb[:, :, :], ALU.add))
                dve.wait_ge(gate_kept, NT)
                dve.tensor_tensor(yf, yf, gate[:, :, :], ALU.mult).then_inc(done, 1)


def rwkv(nc, g, layer):
    with ExitStack() as stack:
        a, r = Scope(nc, stack), Buffers()
        r.cs = g.fm[:, 7:11, :]
        r.yl = a.sb("rk_yl", [P, NT, B_W])
        r.bonus = a.sb("rk_bonus", [P, NT, B_HEADS])
        r.pt, r.mt, r.hh = (a.sb("rk_" + n, [P, 4, T]) for n in ("pt", "mt", "hh"))
        with ExitStack() as chunks:
            c = Scope(nc, chunks)
            r.xc, r.b, r.kd = (c.sb("rk_" + n, [P, 4, T]) for n in ("xc", "b", "kd"))
            r.nkk = c.sb("rk_nkk", [P, 2, T])
            rwkv_gates(nc, g, r, layer)
            rwkv_chunks(nc, g, r, layer)
        rwkv_readout(nc, g, r, layer)




def mix_out(nc, g, layer):
    with ExitStack() as stack:
        a = Scope(nc, stack)
        x, z = a.sb("mo_x", [P, NT, D]), a.sb("mo_z", [P, 2, D])
        w, gate = a.sb("mo_w", [P, KD, D]), a.sb("mo_gate", [P, 2, D])
        junk, st = a.sb("mo_junk", [P, D]), a.sb("mo_st", [P, 4, NT])
        ps = a.ps("mo_ps", [P, 3, D])
        names = ("w_loaded", "rows_loaded", "made", "squared", "var", "root", "inv", "scaled", "added", "stored")
        s = Buffers()
        (s.w_loaded, s.rows_loaded, s.made, s.squared, s.var, s.root, s.inv, s.scaled, s.added, s.stored) = (g.sem("mo_" + n) for n in names)
        x_loaded = [g.sem(f"mo_x_loaded{t}") for t in range(NT)]
        with nc.Block(no_gpsimd_drain=True) as block:

            @block.sync
            def _(sync):
                sync.dma_start(w[:, :, :], at(g.w_out, layer).rearrange("(k p) n -> p k n", p=P)).then_inc(s.w_loaded, 16)
                load_mod_rows(sync, g, gate, 2, s.rows_loaded)
                for t in range(NT):
                    sync.dma_start(x[:, t, :], g.stream[t * P:(t + 1) * P, :]).then_inc(x_loaded[t], 16)
                for t in range(NT):
                    sync.wait_ge(s.added, t + 1)
                    sync.dma_start(g.stream[t * P:(t + 1) * P, :], x[:, t, :]).then_inc(s.stored, 16)
                sync.wait_ge(s.stored, 16 * NT)

            @block.tensor
            def _(pe):
                pe.wait_ge(s.w_loaded, 16)
                for t in range(NT):
                    if t >= 3:
                        pe.wait_ge(s.scaled, t - 2)
                    for half in range(2):
                        for k in range(KD):
                            mm = pe.matmul(ps[:, t % 3, half * 512:half * 512 + 512], g.mixT[:, k, t * P:(t + 1) * P],
                                           w[:, k, half * 512:half * 512 + 512], start=(k == 0), stop=(k == KD - 1))
                    mm.then_inc(s.made, 1)

            @block.scalar
            def _(act):
                for t in range(NT):
                    act.wait_ge(s.made, t + 1)
                    act.wait_ge(s.squared, t)
                    act.activation(junk[:, :], ps[:, t % 3, :], ACT.Square, accum_out=st[:, 0, t:t + 1]).then_inc(s.squared, 1)
                    act.wait_ge(s.var, t + 1)
                    act.activation(st[:, 2, t:t + 1], st[:, 1, t:t + 1], ACT.Sqrt).then_inc(s.root, 1)

            @block.vector
            def _(dve):
                for t in range(NT):
                    dve.wait_ge(s.squared, t + 1)
                    dve.tensor_scalar(st[:, 1, t:t + 1], st[:, 0, t:t + 1], 1.0 / D, EPS, ALU.mult, ALU.add).then_inc(s.var, 1)
                    dve.wait_ge(s.root, t + 1)
                    dve.reciprocal(st[:, 3, t:t + 1], st[:, 2, t:t + 1]).then_inc(s.inv, 1)
                    dve.wait_ge(s.inv, t + 1)
                    if t == 0:
                        dve.wait_ge(s.rows_loaded, 32)
                    if t >= 2:
                        dve.wait_ge(s.added, t - 1)
                    dve.scalar_tensor_tensor(z[:, t % 2, :], ps[:, t % 3, :], st[:, 3, t:t + 1], gate[:, int(t >= NTC), :],
                                             ALU.mult, ALU.mult).then_inc(s.scaled, 1)

            @block.gpsimd
            def _(pool):
                for t in range(NT):
                    pool.wait_ge(s.scaled, t + 1)
                    pool.wait_ge(x_loaded[t], 16)
                    pool.tensor_tensor(x[:, t, :], x[:, t, :], z[:, t % 2, :], ALU.add).then_inc(s.added, 1)



W_SLOTS = 3


def expert_matrix(g, layer, pair, q):
    kind, e = ((g.w_gate_e, 0), (g.w_up_e, 0), (g.w_gate_e, 1), (g.w_up_e, 1), (g.w_down_e, 0), (g.w_down_e, 1))[q]
    return at(at(kind, layer), pair * 2 + e).rearrange("(p k) n -> p k n", k=KD)


def routing(nc, g, f, layer):
    with ExitStack() as stack:
        a = Scope(nc, stack)
        gain, shift = a.sb("rt_gain", [P, 2, D]), a.sb("rt_shift", [P, 2, D])
        junk, st = a.sb("rt_junk", [P, D]), a.sb("rt_st", [P, 24])
        hT, wr = a.sb("rt_hT", [P, 2, KD, P]), a.sb("rt_wr", [P, KD, NE])
        lg, sm = a.sb("rt_lg", [P, NT, NE]), a.sb("rt_sm", [P, 3, NT])
        affT, work, sel, rank = (a.sb("rt_" + n, [NE, T]) for n in ("affT", "work", "sel", "rank"))
        ones, best = a.sb("rt_ones", [NE, SEQ]), a.sb("rt_best", [NE, 8])
        tp = a.ps("rt_tp", [P, 2, 4, P])
        lps = a.ps("rt_lps", [P, NT, NE])
        aps = a.ps("rt_aps", [NE, 1024])
        sps = a.ps("rt_sps", [P, NT, NE])
        norm = PreNorm(g, "rt", f.h, f.h, gain, shift, junk, st)
        x_loaded = [g.sem(f"rt_x_loaded{t}") for t in range(NT)]
        rows_loaded, turned, hT_ready = g.sem("rt_rows_loaded"), g.sem("rt_turned"), g.sem("rt_hT_ready")
        routed, chain, centred, exped = g.sem("rt_routed"), g.sem("rt_chain"), g.sem("rt_centred"), g.sem("rt_exped")
        zeroed = g.sem("rt_zeroed")
        aff_ready, aff_turned = g.sem("rt_aff_ready"), g.sem("rt_aff_turned")
        slots_ready, slots_turned = g.sem("rt_slots_ready"), g.sem("rt_slots_turned")
        lgf = lg[:, :, :]
        with nc.Block(no_gpsimd_drain=True) as block:

            @block.sync
            def _(sync):
                for t in range(NT):
                    sync.dma_start(f.h[:, t, :], g.stream[t * P:(t + 1) * P, :]).then_inc(x_loaded[t], 16)
                load_mod_rows(sync, g, gain, 4, rows_loaded)
                load_mod_rows(sync, g, shift, 3, rows_loaded)
                sync.dma_start(wr[:, :, :], at(g.w_router, layer).rearrange("(k p) n -> p k n", p=P)).then_inc(rows_loaded, 16)
                for q in range(W_SLOTS):
                    sync.dma_start(f.w[:, q, :, :], expert_matrix(g, layer, 0, q)).then_inc(f.w_loaded[q], 16)

            @block.scalar
            def _(act):
                norm.scalar(act, lambda e, t: e.wait_ge(x_loaded[t], 16))
                for n in range(2 * NT):
                    act.wait_ge(turned, n + 1)
                    t, half = n // 2, n % 2
                    if t >= 2:
                        act.wait_ge(routed, t - 1)
                    act.activation(hT[:, t % 2, 4 * half:4 * half + 4, :], tp[:, half, :, :], ACT.Copy).then_inc(hT_ready, 1)
                act.wait_ge(centred, 1)
                act.activation(lgf, lgf, ACT.Exp).then_inc(exped, 1)

            @block.gpsimd
            def _(pool):
                norm.gpsimd(pool)
                pool.memset(f.acc[:, :, :], 0.0).then_inc(zeroed, 1)
                pool.wait_ge(zeroed, 1)

            @block.tensor
            def _(pe):
                def route(t):
                    pe.wait_ge(hT_ready, 2 * t + 2)
                    for k in range(KD):
                        mm = pe.matmul(lps[:, t, :], hT[:, t % 2, k, :], wr[:, k, :], start=(k == 0), stop=(k == KD - 1))
                    mm.then_inc(routed, 1)

                pe.wait_ge(rows_loaded, 80)
                for t in range(NT):
                    pe.wait_ge(norm.shifted, t + 1)
                    for half in range(2):
                        if t:
                            pe.wait_ge(hT_ready, 2 * t - 1 + half)
                        for j in range(4):
                            k = 4 * half + j
                            mm = pe.transpose(tp[:, half, j, :], f.h[:, t, k * P:(k + 1) * P], g.ident)
                        mm.then_inc(turned, 1)
                    if t:
                        route(t - 1)
                route(NT - 1)
                pe.wait_ge(aff_ready, 1)
                for t in range(NT):
                    mm = pe.transpose(aps[:, t * P:(t + 1) * P], f.aff[:, t, :], g.ident)
                mm.then_inc(aff_turned, 1)
                pe.wait_ge(slots_ready, 1)
                for t in range(NT):
                    mm = pe.transpose(sps[:, t, :], rank[:, t * P:(t + 1) * P], g.cst[0:NE, O_ID:O_ID + NE])
                mm.then_inc(slots_turned, 1)

            @block.vector
            def _(dve):
                link = Link(dve, chain)
                norm.vector(dve, lambda e: e.wait_ge(rows_loaded, 80))
                link(dve.memset(ones[:, :], 1.0))
                dve.wait_ge(routed, NT)
                link(dve.tensor_reduce(sm[:, 0, :], lps[:, :, :], AX_X, ALU.max))
                dve.tensor_tensor(lgf, lps[:, :, :], spread(sm[:, 0, :], 2, NE), ALU.subtract).then_inc(centred, 1)
                dve.wait_ge(exped, 1)
                link(dve.tensor_reduce(sm[:, 1, :], lgf, AX_X, ALU.add))
                link(dve.reciprocal(sm[:, 2, :], sm[:, 1, :]))
                dve.tensor_tensor(f.aff[:, :, :], lgf, spread(sm[:, 2, :], 2, NE), ALU.mult).then_inc(aff_ready, 1)
                dve.wait_ge(aff_turned, 1)
                link(dve.tensor_copy(work[:, :], aps[:, 0:T]))
                for lo, hi, cap in ((0, CTX, CAP_C), (CTX, T, CAP_L)):
                    for _ in range(cap // 8):
                        link(dve.max(best[:, :], work[:, lo:hi]))
                        link(dve.match_replace(work[:, lo:hi], best[:, :], work[:, lo:hi], -1.0))
                link(dve.tensor_scalar(sel[:, :], work[:, :], 0.0, None, ALU.is_lt))
                for lo, hi in ((0, CTX), (CTX, T)):
                    link(dve.tensor_tensor_scan(rank[:, lo:hi], ones[:, 0:hi - lo], sel[:, lo:hi], 0.0, ALU.mult, ALU.add))
                link(dve.tensor_tensor(rank[:, :], rank[:, :], sel[:, :], ALU.mult))
                dve.tensor_scalar(rank[:, :], rank[:, :], 1.0, None, ALU.subtract).then_inc(slots_ready, 1)
                dve.wait_ge(slots_turned, 1)
                dve.tensor_copy(f.slot[:, :, :], sps[:, :, :])



U_GATHER, U_TURN_PICK, U_TURN_HID, U_SCATTER = 4, 2, 2, 12
NTL = NT - NTC


def experts(nc, g, f, layer):
    first_uses = U_GATHER + U_TURN_PICK + 2 * U_TURN_HID
    uses = first_uses + U_SCATTER
    with ExitStack() as stack:
        a = Scope(nc, stack)
        pick_l, pick_c = a.sb("ex_pick_l", [P, NTL, 2, CAP_L]), a.sb("ex_pick_c", [P, NTC, 2, CAP_C])
        wt_l, wt_c = a.sb("ex_wt_l", [P, NTL, 2, CAP_L]), a.sb("ex_wt_c", [P, NTC, 2, CAP_C])
        wtT_l, wtT_c = a.sb("ex_wtT_l", [P, NTL * P]), a.sb("ex_wtT_c", [2 * CAP_C, NTC * P])
        xe = a.sb("ex_xe", [P, KD, 2, CAP])
        sg, hid = a.sb("ex_sg", [CAP, DE]), a.sb("ex_hid", [CAP, DE])
        hidT = a.sb("ex_hidT", [P, KD, CAP])
        ye_l, ye_c = a.sb("ex_ye_l", [P, D]), a.sb("ex_ye_c", [2 * CAP_C, D])
        misc = a.ps("ex_misc", [P, 2, 512])
        gp, up, yp = (a.ps("ex_" + n, [CAP, 2, 512]) for n in ("gp", "up", "yp"))
        names = ("picked", "weighted", "used", "free", "silu", "hid", "gate_made", "up_made", "down_made",
                 "ye_kept", "w_used")
        s = Buffers()
        (s.picked, s.weighted, s.used, s.free, s.silu, s.hid, s.gate_made, s.up_made, s.down_made,
         s.ye_kept, s.w_used) = (g.sem("ex_" + n) for n in names)

        def start(j, peeled):
            return 0 if peeled else (j - 1) * uses + first_uses

        def layout_uses(peeled):
            at_, order = {}, ["gather"] * U_GATHER + ([] if peeled else ["scatter"] * U_SCATTER) + \
                ["pick"] * U_TURN_PICK + ["hid0"] * U_TURN_HID + ["hid1"] * U_TURN_HID
            for n, what in enumerate(order):
                at_.setdefault(what, n)
            return at_

        scatter_places = [(t, half) for t in range(NT) for half in range(2)]

        def both(eng, body):
            body(0, True)
            with eng.Fori(1, NE // 2) as j:
                body(j, False)

        def scatter_pe(pe, m0):
            for n, (t, half) in enumerate(scatter_places):
                take(pe, m0 + n, n)
                cols = slice(half * 512, half * 512 + 512)
                if t < NTC:
                    mm = pe.matmul(misc[:, n % 2, :], wtT_c[:, t * P:(t + 1) * P], ye_c[:, cols], start=True, stop=True)
                else:
                    c = (t - NTC) * P
                    mm = pe.matmul(misc[:, n % 2, :], wtT_l[:, c:c + P], ye_l[:, cols], start=True, stop=True)
                mm.then_inc(s.used, 1)

        def take(pe, m, n):
            if not (isinstance(m, int) and m < 2):
                pe.wait_ge(s.free, m - 1)

        def scatter_vector(dve, m0):
            for n, (t, half) in enumerate(scatter_places):
                dve.wait_ge(s.used, m0 + n + 1)
                acc = f.acc[:, t, half * 512:half * 512 + 512]
                dve.tensor_tensor(acc, acc, misc[:, n % 2, :], ALU.add).then_inc(s.free, 1)

        with nc.Block(no_gpsimd_drain=True) as block:

            @block.sync
            def _(sync):
                def body(j, peeled):
                    for q in range(6):
                        if peeled and q < W_SLOTS:
                            continue
                        sync.wait_ge(s.w_used, j * 6 + q - W_SLOTS + 1)
                        sync.dma_start(f.w[:, q % W_SLOTS, :, :], expert_matrix(g, layer, j, q)).then_inc(f.w_loaded[q % W_SLOTS], 16)

                both(sync, body)

            @block.tensor
            def _(pe):
                def body(j, peeled):
                    m, where = start(j, peeled), layout_uses(peeled)

                    def weights(q):
                        pe.wait_ge(f.w_loaded[q % W_SLOTS], j * 32 + (q // W_SLOTS) * 16 + 16)
                        return f.w[:, q % W_SLOTS, :, :]

                    def gate_up(e):
                        for q, out, made, read, per in ((2 * e, gp, s.gate_made, s.silu, 0), (2 * e + 1, up, s.up_made, s.hid, 0)):
                            w = weights(q)
                            if not (peeled and e == 0):
                                pe.wait_ge(read, j * 4 + e * 2)
                            for half in range(2):
                                for k in range(KD):
                                    mm = pe.matmul(out[:, half, :], xe[:, k, e, :], w[:, k, half * 512:half * 512 + 512],
                                                   start=(k == 0), stop=(k == KD - 1))
                                mm.then_inc(made, 1)
                            pe.wait_ge(made, j * 4 + e * 2 + 2)
                            pe.sem_inc(s.w_used, 1)

                    def turn_hid(e):
                        m0 = m + where[f"hid{e}"]
                        pe.wait_ge(s.hid, j * 4 + e * 2 + 2)
                        for n in range(2):
                            take(pe, m0 + n, n)
                            for i in range(4):
                                k = 4 * n + i
                                mm = pe.transpose(misc[:, n, i * CAP:(i + 1) * CAP], hid[:, k:DE:KD], g.cst[0:CAP, O_ID:O_ID + CAP])
                            mm.then_inc(s.used, 1)

                    def down(e):
                        w = weights(4 + e)
                        pe.wait_ge(s.free, m + where[f"hid{e}"] + 2)
                        if not (peeled and e == 0):
                            pe.wait_ge(s.ye_kept, j * 4 + e * 2)
                        for half in range(2):
                            for k in range(KD):
                                mm = pe.matmul(yp[:, half, :], hidT[:, k, :], w[:, k, half * 512:half * 512 + 512],
                                               start=(k == 0), stop=(k == KD - 1))
                        mm.then_inc(s.down_made, 1)
                        pe.wait_ge(s.down_made, j * 2 + e + 1)
                        pe.sem_inc(s.w_used, 1)

                    pe.wait_ge(s.picked, j * 2 + 2)
                    for n in range(U_GATHER):
                        take(pe, m + n, n)
                        for i in range(2):
                            o = misc[:, n % 2, i * 2 * CAP:(i + 1) * 2 * CAP].rearrange("p (e c) -> p e c", e=2)
                            k = 2 * n + i
                            for t in range(NTL):
                                pe.matmul(o[:, :, 0:CAP_L], f.h[:, NTC + t, k:D:KD], pick_l[:, t, :, :],
                                          start=(t == 0), stop=(t == NTL - 1))
                            for t in range(NTC):
                                mm = pe.matmul(o[:, :, CAP_L:CAP], f.h[:, t, k:D:KD], pick_c[:, t, :, :],
                                               start=(t == 0), stop=(t == NTC - 1))
                        mm.then_inc(s.used, 1)
                    pe.wait_ge(s.free, m + U_GATHER)
                    gate_up(0)
                    if not peeled:
                        pe.wait_ge(s.ye_kept, j * 4)
                        scatter_pe(pe, m + where["scatter"])
                    m0 = m + where["pick"]
                    pe.wait_ge(s.weighted, j * 2 + 2)
                    take(pe, m0, 0)
                    take(pe, m0 + 1, 1)
                    for t in range(NTL):
                        mm = pe.transpose(misc[:, 0, t * P:(t + 1) * P], wt_l[:, t, :, :].rearrange("p e c -> p (e c)"), g.ident)
                    mm.then_inc(s.used, 1)
                    for t in range(NTC):
                        mm = pe.transpose(misc[0:2 * CAP_C, 1, t * P:(t + 1) * P], wt_c[:, t, :, :].rearrange("p e c -> p (e c)"), g.ident)
                    mm.then_inc(s.used, 1)
                    turn_hid(0)
                    gate_up(1)
                    down(0)
                    turn_hid(1)
                    down(1)

                both(pe, body)
                pe.wait_ge(s.ye_kept, NE * 2)
                scatter_pe(pe, start(NE // 2, False))

            @block.scalar
            def _(act):
                def body(j, peeled):
                    def silu(e):
                        for half in range(2):
                            act.wait_ge(s.gate_made, j * 4 + e * 2 + half + 1)
                            if half == 0 and not (peeled and e == 0):
                                act.wait_ge(s.hid, j * 4 + e * 2)
                            act.activation(sg[:, half * 512:half * 512 + 512], gp[:, half, :], ACT.Silu).then_inc(s.silu, 1)

                    def keep(e):
                        act.wait_ge(s.down_made, j * 2 + e + 1)
                        act.activation(ye_l[e * CAP_L:(e + 1) * CAP_L, :], yp[0:CAP_L, :, :].rearrange("p h n -> p (h n)"),
                                       ACT.Copy).then_inc(s.ye_kept, 1)
                        act.activation(ye_c[e * CAP_C:(e + 1) * CAP_C, :], yp[CAP_L:CAP, :, :].rearrange("p h n -> p (h n)"),
                                       ACT.Copy).then_inc(s.ye_kept, 1)

                    silu(0)
                    silu(1)
                    keep(0)
                    keep(1)

                both(act, body)

            @block.vector
            def _(dve):
                def body(j, peeled):
                    m, where = start(j, peeled), layout_uses(peeled)
                    iota = g.cst[:, O_IOTA:O_IOTA + CAP_L]
                    lat, con = slice(NTC, NT), slice(0, NTC)
                    e2 = ds(j * 2, 2)
                    for dst, tiles, cap, n in ((pick_l, lat, CAP_L, NTL), (pick_c, con, CAP_C, NTC)):
                        dve.tensor_tensor(dst[:, :, :, :], spread(f.slot[:, tiles, e2], 3, cap),
                                          spread(spread(iota[:, 0:cap], 1, 2), 1, n), ALU.is_equal).then_inc(s.picked, 1)
                    dve.wait_ge(s.picked, j * 2 + 2)
                    for dst, src, tiles, cap in ((wt_l, pick_l, lat, CAP_L), (wt_c, pick_c, con, CAP_C)):
                        dve.tensor_tensor(dst[:, :, :, :], src[:, :, :, :], spread(f.aff[:, tiles, e2], 3, cap),
                                          ALU.mult).then_inc(s.weighted, 1)
                    for n in range(U_GATHER):
                        dve.wait_ge(s.used, m + n + 1)
                        dve.tensor_copy(xe[:, 2 * n:2 * n + 2, :, :].rearrange("p k e c -> p (k e c)"),
                                        misc[:, n % 2, 0:4 * CAP]).then_inc(s.free, 1)

                    def gated(e):
                        for half in range(2):
                            dve.wait_ge(s.silu, j * 4 + e * 2 + half + 1)
                            dve.wait_ge(s.up_made, j * 4 + e * 2 + half + 1)
                            c = slice(half * 512, half * 512 + 512)
                            dve.tensor_tensor(hid[:, c], sg[:, c], up[:, half, :], ALU.mult).then_inc(s.hid, 1)

                    def hid_turned(e):
                        m0 = m + where[f"hid{e}"]
                        for n in range(2):
                            dve.wait_ge(s.used, m0 + n + 1)
                            if e == 1 and n == 0:
                                dve.wait_ge(s.down_made, j * 2 + 1)
                            dve.tensor_copy(hidT[:, 4 * n:4 * n + 4, :].rearrange("p k c -> p (k c)"),
                                            misc[:, n, 0:4 * CAP]).then_inc(s.free, 1)

                    gated(0)
                    if not peeled:
                        scatter_vector(dve, m + where["scatter"])
                    m0 = m + where["pick"]
                    dve.wait_ge(s.used, m0 + 1)
                    dve.tensor_copy(wtT_l[:, :], misc[:, 0, :]).then_inc(s.free, 1)
                    dve.wait_ge(s.used, m0 + 2)
                    dve.tensor_copy(wtT_c[:, :], misc[0:2 * CAP_C, 1, 0:NTC * P]).then_inc(s.free, 1)
                    hid_turned(0)
                    gated(1)
                    hid_turned(1)

                both(dve, body)
                scatter_vector(dve, start(NE // 2, False))


def ffn_out(nc, g, f, layer):
    with ExitStack() as stack:
        a = Scope(nc, stack)
        gate, junk, st = a.sb("fo_gate", [P, 2, D]), a.sb("fo_junk", [P, D]), a.sb("fo_st", [P, 4, NT])
        names = ("rows_loaded", "squared", "var", "root", "inv", "scaled", "added", "stored")
        s = Buffers()
        (s.rows_loaded, s.squared, s.var, s.root, s.inv, s.scaled, s.added, s.stored) = (g.sem("fo_" + n) for n in names)
        x_loaded = [g.sem(f"fo_x_loaded{t}") for t in range(NT)]
        with nc.Block(no_gpsimd_drain=True) as block:

            @block.sync
            def _(sync):
                load_mod_rows(sync, g, gate, 5, s.rows_loaded)
                for t in range(NT):
                    sync.dma_start(f.h[:, t, :], g.stream[t * P:(t + 1) * P, :]).then_inc(x_loaded[t], 16)
                for t in range(NT):
                    sync.wait_ge(s.added, t + 1)
                    sync.dma_start(g.stream[t * P:(t + 1) * P, :], f.h[:, t, :]).then_inc(s.stored, 16)
                sync.wait_ge(s.stored, 16 * NT)

            @block.scalar
            def _(act):
                for t in range(NT):
                    act.activation(junk[:, :], f.acc[:, t, :], ACT.Square, accum_out=st[:, 0, t:t + 1]).then_inc(s.squared, 1)
                    act.wait_ge(s.squared, t + 1)
                act.wait_ge(s.var, 1)
                act.activation(st[:, 2, :], st[:, 1, :], ACT.Sqrt).then_inc(s.root, 1)

            @block.vector
            def _(dve):
                dve.wait_ge(s.squared, NT)
                dve.tensor_scalar(st[:, 1, :], st[:, 0, :], 1.0 / D, EPS, ALU.mult, ALU.add).then_inc(s.var, 1)
                dve.wait_ge(s.root, 1)
                dve.reciprocal(st[:, 3, :], st[:, 2, :]).then_inc(s.inv, 1)
                dve.wait_ge(s.inv, 1)
                dve.wait_ge(s.rows_loaded, 32)
                for t in range(NT):
                    dve.scalar_tensor_tensor(f.acc[:, t, :], f.acc[:, t, :], st[:, 3, t:t + 1], gate[:, int(t >= NTC), :],
                                             ALU.mult, ALU.mult).then_inc(s.scaled, 1)

            @block.gpsimd
            def _(pool):
                for t in range(NT):
                    pool.wait_ge(s.scaled, t + 1)
                    pool.wait_ge(x_loaded[t], 16)
                    pool.tensor_tensor(f.h[:, t, :], f.h[:, t, :], f.acc[:, t, :], ALU.add).then_inc(s.added, 1)


def ffn(nc, g, layer):
    with ExitStack() as stack:
        a, f = Scope(nc, stack), Buffers()
        f.h, f.acc = a.sb("ff_h", [P, NT, D]), a.sb("ff_acc", [P, NT, D])
        f.aff, f.slot = a.sb("ff_aff", [P, NT, NE]), a.sb("ff_slot", [P, NT, NE])
        f.w = a.sb("ff_w", [P, W_SLOTS, KD, D])
        f.w_loaded = [g.sem(f"ff_w_loaded{i}") for i in range(W_SLOTS)]
        routing(nc, g, f, layer)
        experts(nc, g, f, layer)
        ffn_out(nc, g, f, layer)


class Shared:

    def __init__(self, nc, stack):
        self.nc, self.stack, self.nums = nc, stack, []

    def sem(self, name):
        s = self.stack.enter_context(self.nc.semaphore(name))
        self.nums.append(s.num)
        return s

    @contextmanager
    def semaphores(self):
        outer, nums = self.stack, self.nums
        with ExitStack() as stack:
            self.stack, self.nums = stack, []
            yield
            first, last = min(self.nums), max(self.nums)
            assert last - first + 1 == len(self.nums)
            self.nc.all_engine_barrier(sems_to_clear=range(first, last + 1))
        self.stack, self.nums = outer, nums


def load_constants(nc, g, c_cols, consts, stream_in):
    loaded, silu_done, copied = g.sem("const_loaded"), g.sem("silu_done"), g.sem("stream_copied")
    with nc.Block(no_gpsimd_drain=True) as block:

        @block.sync
        def _(sync):
            sync.dma_start(g.cst[:, :], consts).then_inc(loaded, 16)
            sync.dma_start(g.silu_c[:, :, :], c_cols).then_inc(loaded, 16)
            for i, src in enumerate(stream_in):
                sync.dma_start(g.stream[i * CTX:i * CTX + src.shape[0], :], src).then_inc(copied, 16)
            sync.wait_ge(copied, 32)

        @block.scalar
        def _(act):
            act.wait_ge(loaded, 32)
            act.activation(g.silu_c[:, :, :], g.silu_c[:, :, :], ACT.Silu).then_inc(silu_done, 1)
            act.wait_ge(silu_done, 1)


def mixing(nc, g, layer):
    with ExitStack() as stack:
        m = Scope(nc, stack)
        g.mixT = m.sb("mixT", [P, KD, T])
        g.vb = m.sb("vb", [P, NT, B_W])
        g.fm = m.sb("fm", [P, 11, T])
        with ExitStack() as attending:
            a = Scope(nc, attending)
            g.qkv = a.sb("qkv", [P, NT, A_W + 2 * A_KVW])
            g.vn = a.sb("vn", [P, NT, C_W])
            projection(nc, g, layer)
            attention(nc, g, layer)
        rwkv(nc, g, layer)
        mix_out(nc, g, layer)


def build(nc, c_cols, consts, rope, x, ctx, w_mod, b_mod, gains, w_in, w_out, cols, rows, bias, w_up, a_up, g_up,
          w_router, w_e_gate, w_e_up, w_e_down, out):
    with ExitStack() as stack:
        g = Shared(nc, stack)
        g.w_mod, g.b_mod, g.gains, g.w_in, g.w_out, g.cols_d, g.rows_d = w_mod, b_mod, gains, w_in, w_out, cols, rows
        g.rope_d, g.bias_d, g.w_up, g.a_up, g.g_up, g.w_router = rope, bias, w_up, a_up, g_up, w_router
        g.w_gate_e, g.w_up_e, g.w_down_e = w_e_gate, w_e_up, w_e_down
        g.stream = nc.dram_tensor("stream", [T, D], F32).ap()
        g.mod_rows = nc.dram_tensor("mod_rows", [2, 6 * D], F32).ap()
        a = Scope(nc, stack)
        g.cst = a.sb("cst", [P, N_CST])
        g.silu_c = a.sb("silu_c", [P, KD, 2])
        g.ident = g.cst[:, O_ID:O_ID + P]
        load_constants(nc, g, c_cols, consts, [ctx, x])
        with nc.Fori(0, DEPTH) as layer:
            with g.semaphores():
                modulation(nc, g, layer)
                mixing(nc, g, layer)
            with g.semaphores():
                ffn(nc, g, layer)
        store_out(nc, g, out)


def store_out(nc, g, out):
    stored = g.sem("out_stored")
    with nc.Block(no_gpsimd_drain=True) as block:

        @block.sync
        def _(sync):
            sync.dma_start(out[0, :, :], g.stream[CTX:T, :]).then_inc(stored, 16)
            sync.wait_ge(stored, 16)


def constants():
    cst = np.zeros((P, N_CST), np.float32)
    p, r, c = np.arange(P), np.arange(P) % 64, np.arange(64)
    cst[:, O_ID:O_ID + P] = np.eye(P)
    tri = [r[:, None] < c, r[:, None] <= c, r[:, None] > c, r[:, None] >= c]
    cst[:, O_TRI:O_TRI + 256] = np.concatenate(tri, 1)
    for lv in range(6):
        same = (r[:, None] >> (lv + 1)) == (c >> (lv + 1))
        cst[:, O_LM + 64 * lv:O_LM + 64 * lv + 64] = same & ((r[:, None] >> lv) != (c >> lv))
    cst[:, O_HB:O_HB + P] = (p[:, None] // 64) == (p[None, :] // 64)
    cst[:, O_HS:O_HS + 2] = (p[:, None] // 64) == np.arange(2)
    cst[:, O_IOTA:O_IOTA + 64] = c
    cst[:, O_I64:O_I64 + 64] = r[:, None] == c
    rope = np.zeros((T, 2, HD), np.float32)
    rope[:CTX, 0] = 1.0
    inv = (np.float32(10000.0) ** (-np.arange(16, dtype=np.float32) / np.float32(16))).astype(np.float32)
    for i, pos in enumerate((np.arange(SEQ) // GRID, np.arange(SEQ) % GRID)):
        ang = pos.astype(np.float32)[:, None] * inv[None, :]
        cos, sin = np.cos(ang), np.sin(ang)
        rope[CTX:, 0, 32 * i:32 * i + 32] = np.concatenate([cos, cos], 1)
        rope[CTX:, 1, 32 * i:32 * i + 32] = np.concatenate([-sin, sin], 1)
    return cst, np.ascontiguousarray(rope.reshape(NT, P, 2 * HD).transpose(1, 0, 2))


def bias_layout(rpb):
    rp, c = np.arange(P) // GRID, np.arange(P) % GRID
    m, kc = np.arange(1, RPB_M + 1), np.arange(GRID)
    start = np.clip(c - WIN_COLS // 2, 0, GRID - WIN_COLS)
    row = m[None, :] - rp[:, None]
    col = kc[None, :] - c[:, None] + WIN_COLS - 1
    inside = (kc[None, :] >= start[:, None]) & (kc[None, :] < start[:, None] + WIN_COLS)
    padded = np.full((*rpb.shape[:3], 2 * WIN_COLS), np.float32(NEG))
    padded[..., :2 * WIN_COLS - 1] = rpb
    col = np.where(inside, col, 2 * WIN_COLS - 1)
    laid = padded[:, :, row[:, :, None], col[:, None, :]]
    return np.ascontiguousarray(laid.transpose(0, 2, 1, 3, 4)).reshape(DEPTH, P, C_HEADS * RPB_M * GRID)


def layout(inputs):
    f = {k: np.asarray(v) for k, v in inputs.items()}
    cst, rope = constants()

    def columns(v):
        return v.reshape(DEPTH, -1, P).transpose(0, 2, 1)

    both = np.stack([f["c_ctx"], f["c"][0]], axis=-1)
    arrays = {
        "c_cols": both.reshape(KD, P, 2).transpose(1, 0, 2),
        "consts": cst,
        "rope": rope,
        "x": f["x"][0],
        "ctx": f["ctx"][0],
        "w_mod": f["w_mod"],
        "b_mod": f["b_mod"],
        "gains": np.concatenate([f[n] for n in ("g_pre_mix", "g_post_mix", "g_pre_ffn", "g_post_ffn")], 1),
        "w_in": f["w_in"],
        "w_out": f["w_out"],
        "cols": np.concatenate([columns(f[n]) for n in ("rk_w0", "rk_a0", "rk_k_k", "rk_k_a", "rk_r_k")], 2),
        "rows": np.concatenate([np.tile(f["q_gain"], (1, A_HEADS)), np.tile(f["k_gain"], (1, A_KV)),
                                f["rk_lnx_w"], f["rk_lnx_b"]], 1),
        "bias": bias_layout(f["rpb"]),
        "w_up": f["rk_w_up"].reshape(DEPTH, P, B_W),
        "a_up": f["rk_a_up"].reshape(DEPTH, P, B_W),
        "g_up": f["rk_g_up"],
        "w_router": f["w_router"],
        "w_e_gate": f["w_e_gate"],
        "w_e_up": f["w_e_up"],
        "w_e_down": f["w_e_down"],
    }
    return {k: np.ascontiguousarray(v) for k, v in arrays.items()}


def kernel(**inputs):
    import concourse.bacc as bacc
    from concourse.bass_utils import run_bass_kernel_spmd

    nc = bacc.Bacc("TRN2", target_bir_lowering=False, num_devices=1)
    arrays = layout(inputs)
    args = {n: nc.dram_tensor(n, v.shape, mybir.dt.from_np(v.dtype), kind="ExternalInput").ap() for n, v in arrays.items()}
    out = nc.dram_tensor("out", (1, SEQ, D), F32, kind="ExternalOutput").ap()
    build(nc, **args, out=out)
    r = run_bass_kernel_spmd(nc, [arrays], core_ids=[0])
    return r.results[0]["out"]
```

```python
from contextlib import ExitStack, contextmanager

import numpy as np

import concourse.bass as bass
from concourse import mybir

F32 = mybir.dt.float32
F32R = mybir.dt.float32r
ACT = mybir.ActivationFunctionType
ALU = mybir.AluOpType
AX_X = mybir.AxisListType.X
ds = bass.ds

P = 128
D = 1024
KD = D // P
SEQ, CTX = 512, 256
T = SEQ + CTX
NT, NTC = T // P, CTX // P
DEPTH = 2
HD = 64
A_HEADS, A_KV = 8, 2
A_GROUP = A_HEADS // A_KV
A_W, A_KVW = A_HEADS * HD, A_KV * HD
B_HEADS, B_W = 4, 256
C_HEADS, C_W = 4, 256
N_IN = A_W + 2 * A_KVW + 3 * B_W + 3 * P + 3 * C_W
GRID = 64
WIN_ROWS, WIN_COLS = 8, 16
RPB_M = 14
NE, DE = 16, 1024
CAP_L, CAP_C = 2 * SEQ // NE, 2 * CTX // NE
CAP = CAP_L + CAP_C
EPS, LNX_EPS = 1e-6, 64e-5
SCALE = HD ** -0.5
CH = 64
NCH = T // CH
NCC = CTX // CH
KAPPA = -float(np.exp(-0.5))
NEG = -1e30

O_ID, O_TRI, O_LM, O_HB, O_HS, O_IOTA, O_I64 = 0, 128, 384, 768, 896, 898, 962
N_CST = 1026
TRI_LT, TRI_LE, TRI_GT, TRI_GE = range(4)
C_W0, C_A0, C_KK, C_KA, C_RK, N_COL = 0, 4, 8, 10, 12, 14
R_GAIN, R_LNW, R_LNB, N_ROW = 0, 640, 896, 1152


class Scope:

    def __init__(self, nc, stack, side="left"):
        self.nc, self.stack, self.side = nc, stack, side

    def sb(self, name, shape, dtype=F32):
        return self.stack.enter_context(self.nc.sbuf_tensor(name, shape, dtype, side=self.side))

    def ps(self, name, shape):
        return self.stack.enter_context(self.nc.psum_tensor(name, shape, F32))


class Link:

    def __init__(self, eng, sem, base=0):
        self.eng, self.sem, self.n, self.base = eng, sem, 0, base

    def __call__(self, ins):
        ins.then_inc(self.sem, 1)
        self.n += 1
        self.eng.wait_ge(self.sem, self.base + self.n)


def at(ap, i):
    return ap[ds(i, 1)].squeeze(0)


def spread(ap, axis, n):
    v = ap.unsqueeze(axis)
    shape = list(v.shape)
    shape[axis] = n
    return v.to_broadcast(shape)




def modulation(nc, g, j, layer):
    NCHUNK, SLOTS, W = 6 * D // 512, 4, 512
    with ExitStack() as stack:
        a = Scope(nc, stack)
        fm, qkv = (v.rearrange("p a b -> p (a b)") for v in (g.fm[:, :, :], g.qkv[:, :, :]))
        wm = [v.rearrange("p (k n) -> p k n", k=KD) for v in (fm[:, 0:KD * W], fm[:, KD * W:2 * KD * W], qkv[:, 0:KD * W])]
        wm.append(a.sb("mod_w", [P, KD, W])[:, :, :])
        rows = a.sb("mod_rows_sb", [2, 6, D])
        gains = a.sb("mod_gains", [2, 4, D])
        rowsf = rows[:, :, :].rearrange("s a b -> s (a b)")
        ps = a.ps("mod_ps", [2, SLOTS, W])
        w_loaded = [g.sem(f"mod_w_loaded{s}") for s in range(SLOTS)]
        w_free = g.sem("mod_w_free")
        rows_loaded = g.sem("mod_rows_loaded")
        prod = g.sem("mod_product")
        ps_free = g.sem("mod_ps_free")
        folded = g.sem("mod_folded")
        stored = g.sem("mod_stored")
        wv = at(g.w_mod, layer).rearrange("(k p) n -> p k n", p=P)
        with nc.Block(no_gpsimd_drain=True) as block:

            @block.sync
            def _(sync):
                sync.sem_inc(w_free, SLOTS)
                for t in range(NT):
                    sync.dma_start(j.x[:, t, :], g.stream[t * P:(t + 1) * P, :]).then_inc(j.x_loaded[t], 16)
                sync.dma_start(rowsf, at(g.b_mod, layer).partition_broadcast(2)).then_inc(rows_loaded, 16)
                sync.dma_start(gains[:, :, :].rearrange("s a b -> s (a b)"),
                               at(g.gains, layer).partition_broadcast(2)).then_inc(rows_loaded, 16)
                with sync.Fori(0, NCHUNK // SLOTS) as i:
                    for s in range(SLOTS):
                        sync.wait_ge(w_free, i * SLOTS + s + 1)
                        sync.dma_start(wm[s], wv[:, :, ds((i * SLOTS + s) * W, W)]).then_inc(w_loaded[s], 16)
                sync.wait_ge(folded, 4)
                sync.dma_start(g.mod_rows[:, :], rowsf).then_inc(stored, 16)
                for c in range(PJ_RAW):
                    load_w_in(sync, g, j, layer, c)
                sync.wait_ge(stored, 16)

            @block.scalar
            def _(act):
                j.norm.scalar(act, lambda e, t: e.wait_ge(j.x_loaded[t], 16))

            @block.tensor
            def _(pe):
                pe.sem_inc(ps_free, SLOTS)
                with pe.Fori(0, NCHUNK // SLOTS) as i:
                    for s in range(SLOTS):
                        pe.wait_ge(w_loaded[s], i * 16 + 16)
                        pe.wait_ge(ps_free, i * SLOTS + s + 1)
                        for k in range(KD):
                            mm = pe.matmul(ps[:, s, :], g.silu_c[:, k, :], wm[s][:, k, :],
                                           start=(k == 0), stop=(k == KD - 1))
                        mm.then_inc(prod, 1)
                        pe.wait_ge(prod, i * SLOTS + s + 1)
                        pe.sem_inc(w_free, 1)

            @block.vector
            def _(dve):
                j.norm.roots(dve)
                dve.wait_ge(rows_loaded, 32)
                with dve.Fori(0, NCHUNK // SLOTS) as i:
                    for s in range(SLOTS):
                        dve.wait_ge(prod, i * SLOTS + s + 1)
                        c = (i * SLOTS + s) * W
                        dve.tensor_tensor(rowsf[:, ds(c, W)], ps[:, s, :], rowsf[:, ds(c, W)],
                                          ALU.add).then_inc(ps_free, 1)
                dve.wait_ge(ps_free, SLOTS + NCHUNK)
                for sec, gain, pre in ((1, 0, True), (2, 1, False), (4, 2, True), (5, 3, False)):
                    dve.scalar_tensor_tensor(rows[:, sec, :], rows[:, sec, :], 1.0 if pre else 0.0, gains[:, gain, :],
                                             ALU.add, ALU.mult).then_inc(folded, 1)




class PreNorm:

    def __init__(self, g, name, x, h, gain, shift, junk, stats):
        self.x, self.h, self.gain, self.shift, self.junk, self.st = x, h, gain, shift, junk, stats
        self.squares, self.var, self.root, self.inv, self.scaled, self.shifted = (
            g.sem(f"{name}_{n}") for n in ("squares", "var", "root", "inv", "scaled", "shifted"))

    def scalar(self, act, x_ready):
        for t in range(NT):
            x_ready(act, t)
            act.activation(self.junk, self.x[:, t, :], ACT.Square,
                           accum_out=self.st[:, t:t + 1]).then_inc(self.squares, 1)
            act.wait_ge(self.squares, t + 1)
        act.wait_ge(self.var, 1)
        act.activation(self.st[:, 8:8 + NT], self.st[:, 8:8 + NT], ACT.Sqrt).then_inc(self.root, 1)

    def roots(self, dve):
        dve.wait_ge(self.squares, NT)
        dve.tensor_scalar(self.st[:, 8:8 + NT], self.st[:, 0:NT], 1.0 / D, EPS, ALU.mult, ALU.add).then_inc(self.var, 1)
        dve.wait_ge(self.root, 1)
        dve.reciprocal(self.st[:, 16:16 + NT], self.st[:, 8:8 + NT]).then_inc(self.inv, 1)
        dve.wait_ge(self.inv, 1)

    def vector(self, dve, rows_ready):
        rows_ready(dve)
        for t in range(NT):
            dve.scalar_tensor_tensor(self.h[:, t, :], self.x[:, t, :], self.st[:, 16 + t:17 + t],
                                     self.gain[:, int(t >= NTC), :], ALU.mult, ALU.mult).then_inc(self.scaled, 1)

    def gpsimd(self, pool):
        for t in range(NT):
            pool.wait_ge(self.scaled, t + 1)
            pool.tensor_tensor(self.h[:, t, :], self.h[:, t, :], self.shift[:, int(t >= NTC), :],
                               ALU.add).then_inc(self.shifted, 1)


def load_mod_rows(eng, g, dst, section, sem):
    for s in range(2):
        eng.dma_start(dst[:, s, :], g.mod_rows[s, section * D:(section + 1) * D].partition_broadcast(P)).then_inc(sem, 16)



FM_OF = {768: 0, 896: 1, 1024: 2, 1152: 3, 1536: 4, 1664: 5, 1792: 6, 1920: 7, 2048: 8, 2176: 9, 2304: 10}


def proj_jobs():
    jobs = []
    for c in range(11):
        base = c * 256
        if base < 768:
            jobs.append((c, "qkv", 0, 256, base))
        elif base == 1280:
            jobs.append((c, "vb", 0, 256, 0))
        else:
            for off in (0, 128):
                col = base + off
                if col in FM_OF:
                    jobs.append((c, "fm", off, 128, FM_OF[col]))
                elif col < N_IN:
                    jobs.append((c, "vn", off, 128, col - 2432))
    return jobs


PJ_RAW, PJ_HI, PJ_W = 2, 2, 256


def load_w_in(sync, g, j, layer, c):
    width = min(PJ_W, N_IN - c * PJ_W)
    sync.dma_start(j.w[:, c % PJ_RAW, :, 0:width],
                   at(g.w_in, layer).rearrange("(k p) n -> p k n", p=P)[:, :, c * PJ_W:c * PJ_W + width]
                   ).then_inc(j.w_loaded[c % PJ_RAW], 16)


def projection_buffers(g, a):
    j = Buffers()
    j.x, j.stats = a.sb("pj_x", [P, NT, D]), a.sb("pj_stats", [P, 24])
    j.w = a.sb("pj_w", [P, PJ_RAW, KD, PJ_W])
    j.x_loaded = [g.sem(f"pj_x_loaded{t}") for t in range(NT)]
    j.w_loaded = [g.sem(f"pj_w_loaded{s}") for s in range(PJ_RAW)]
    j.norm = PreNorm(g, "pj", j.x, j.x, None, None, g.vb[:, :, :].rearrange("p t n -> p (t n)")[:, 0:D], j.stats)
    return j


def projection(nc, g, j, layer):
    BANKS = 6
    NC = (N_IN + PJ_W - 1) // PJ_W
    jobs = proj_jobs()
    groups = [(job, t) for t in range(NT) for job in jobs[0:2]]
    for job in jobs[2:]:
        groups += [(job, i) for i in range(2 if job[1] == "fm" else NT)]
    last_group = {}
    for n, (job, _) in enumerate(groups):
        last_group[job[0]] = n
    with ExitStack() as stack:
        a = Scope(nc, stack)
        h, w, w_loaded, norm = j.x, j.w, j.w_loaded, j.norm
        hT_hi, hT_lo = (a.sb("pj_hT" + n, [P, KD, T], F32R) for n in ("_hi", "_lo"))
        w_hi, w_lo = (a.sb("pj_w" + n, [P, PJ_HI, KD, PJ_W], F32R) for n in ("_hi", "_lo"))
        gain, shift = a.sb("pj_gain", [P, 2, D]), a.sb("pj_shift", [P, 2, D])
        norm.gain, norm.shift = gain, shift
        tp = a.ps("pj_tp", [P, 2, 4, P])
        ps = a.ps("pj_ps", [P, BANKS, 512])
        rows_loaded = g.sem("pj_rows_loaded")
        turned = g.sem("pj_turned")
        hi_ready, lo_ready = g.sem("pj_hT_hi_ready"), g.sem("pj_hT_lo_ready")
        w_hi_ready, w_lo_ready = g.sem("pj_w_hi_ready"), g.sem("pj_w_lo_ready")
        group_done = g.sem("pj_group_done")
        out_s = g.sem("pj_copied_scalar")
        out_v = g.sem("pj_copied_vector")

        def dest(n):
            (c, kind, off, width, place), i = groups[n]
            src = ps[:, n % BANKS, 0:(T // 2 if kind == "fm" else width)]
            if kind == "fm":
                return g.fm[:, place, i * (T // 2):(i + 1) * (T // 2)], src
            buf = {"qkv": g.qkv, "vb": g.vb, "vn": g.vn}[kind]
            return buf[:, i, place:place + width], src

        def width_of(c):
            return min(PJ_W, N_IN - c * PJ_W)

        with nc.Block(no_gpsimd_drain=True) as block:

            @block.sync
            def _(sync):
                load_mod_rows(sync, g, gain, 1, rows_loaded)
                load_mod_rows(sync, g, shift, 0, rows_loaded)
                for c in range(PJ_RAW, NC):
                    sync.wait_ge(w_lo_ready, c - PJ_RAW + 1)
                    load_w_in(sync, g, j, layer, c)

            @block.scalar
            def _(act):
                def high(c):
                    act.wait_ge(w_loaded[c % PJ_RAW], 16 * (c // PJ_RAW + 1))
                    if c >= PJ_HI:
                        act.wait_ge(group_done, last_group[c - PJ_HI] + 1)
                    act.activation(w_hi[:, c % PJ_HI, :, 0:width_of(c)], w[:, c % PJ_RAW, :, 0:width_of(c)],
                                   ACT.Copy).then_inc(w_hi_ready, 1)

                def copies(first, last):
                    for n in range(first, last):
                        if n % 2 == 0:
                            act.wait_ge(group_done, n + 1)
                            act.activation(*dest(n), ACT.Copy).then_inc(out_s, 1)
                        for c in range(PJ_HI, NC):
                            if last_group[c - PJ_HI] == n:
                                high(c)

                high(0)
                high(1)
                for n in range(2 * NT):
                    act.wait_ge(turned, n + 1)
                    t, half = n // 2, n % 2
                    act.activation(hT_hi[:, 4 * half:4 * half + 4, t * P:(t + 1) * P], tp[:, half, :, :],
                                   ACT.Copy).then_inc(hi_ready, 1)
                    if half:
                        copies(2 * max(t - 1, 0), 2 * t)
                copies(2 * NT - 2, len(groups))

            @block.vector
            def _(dve):
                def low(c):
                    dve.wait_ge(w_hi_ready, c + 1)
                    lo, raw = w_lo[:, c % PJ_HI, :, 0:width_of(c)], w[:, c % PJ_RAW, :, 0:width_of(c)]
                    dve.tensor_tensor(lo, raw, w_hi[:, c % PJ_HI, :, 0:width_of(c)].bitcast(F32),
                                      ALU.subtract).then_inc(w_lo_ready, 1)

                def copies(first, last):
                    for n in range(first, last):
                        if n % 2 == 1:
                            dve.wait_ge(group_done, n + 1)
                            dve.tensor_copy(*dest(n)).then_inc(out_v, 1)
                        for c in range(PJ_HI, NC):
                            if last_group[c - PJ_HI] == n:
                                low(c)

                low(0)
                low(1)
                norm.vector(dve, lambda e: e.wait_ge(rows_loaded, 64))
                for n in range(2 * NT):
                    dve.wait_ge(hi_ready, n + 1)
                    t, half = n // 2, n % 2
                    blocks, cols = slice(4 * half, 4 * half + 4), slice(t * P, (t + 1) * P)
                    dve.tensor_tensor(hT_lo[:, blocks, cols], tp[:, half, :, :], hT_hi[:, blocks, cols].bitcast(F32),
                                      ALU.subtract).then_inc(lo_ready, 1)
                    if half:
                        copies(2 * max(t - 1, 0), 2 * t)
                copies(2 * NT - 2, len(groups))

            @block.gpsimd
            def _(pool):
                norm.gpsimd(pool)

            @block.tensor
            def _(pe):
                def turn(t):
                    pe.wait_ge(norm.shifted, t + 1)
                    for half in range(2):
                        if t:
                            pe.wait_ge(lo_ready, 2 * t - 1 + half)
                        for i in range(4):
                            k = 4 * half + i
                            mm = pe.transpose(tp[:, half, i, :], h[:, t, k * P:(k + 1) * P], g.ident)
                        mm.then_inc(turned, 1)

                def group(n):
                    (c, kind, off, width, place), i = groups[n]
                    pe.wait_ge(w_lo_ready, c + 1)
                    if n >= BANKS:
                        pe.wait_ge(out_s if n % 2 == 0 else out_v, (n - BANKS) // 2 + 1)
                    out = ps[:, n % BANKS, 0:(T // 2 if kind == "fm" else width)]
                    cols = slice(i * (T // 2), (i + 1) * (T // 2)) if kind == "fm" else slice(i * P, (i + 1) * P)
                    for k in range(KD):
                        whk = w_hi[:, c % PJ_HI, k, off:off + width]
                        wlk = w_lo[:, c % PJ_HI, k, off:off + width]
                        hhk, hlk = hT_hi[:, k, cols], hT_lo[:, k, cols]
                        for last, wk, hk in ((False, whk, hhk), (False, whk, hlk), (True, wlk, hhk)):
                            stationary, moving = (wk, hk) if kind == "fm" else (hk, wk)
                            mm = pe.matmul(out, stationary, moving, start=(wk is whk and hk is hhk and k == 0),
                                           stop=(last and k == KD - 1))
                    mm.then_inc(group_done, 1)

                turn(0)
                for t in range(NT):
                    if t + 1 < NT:
                        turn(t + 1)
                    pe.wait_ge(lo_ready, 2 * t + 2)
                    group(2 * t)
                    group(2 * t + 1)
                for n in range(2 * NT, len(groups)):
                    group(n)



N_ITEM = A_HEADS + C_HEADS
Q_BLOCKS = A_GROUP + 2


def attention_prepare(nc, g, a, b, layer):
    NH = A_HEADS + A_KV
    ss, tmp, tmp2 = a.sb("qk_ss", [P, 3, NT, NH]), a.sb("qk_tmp", [P, 2, NH, HD]), a.sb("qk_tmp2", [P, 2, NH, HD])
    rot = a.sb("qk_rot", [P, 2, NH, HD])
    ssf = ss[:, :, :, :].rearrange("p a t h -> p a (t h)")
    rope_loaded, bias_loaded = g.sem("rope_loaded"), g.sem("bias_loaded")
    squared, summed, var, root, inv = (g.sem(f"qk_{n}") for n in ("squared", "summed", "var", "root", "inv"))
    scaled, gained, cosed, sined, rotated = (g.sem(f"qk_{n}") for n in ("scaled", "gained", "cosed", "sined", "rotated"))
    turned, stored = g.sem("qk_turned"), g.sem("qk_stored")
    b.qk_ready, b.bias_ready = stored, bias_loaded

    def qk(t):
        return g.qkv[:, t, 0:NH * HD].rearrange("p (h d) -> p h d", h=NH)

    def parts(v):
        return v.rearrange("p h (r s e) -> p h r s e", r=2, s=2)

    def sync(sync):
        sync.dma_start(b.rope[:, :, :], g.rope_d).then_inc(rope_loaded, 16)
        sync.dma_start(b.rows[:, :], at(g.rows_d, layer)[R_GAIN:R_GAIN + NH * HD].partition_broadcast(P)).then_inc(rope_loaded, 16)
        sync.dma_start(b.bias[:, :, :].rearrange("p h n -> p (h n)"), at(g.bias_d, layer)).then_inc(bias_loaded, 16)

    def vector(dve):
        for t in range(NT):
            if t >= 2:
                dve.wait_ge(summed, t - 1)
            dve.tensor_tensor(tmp[:, t % 2, :, :], qk(t), qk(t), ALU.mult).then_inc(squared, 1)
            dve.wait_ge(squared, t + 1)
            dve.tensor_reduce(ss[:, 0, t, :], tmp[:, t % 2, :, :], AX_X, ALU.add).then_inc(summed, 1)
        dve.wait_ge(summed, NT)
        dve.tensor_scalar(ssf[:, 1, :], ssf[:, 0, :], 1.0 / HD, EPS, ALU.mult, ALU.add).then_inc(var, 1)
        dve.wait_ge(root, 1)
        dve.reciprocal(ssf[:, 0, :], ssf[:, 2, :]).then_inc(inv, 1)
        dve.wait_ge(inv, 1)
        for t in range(NT):
            dve.tensor_tensor(qk(t), qk(t), spread(ss[:, 0, t, :], 2, HD), ALU.mult).then_inc(scaled, 1)
            if t >= 1:
                finish(dve, t - 1)
        finish(dve, NT - 1)

    def finish(dve, t):
        i = t % 2
        dve.wait_ge(gained, t + 1)
        dve.wait_ge(rope_loaded, 32)
        dve.wait_ge(rotated, 2 * max(t - 1, 0))
        dve.tensor_tensor(tmp[:, i, :, :], qk(t), spread(b.rope[:, t, 0:HD], 1, NH), ALU.mult).then_inc(cosed, 1)
        dve.wait_ge(cosed, t + 1)
        dve.wait_ge(sined, 2 * t + 2)
        if t >= 2:
            dve.wait_ge(turned, t - 1)
        dve.tensor_tensor(rot[:, i, 0:A_HEADS, :].rearrange("p (g v) d -> p v g d", v=A_KV),
                          tmp[:, i, 0:A_HEADS, :].rearrange("p (v g) d -> p v g d", v=A_KV),
                          tmp2[:, i, 0:A_HEADS, :].rearrange("p (v g) d -> p v g d", v=A_KV), ALU.add).then_inc(rotated, 1)
        dve.tensor_tensor(rot[:, i, A_HEADS:NH, :], tmp[:, i, A_HEADS:NH, :], tmp2[:, i, A_HEADS:NH, :],
                          ALU.add).then_inc(rotated, 1)

    def gpsimd(pool):
        pool.wait_ge(rope_loaded, 32)
        for t in range(NT):
            i = t % 2
            pool.wait_ge(scaled, t + 1)
            pool.tensor_tensor(qk(t), qk(t), b.rows[:, :].rearrange("p (h d) -> p h d", h=NH), ALU.mult).then_inc(gained, 1)
            pool.wait_ge(gained, t + 1)
            if t >= 2:
                pool.wait_ge(rotated, 2 * t - 2)
            for s in range(2):
                pool.tensor_tensor(parts(tmp2[:, i, :, :])[:, :, :, s, :], parts(qk(t))[:, :, :, 1 - s, :],
                                   spread(b.rope[:, t, HD:2 * HD].rearrange("p (r s e) -> p r s e", r=2, s=2)[:, :, s, :],
                                          1, NH), ALU.mult).then_inc(sined, 1)

    def scalar(act):
        act.wait_ge(var, 1)
        act.activation(ssf[:, 2, :], ssf[:, 1, :], ACT.Sqrt).then_inc(root, 1)
        for t in range(NT):
            act.wait_ge(turned, t + 1)
            act.activation(b.qkT[:, :, t * P:(t + 1) * P], b.prep_ps[:, t % 2, :, :], ACT.Copy).then_inc(stored, 1)

    def tensor(pe):
        for t in range(NT):
            pe.wait_ge(rotated, 2 * t + 2)
            if t >= 2:
                pe.wait_ge(stored, t - 1)
            for j in range(5):
                mm = pe.transpose(b.prep_ps[:, t % 2, j, :],
                                  rot[:, t % 2, 2 * j:2 * j + 2, :].rearrange("p h d -> p (h d)"), g.ident)
            mm.then_inc(turned, 1)

    return sync, scalar, vector, gpsimd, tensor


def attend(nc, g, b, block, name, tiles, first, key_tiles, local_bias):
    TURN = 2
    items, groups = TURN * N_ITEM, TURN * N_ITEM // 4
    keys = key_tiles * P
    ka = (key_tiles + 1) // 2
    kb = key_tiles - ka
    staged, scored, maxed = g.sem(name + "_staged"), g.sem(name + "_scored"), g.sem(name + "_maxed")
    link_sem = g.sem(name + "_dve_chain")
    exped, turned = g.sem(name + "_exped"), g.sem(name + "_turned")
    copied_a, copied_b = g.sem(name + "_copied_scalar"), g.sem(name + "_copied_vector")
    inverted, valued, rows_kept, normed = (g.sem(f"{name}_{n}") for n in ("inverted", "valued", "rows_kept", "normed"))

    def is_local(m):
        return local_bias and m % N_ITEM >= A_HEADS

    def head(m):
        n = m % N_ITEM
        if n < A_HEADS:
            v = n // A_GROUP
            return n % A_GROUP, v * HD, None, lambda kt: g.qkv[:, kt, A_W + A_KVW + v * HD:A_W + A_KVW + (v + 1) * HD]
        h = n - A_HEADS
        return A_GROUP + h // 2, (h % 2) * HD, 9 + h // 2, lambda kt: g.vn[:, kt, h * HD:(h + 1) * HD]

    @block.tensor
    def _(pe):
        pe.sem_inc(normed, 4)
        with pe.Fori(0, tiles // TURN) as i:
            def scores(m):
                q, part, kblk, _ = head(m)
                src = b.qkT[part:part + HD, A_GROUP, :] if kblk is None else g.fm[part:part + HD, kblk, :]
                for c in range(0, keys, 512):
                    w = min(512, keys - c)
                    mm = pe.matmul(b.sc_ps[:, m % 2, c:c + w], b.q_now[part:part + HD, m // N_ITEM, q, :], src[:, c:c + w],
                                   start=True, stop=True)
                mm.then_inc(scored, 1)

            def turns(m):
                pe.wait_ge(exped, i * items + m + 1)
                for kt in range(key_tiles):
                    if kt == 0 and m > 0:
                        pe.wait_ge(copied_a, i * items + m)
                    if kt == ka and m > 0:
                        pe.wait_ge(copied_b, i * items + m)
                    half, j = (0, kt) if kt < ka else (1, kt - ka)
                    mm = pe.transpose(b.pt_ps[:, half, j, :], b.e[:, m % 2, kt * P:(kt + 1) * P], g.ident)
                    if kt in (ka - 1, key_tiles - 1):
                        mm.then_inc(turned, 1)

            def values(m):
                pe.wait_ge(copied_a, i * items + m + 1)
                pe.wait_ge(copied_b, i * items + m + 1)
                if m % 4 == 0:
                    pe.wait_ge(normed, (i * groups + m // 4) * 2 + 2)
                for kt in range(key_tiles):
                    pe.matmul(b.o_ps[0:HD, m // 4 % 2, m % 4, :], head(m)[3](kt), b.pT[:, m % 2, kt, :],
                              start=(kt == 0), stop=(kt == key_tiles - 1))
                pe.wait_ge(inverted, i * items + m + 1)
                mm = pe.matmul(b.o_ps[HD:P, m // 4 % 2, m % 4, :], b.inv[:, m:m + 1].to_broadcast([P, HD]), g.ident,
                               start=True, stop=True)
                if m % 4 == 3:
                    mm.then_inc(valued, 1)

            pe.wait_ge(staged, i * 2 * TURN + 2)
            scores(0)
            scores(1)
            for m in range(items):
                turns(m)
                if m >= 1:
                    values(m - 1)
                if m + 2 == N_ITEM:
                    pe.wait_ge(staged, i * 2 * TURN + 4)
                if m + 2 < items:
                    scores(m + 2)
            values(items - 1)

    @block.scalar
    def _(act):
        act.wait_ge(b.qk_ready, NT)
        with act.Fori(0, tiles // TURN) as i:
            def exp(m):
                act.wait_ge(maxed, i * items + m + 1)
                src, scale = (b.s[:, m % 2, 0:keys], 1.0) if is_local(m) else (b.sc_ps[:, m % 2, 0:keys], SCALE)
                act.activation(b.e[:, m % 2, 0:keys], src, ACT.Exp, bias=b.negmax[:, m:m + 1], scale=scale,
                               accum_out=b.total[:, m:m + 1]).then_inc(exped, 1)

            def keep_rows(k):
                act.wait_ge(valued, i * groups + k + 1)
                act.activation(b.inv_rows[:, k % 2, :, :], b.o_ps[HD:P, k % 2, :, :], ACT.Copy).then_inc(rows_kept, 1)

            def stage(u):
                col = (i * TURN + first + u) * P
                act.activation(b.q_now[:, u, 0:A_GROUP, :], b.qkT[:, 0:A_GROUP, ds(col, P)], ACT.Copy).then_inc(staged, 1)
                act.activation(b.q_now[:, u, A_GROUP:, :], g.fm[:, 7:9, ds(col, P)], ACT.Copy).then_inc(staged, 1)

            stage(0)
            exp(0)
            stage(1)
            for m in range(items):
                act.wait_ge(turned, i * 2 * items + 2 * m + 1)
                act.activation(b.pT[:, m % 2, 0:ka, :], b.pt_ps[:, 0, 0:ka, :], ACT.Copy).then_inc(copied_a, 1)
                if m + 1 < items:
                    exp(m + 1)
                if m >= 4 and m % 4 == 0:
                    keep_rows(m // 4 - 1)
            keep_rows(groups - 1)

    @block.vector
    def _(dve):
        n_local = TURN * C_HEADS if local_bias else 0
        per = (items - n_local) + 3 * n_local
        if local_bias:
            dve.wait_ge(b.bias_ready, 16)
        with dve.Fori(0, tiles // TURN) as i:
            link = Link(dve, link_sem, i * per)

            def maximum(m):
                dve.wait_ge(scored, i * items + m + 1)
                if not is_local(m):
                    link(dve.tensor_reduce(b.mx[:, m:m + 1], b.sc_ps[:, m % 2, 0:keys], AX_X, ALU.max))
                    scale = -SCALE
                else:
                    tile = i * TURN + m // N_ITEM
                    dve.scalar_tensor_tensor(b.s[:, m % 2, CTX:keys], b.sc_ps[:, m % 2, CTX:keys], SCALE,
                                             b.bias[:, m % N_ITEM - A_HEADS,
                                                    ds((RPB_M - WIN_ROWS) * GRID - tile * 2 * GRID, WIN_ROWS * GRID)],
                                             ALU.mult, ALU.add).then_inc(link_sem, 1)
                    link.n += 1
                    link(dve.tensor_scalar(b.s[:, m % 2, 0:CTX], b.sc_ps[:, m % 2, 0:CTX], SCALE, None, ALU.mult))
                    link(dve.tensor_reduce(b.mx[:, m:m + 1], b.s[:, m % 2, 0:keys], AX_X, ALU.max))
                    scale = -1.0
                dve.tensor_scalar(b.negmax[:, m:m + 1], b.mx[:, m:m + 1], scale, None, ALU.mult).then_inc(maxed, 1)

            def normalise(k):
                tile, blk = i * TURN + first + k * 4 // N_ITEM, (0, 2, 6)[k % (N_ITEM // 4)]
                dve.wait_ge(rows_kept, i * groups + k + 1)
                for par in range(2):
                    dve.tensor_tensor(g.mixT[par * HD:par * HD + HD, blk:blk + 2, ds(tile * P, P)],
                                      b.o_ps[0:HD, k % 2, par:4:2, :], b.inv_rows[:, k % 2, par:4:2, :],
                                      ALU.mult).then_inc(normed, 1)

            maximum(0)
            for m in range(items):
                if m + 1 < items:
                    maximum(m + 1)
                dve.wait_ge(turned, i * 2 * items + 2 * m + 2)
                dve.tensor_copy(b.pT[:, m % 2, ka:key_tiles, :], b.pt_ps[:, 1, 0:kb, :]).then_inc(copied_b, 1)
                dve.reciprocal(b.inv[:, m:m + 1], b.total[:, m:m + 1]).then_inc(inverted, 1)
                if m >= 5 and m % 4 == 1:
                    normalise(m // 4 - 1)
            normalise(groups - 1)
            assert link.n == per, (link.n, per)


class Buffers:
    pass


def attention(nc, g, layer):
    with ExitStack() as stack:
        a, b = Scope(nc, stack), Buffers()
        b.rope = a.sb("at_rope", [P, NT, 2 * HD])
        b.rows = a.sb("at_gain", [P, (A_HEADS + A_KV) * HD])
        b.bias = a.sb("at_bias", [P, C_HEADS, RPB_M * GRID])
        b.qkT = a.sb("at_qkT", [P, A_GROUP + 1, T])
        with ExitStack() as first:
            f = Scope(nc, first)
            b.prep_ps = f.ps("at_prep_ps", [P, 2, 8, P])[:, :, 0:5, :]
            sync, scalar, vector, gpsimd, tensor = attention_prepare(nc, g, f, b, layer)
            with nc.Block(no_gpsimd_drain=True) as block:
                block.sync(sync)
                block.scalar(scalar)
                block.vector(vector)
                block.gpsimd(gpsimd)
                block.tensor(tensor)
        b.q_now = a.sb("at_q_now", [P, 2, Q_BLOCKS, P])
        b.e = a.sb("at_e", [P, 2, T])
        b.s = a.sb("at_s", [P, 2, T])
        b.pT = a.sb("at_pT", [P, 2, NT, P])
        b.mx, b.negmax = (a.sb("at_" + n, [P, 2 * N_ITEM]) for n in ("mx", "negmax"))
        b.total, b.inv = (a.sb("at_" + n, [P, 2 * N_ITEM]) for n in ("total", "inv"))
        b.inv_rows = a.sb("at_inv_rows", [HD, 2, 4, P])
        b.sc_ps = a.ps("at_sc_ps", [P, 2, 1024])
        b.pt_ps = a.ps("at_pt_ps", [P, 2, 4, P])
        b.o_ps = a.ps("at_o_ps", [P, 2, 4, P])
        with nc.Block(no_gpsimd_drain=True) as block:
            attend(nc, g, b, block, "lat", NT - NTC, NTC, NT, True)
        with nc.Block(no_gpsimd_drain=True) as block:
            attend(nc, g, b, block, "ctx", NTC, 0, NTC, False)



HALF = T // 2


def rwkv_gates(nc, g, r, layer):
    fm = g.fm
    rT, kT, wl, al, gl = fm[:, 0:2, :], fm[:, 2:4, :], fm[:, 4, :], fm[:, 5, :], fm[:, 6, :]
    with ExitStack() as stack:
        a = Scope(nc, stack)
        tmp, tmp2 = a.sb("rg_tmp", [P, 2, T]), a.sb("rg_tmp2", [P, 2, T])
        restart = a.sb("rg_restart", [P, T])
        cols, wu, au = a.sb("rg_cols", [P, N_COL]), a.sb("rg_wu", [P, B_W]), a.sb("rg_au", [P, B_W])
        z = a.ps("rg_z", [P, 4, 512])
        ns = a.ps("rg_ns", [P, 2, 2, 512])
        bon = z[:, 0, 0:NT * B_HEADS].rearrange("p (t h) -> p t h", h=B_HEADS)
        loaded, acted, looked, gated = g.sem("rg_loaded"), g.sem("rg_acted"), g.sem("rg_looked"), g.sem("rg_gated")
        squared, summed, rooted, chain = g.sem("rg_squared"), g.sem("rg_summed"), g.sem("rg_rooted"), g.sem("rg_chain")
        bonus_in, bonus_out = g.sem("rg_bonus_in"), g.sem("rg_bonus_out")
        with nc.Block(no_gpsimd_drain=True) as block:

            @block.sync
            def _(sync):
                sync.dma_start(cols[:, :], at(g.cols_d, layer)).then_inc(loaded, 16)
                sync.dma_start(wu[:, :], at(g.w_up, layer)).then_inc(loaded, 16)
                sync.dma_start(au[:, :], at(g.a_up, layer)).then_inc(loaded, 16)

            @block.scalar
            def _(act):
                act.activation(wl, wl, ACT.Tanh).then_inc(acted, 1)
                act.activation(gl, gl, ACT.Sigmoid).then_inc(acted, 1)
                act.wait_ge(loaded, 48)
                for n in range(16):
                    d, blk, half = (n % 8) // 4, (n % 4) // 2, n % 2
                    dst, col = (r.xc, C_W0) if n < 8 else (r.b, C_A0)
                    act.wait_ge(looked, n + 1)
                    act.activation(dst[:, 2 * d + blk, half * HALF:(half + 1) * HALF], z[:, n % 4, 0:HALF], ACT.Sigmoid,
                                   bias=cols[:, col + 2 * d + blk:col + 2 * d + blk + 1]).then_inc(gated, 1)
                act.wait_ge(summed, 1)
                act.activation(tmp2[:, :, :].rearrange("p b (h n) -> p b h n", h=2), ns[:, :, :, 0:HALF],
                               ACT.Sqrt).then_inc(rooted, 1)

            @block.tensor
            def _(pe):
                pe.wait_ge(loaded, 48)
                pe.wait_ge(acted, 1)
                for n in range(16):
                    d, blk, half = (n % 8) // 4, (n % 4) // 2, n % 2
                    wt, src = (wu, wl) if n < 8 else (au, al)
                    if n >= 4:
                        pe.wait_ge(gated, n - 3)
                    pe.matmul(z[:, n % 4, 0:HALF], wt[d * 64:d * 64 + 64, blk * P:(blk + 1) * P],
                              src[d * 64:d * 64 + 64, half * HALF:(half + 1) * HALF], start=True, stop=True).then_inc(looked, 1)
                pe.wait_ge(squared, 1)
                for blk in range(2):
                    for half in range(2):
                        mm = pe.matmul(ns[:, blk, half, 0:HALF], g.cst[:, O_HB:O_HB + P],
                                       tmp[:, blk, half * HALF:(half + 1) * HALF], start=True, stop=True)
                mm.then_inc(summed, 1)
                pe.wait_ge(bonus_in, 2)
                for t in range(NT):
                    for blk in range(2):
                        mm = pe.matmul(bon[:, t, 2 * blk:2 * blk + 2], tmp[:, blk, t * P:(t + 1) * P],
                                       g.cst[:, O_HS:O_HS + 2], start=True, stop=True)
                mm.then_inc(bonus_out, 1)

            @block.vector
            def _(dve):
                link = Link(dve, chain)
                dve.wait_ge(loaded, 48)
                for blk in range(2):
                    link(dve.tensor_scalar(r.nkk[:, blk, :], kT[:, blk, :], cols[:, C_KK + blk:C_KK + blk + 1], None, ALU.mult))
                dve.tensor_tensor(tmp[:, :, :], r.nkk[:, :, :], r.nkk[:, :, :], ALU.mult).then_inc(squared, 1)
                link(dve.memset(restart[:, :], 1.0))
                link(dve.memset(restart[:, 0:T:CH], 0.0))
                dve.wait_ge(gated, 8)
                for db in range(4):
                    way = slice(None) if db < 2 else slice(None, None, -1)
                    link(dve.tensor_tensor_scan(r.cs[:, db, way], restart[:, :], r.xc[:, db, way], 0.0, ALU.mult, ALU.add))
                link(dve.tensor_tensor(r.xc[:, :, :], r.cs[:, :, :], r.xc[:, :, :], ALU.subtract))
                dve.wait_ge(rooted, 1)
                link(dve.tensor_scalar(tmp2[:, :, :], tmp2[:, :, :], 1e-12, None, ALU.max))
                link(dve.reciprocal(tmp2[:, :, :], tmp2[:, :, :]))
                link(dve.scalar_tensor_tensor(r.nkk[:, :, :], r.nkk[:, :, :], -1.0, tmp2[:, :, :], ALU.mult, ALU.mult))
                dve.wait_ge(gated, 16)
                for db in range(4):
                    blk = db % 2
                    link(dve.tensor_scalar(r.kd[:, db, :], r.b[:, db, :], 1.0, cols[:, C_KA + blk:C_KA + blk + 1],
                                           ALU.subtract, ALU.mult))
                for d in range(2):
                    link(dve.scalar_tensor_tensor(r.kd[:, 2 * d:2 * d + 2, :], r.kd[:, 2 * d:2 * d + 2, :], 1.0, kT,
                                                  ALU.add, ALU.mult))
                for d in range(2):
                    link(dve.scalar_tensor_tensor(r.b[:, 2 * d:2 * d + 2, :], r.b[:, 2 * d:2 * d + 2, :], -1.0, r.nkk[:, :, :],
                                                  ALU.mult, ALU.mult))
                link(dve.tensor_tensor(tmp[:, :, :], r.kd[:, 0:2, :], r.kd[:, 2:4, :], ALU.add))
                for blk in range(2):
                    dve.scalar_tensor_tensor(tmp[:, blk, :], tmp[:, blk, :], cols[:, C_RK + blk:C_RK + blk + 1],
                                             rT[:, blk, :], ALU.mult, ALU.mult).then_inc(bonus_in, 1)
                dve.wait_ge(bonus_out, 1)
                dve.tensor_copy(r.bonus[:, :, :], bon)


def rwkv_chunks(nc, g, r, layer):
    with ExitStack() as stack:
        a = Scope(nc, stack)
        e = a.sb("rc_e", [P, 3, 4, P])
        bh, kh = e[:, 0, :, :], e[:, 1, :, :]
        dg = e[:, 2, :, :].rearrange("p db (c n) -> p (db c) n", c=2)
        wend = a.sb("rc_wend", [P, 8])
        ar = a.sb("rc_ar", [P, 2, 4, P])
        bt, kt = a.sb("rc_bt", [P, 4, P]), a.sb("rc_kt", [P, 4, P])
        vt = a.sb("rc_vt", [P, B_W])
        ag = a.sb("rc_ag", [P, 8, 2, CH])
        bht, kht = a.sb("rc_bht", [P, 8, CH]), a.sb("rc_kht", [P, 8, CH])
        lb, lk = a.sb("rc_lb", [P, 8, 2 * CH]), a.sb("rc_lk", [P, 8, 2 * CH])
        nl = a.sb("rc_nl", [P, 5, 8, CH])
        tu = a.sb("rc_tu", [P, 2, 2, 4, CH])
        y = a.sb("rc_y", [P, 8, CH])
        tag = a.sb("rc_tag", [P, 8, 2 * CH])
        mk = a.sb("rc_mk", [P, 2, 2 * CH])
        m0 = a.sb("rc_m0", [P, 2, CH])
        ps = a.ps("rc_ps", [P, 8, 512])
        names = ("masks", "decays", "tildes", "hats", "v_staged", "products", "turned", "turned_kept", "masked",
                 "levels", "y_made", "y_kept", "step_made", "inverse", "g0_made", "g0_kept", "tag_made",
                 "tag_kept_v", "tag_kept_s", "results", "kept_v", "kept_s", "passed")
        s = Buffers()
        (s.masks, s.decays, s.tildes, s.hats, s.v_staged, s.products, s.turned, s.turned_kept, s.masked,
         s.levels, s.y_made, s.y_kept, s.step_made, s.inverse, s.g0_made, s.g0_kept, s.tag_made,
         s.tag_kept_v, s.tag_kept_s, s.results, s.kept_v, s.kept_s, s.passed) = (g.sem("rc_" + n) for n in names)
        lm = [g.cst[:, O_LM + 64 * lv:O_LM + 64 * lv + 64] for lv in range(6)]
        tri = [g.cst[:, O_TRI + 64 * i:O_TRI + 64 * i + 64] for i in range(4)]
        i64 = g.cst[:, O_I64:O_I64 + CH]
        units = [(par, db, ck) for par in range(2) for db in range(4) for ck in range(2)]
        half = [slice(0, 64), slice(64, 128)]

        def value(par, db):
            h = (db % 2) * 2 + par
            return slice(h * HD, h * HD + HD)

        def by_ck(v, col):
            return v[:, :, ds(col, P)].rearrange("p b (c n) -> p b c n", c=2)

        def from_ck(bank, c):
            return ps[:, bank:bank + 2, c:c + 256].rearrange("p c (b n) -> p b c n", b=4)

        def by_db(v, groups=4):
            return v.rearrange("p (b n) -> p b n", b=groups)

        with nc.Block(no_gpsimd_drain=True) as block:

            @block.scalar
            def _(act):
                with act.Fori(0, NT) as i:
                    col = i * P
                    act.wait_ge(s.results, i * 4)
                    act.wait_ge(s.kept_v, i * 2)
                    for n, (src, scale) in enumerate(((r.cs, KAPPA), (r.xc, KAPPA), (r.cs, -KAPPA))):
                        act.activation(e[:, n, :, :], src[:, :, ds(col, P)], ACT.Exp, scale=scale).then_inc(s.decays, 1)
                    for n, (dst, bank) in enumerate(((ag[:, :, 0, :], 6), (bht[:, :, :], 7), (kht[:, :, :], 6))):
                        act.wait_ge(s.turned, i * 3 + n + 1)
                        act.activation(dst, by_db(ps[:, bank, :], 8), ACT.Copy).then_inc(s.turned_kept, 1)
                    act.wait_ge(s.g0_made, i + 1)
                    act.activation(ag[:, :, 1, :], ps[:, 7, :].rearrange("p (u n) -> p u n", u=8), ACT.Copy).then_inc(s.g0_kept, 1)
                    for lv in range(5):
                        for d in range(2):
                            act.wait_ge(s.y_made, i * 10 + lv * 2 + d + 1)
                            act.activation(y[:, d:8:2, :], by_db(ps[:, 4 + d, 0:256]),
                                           ACT.Copy).then_inc(s.y_kept, 1)
                    act.wait_ge(s.tag_made, i * 2 + 2)
                    act.activation(tag[:, 1:8:2, :], by_db(ps[:, 3, :]), ACT.Copy).then_inc(s.tag_kept_s, 1)
                    act.wait_ge(s.results, i * 4 + 3)
                    act.activation(r.yl[:, ds(i, 1), :].squeeze(1), ps[:, 2, 0:256], ACT.Copy).then_inc(s.kept_s, 1)
                    act.wait_ge(s.results, i * 4 + 4)
                    act.activation(by_ck(r.hh, col), from_ck(5, 0), ACT.Copy).then_inc(s.kept_s, 1)

            @block.vector
            def _(dve):
                for d in range(2):
                    strict, incl, other = (TRI_LT, TRI_LE, TRI_GT) if d == 0 else (TRI_GT, TRI_GE, TRI_LT)
                    dve.tensor_copy(mk[:, d, 0:CH], tri[strict]).then_inc(s.masks, 1)
                    dve.tensor_copy(mk[:, d, CH:], tri[incl]).then_inc(s.masks, 1)
                    dve.tensor_tensor(m0[:, d, :], tri[other], lm[0], ALU.mult).then_inc(s.masks, 1)
                dve.wait_ge(s.masks, 6)
                with dve.Fori(0, NT) as i:
                    col = i * P
                    dve.wait_ge(s.decays, i * 3 + 3)
                    dve.tensor_copy(wend[:, 0:4].rearrange("p (b c) -> p b c", b=2), e[:, 0, 0:2, CH - 1:P:CH]).then_inc(s.tildes, 1)
                    dve.tensor_copy(wend[:, 4:8].rearrange("p (b c) -> p b c", b=2), e[:, 0, 2:4, 0:P:CH]).then_inc(s.tildes, 1)
                    for d in range(2):
                        for n, (decay, src) in enumerate(((1, r.nkk), (0, g.fm[:, 0:2, :]))):
                            dve.tensor_tensor(ar[:, n, 2 * d:2 * d + 2, :], e[:, decay, 2 * d:2 * d + 2, :],
                                              src[:, :, ds(col, P)], ALU.mult).then_inc(s.tildes, 1)
                    dve.tensor_tensor(bt[:, :, :], e[:, 2, :, :], r.b[:, :, ds(col, P)], ALU.mult).then_inc(s.tildes, 1)
                    dve.tensor_tensor(kt[:, :, :], e[:, 2, :, :], r.kd[:, :, ds(col, P)], ALU.mult).then_inc(s.tildes, 1)
                    for par in range(2):
                        dve.wait_ge(s.products, i * 2 + par + 1)

                        def by_d(v):
                            return v.rearrange("p (d b) n -> p d b n", d=2)

                        for dst, bank in ((lb, par), (lk, 2 + par)):
                            dve.tensor_tensor(by_d(dst[:, par:8:2, :]), by_d(by_db(ps[:, bank, :])),
                                              spread(mk[:, :, :], 2, 2), ALU.mult).then_inc(s.masked, 1)
                        dve.tensor_tensor(by_d(tu[:, par, 0, :, :]), by_d(by_db(ps[:, 4 + par, 0:256])),
                                          spread(m0[:, :, :], 2, 2), ALU.mult).then_inc(s.masked, 1)
                        dve.wait_ge(s.masked, i * 8 + par * 4 + 3)
                        dve.tensor_tensor(tu[:, par, 1, :, :], lb[:, par:8:2, 0:CH], spread(lm[0], 1, 4), ALU.mult).then_inc(s.masked, 1)
                        dve.wait_ge(s.masked, i * 8 + par * 4 + 4)
                        tud = tu[:, par, :, :, :].rearrange("p a h n -> p (a h) n")
                        dve.tensor_tensor(tud, tud, spread(i64, 1, 8), ALU.add).then_inc(s.inverse, 1)
                    for lv in range(5):
                        for d in range(2):
                            n = lv * 2 + d
                            dve.wait_ge(s.step_made, i * 10 + n + 1)
                            dve.wait_ge(s.inverse, i * 12 + n + 1)
                            if lv < 4:
                                dst, src = tu[:, d, :, :, :].rearrange("p a h n -> p (a h n)"), ps[:, d, :]
                            else:
                                dst, src = tu[:, d, 1, :, :].rearrange("p h n -> p (h n)"), ps[:, d, 256:512]
                            dve.tensor_tensor(dst, dst, src, ALU.add).then_inc(s.inverse, 1)
                    dve.wait_ge(s.tag_made, i * 2 + 1)
                    dve.tensor_copy(tag[:, 0:8:2, :], by_db(ps[:, 2, :])).then_inc(s.tag_kept_v, 1)
                    dve.wait_ge(s.results, i * 4 + 2)
                    dve.tensor_tensor(by_ck(r.pt, col), from_ck(0, 0), ar[:, 1, :, :].rearrange("p b (c n) -> p b c n", c=2),
                                      ALU.add).then_inc(s.kept_v, 1)
                    dve.wait_ge(s.hats, i * 3 + 3)
                    dve.tensor_tensor(by_ck(r.mt, col), from_ck(0, 256), e[:, 2, :, :].rearrange("p b (c n) -> p b c n", c=2),
                                      ALU.add).then_inc(s.kept_v, 1)

            @block.gpsimd
            def _(pool):
                with pool.Fori(0, NT) as i:
                    pool.wait_ge(s.results, i * 4)
                    pool.tensor_copy(vt[:, :], g.vb[:, ds(i, 1), :].squeeze(1)).then_inc(s.v_staged, 1)
                    pool.wait_ge(s.tildes, i * 8 + 8)
                    w8 = spread(wend[:, :], 2, CH)
                    for dst, src in ((bh, bt), (kh, kt)):
                        pool.tensor_tensor(dst.rearrange("p b (c n) -> p (b c) n", c=2),
                                           src[:, :, :].rearrange("p b (c n) -> p (b c) n", c=2), w8, ALU.mult).then_inc(s.hats, 1)
                    pool.tensor_tensor(dg, spread(i64, 1, 8), w8, ALU.mult).then_inc(s.hats, 1)
                    for d in range(2):
                        pool.wait_ge(s.masked, i * 8 + d * 4 + 1)
                        for lv in range(5):
                            pool.tensor_tensor(nl[:, lv, d:8:2, :], lb[:, d:8:2, 0:CH],
                                               spread(lm[lv + 1], 1, 4), ALU.mult).then_inc(s.levels, 1)

            @block.tensor
            def _(pe):
                def pe_wait(sem, value):
                    pe.wait_ge(sem, value)
                    pe.sem_inc(s.passed, 1)

                with pe.Fori(0, NT) as i:
                    pe_wait(s.tildes, i * 8 + 8)
                    pe_wait(s.kept_v, i * 2)
                    pe_wait(s.kept_s, i * 2)
                    pe_wait(s.tag_kept_s, i)
                    for par in range(2):
                        ch = half[par]
                        for db in range(4):
                            for ck in range(2):
                                st, steps = half[ck], slice(ck * CH, ck * CH + CH)
                                for bank, lhs in ((par, bt), (2 + par, kt)):
                                    pe.matmul(ps[st, bank, db * 128:db * 128 + 128].rearrange("p (a n) -> p a n", a=2),
                                              lhs[ch, db, steps], ar[ch, :, db, steps], start=True, stop=True)
                                mm = pe.matmul(ps[st, 4 + par, db * CH:db * CH + CH], ar[ch, 0, db, steps], bt[ch, db, steps],
                                               start=True, stop=True)
                        mm.then_inc(s.products, 1)
                    for n, (src, bank) in enumerate(((ar[:, 0, :, :], 6), (bh, 7), (kh, 6))):
                        if n:
                            pe_wait(s.hats, i * 3 + n)
                        if n == 2:
                            pe_wait(s.turned_kept, i * 3 + 1)
                        for db in range(4):
                            mm = pe.transpose(ps[:, bank, db * P:db * P + P], src[:, db, :], g.ident)
                        mm.then_inc(s.turned, 1)
                    pe_wait(s.turned_kept, i * 3 + 3)
                    pe_wait(s.masked, i * 8 + 7)
                    pe_wait(s.v_staged, i + 1)
                    for par, db, ck in units:
                        st, u = half[ck], 2 * db + par
                        mm = pe.matmul(ps[st, 7, u * CH:u * CH + CH], lk[st, u, 0:CH], vt[st, value(par, db)], start=True, stop=True)
                    mm.then_inc(s.g0_made, 1)
                    for lv in range(5):
                        for par in range(2):
                            pe_wait(s.levels, i * 10 + par * 5 + lv + 1)
                            pe_wait(s.inverse, i * 12 + lv * 2 + par + 1)
                            for db in range(4):
                                for st in half:
                                    mm = pe.matmul(ps[st, 4 + par, db * CH:db * CH + CH], nl[st, lv, 2 * db + par, :],
                                                   tu[st, par, 0, db, :], start=True, stop=True)
                            mm.then_inc(s.y_made, 1)
                        for par in range(2):
                            pe_wait(s.y_kept, i * 10 + lv * 2 + par + 1)
                            for db in range(4):
                                for st in half:
                                    t_, y_, c = tu[st, par, 1, db, :], y[st, 2 * db + par, :], db * CH
                                    if lv < 4:
                                        pe.matmul(ps[st, par, c:c + CH], t_, y_, start=True, stop=True)
                                    mm = pe.matmul(ps[st, par, 256 + c:256 + c + CH], y_, t_, start=True, stop=True)
                            mm.then_inc(s.step_made, 1)
                    pe_wait(s.g0_kept, i + 1)
                    for par in range(2):
                        pe_wait(s.inverse, i * 12 + 11 + par)
                        for db in range(4):
                            for st in half:
                                mm = pe.matmul(ps[st, 2 + par, db * 128:db * 128 + 128], tu[st, par, 1, db, :],
                                               ag[st, 2 * db + par, :, :].rearrange("p a n -> p (a n)"), start=True, stop=True)
                        mm.then_inc(s.tag_made, 1)
                    pe_wait(s.tag_kept_v, i + 1)
                    pe_wait(s.tag_kept_s, i + 1)
                    for base, rhs in ((0, lambda st, u: lb[st, u, CH:]), (256, lambda st, u: bht[st, u, :])):
                        for par, db, ck in units:
                            u, st, ch, c = 2 * db + par, half[ck], half[par], base + db * CH
                            mm = pe.matmul(ps[ch, ck, c:c + CH], tag[st, u, 0:CH], rhs(st, u), start=True, stop=True)
                        mm.then_inc(s.results, 1)
                    for h in range(4):
                        for st in half:
                            for d in range(2):
                                u, o = d * 4 + h, ps[st, 2, h * HD:h * HD + HD]
                                pe.matmul(o, lb[st, u, CH:], tag[st, u, CH:], start=(d == 0), stop=False)
                                mm = pe.matmul(o, lk[st, u, CH:], vt[st, h * HD:h * HD + HD], start=False, stop=(d == 1))
                    mm.then_inc(s.results, 1)
                    for par, db, ck in units:
                        u, st, ch = 2 * db + par, half[ck], half[par]
                        o = ps[ch, 5 + ck, db * CH:db * CH + CH]
                        pe.matmul(o, bht[st, u, :], tag[st, u, CH:], start=True, stop=False)
                        mm = pe.matmul(o, kht[st, u, :], vt[st, value(par, db)], start=False, stop=True)
                    mm.then_inc(s.results, 1)


def rwkv_readout(nc, g, r, layer):
    order = [list(range(NCH)), list(range(NCC - 1, -1, -1)) + list(range(NCH - 1, NCC - 1, -1))]
    with ExitStack() as stack:
        a = Scope(nc, stack)
        xs = a.sb("ro_xs", [P, 4, NCH, CH])
        gate = a.sb("ro_gate", [P, NT, B_W])
        gup, ln = a.sb("ro_gup", [P, B_W]), a.sb("ro_ln", [P, 2, B_W])
        tmp = a.sb("ro_tmp", [P, NT * B_HEADS, HD])
        st = a.sb("ro_st", [P, 4, NT * B_HEADS])
        sps = a.ps("ro_sps", [P, 2, B_W])
        yps = a.ps("ro_yps", [P, 2, 2, 512])
        gps = a.ps("ro_gps", [P, 2, 512])
        tps = gps
        loaded, zeroed, moved, stepped = g.sem("ro_loaded"), g.sem("ro_zeroed"), g.sem("ro_moved"), g.sem("ro_stepped")
        read, added, gated, gate_kept = g.sem("ro_read"), g.sem("ro_added"), g.sem("ro_gated"), g.sem("ro_gate_kept")
        chain, var, root, done = g.sem("ro_chain"), g.sem("ro_var"), g.sem("ro_root"), g.sem("ro_done")
        vbon, turned, kept = g.sem("ro_vbonus"), g.sem("ro_turned"), g.sem("ro_kept")
        yh = r.yl[:, :, :].rearrange("p t (h n) -> p (t h) n", h=B_HEADS)
        yf = r.yl[:, :, :]
        with nc.Block(no_gpsimd_drain=True) as block:

            @block.sync
            def _(sync):
                sync.dma_start(gup[:, :], at(g.g_up, layer)).then_inc(loaded, 16)
                sync.dma_start(ln[:, :, :].rearrange("p a n -> p (a n)"),
                               at(g.rows_d, layer)[R_LNW:R_LNW + 2 * B_W].partition_broadcast(P)).then_inc(loaded, 16)

            @block.tensor
            def _(pe):
                pe.wait_ge(zeroed, 2)
                for n in range(NCH - 1):
                    if n:
                        pe.wait_ge(stepped, 2 * n)
                    for d in range(2):
                        c = order[d][n]
                        for blk in range(2):
                            for par in (0, 64):
                                ch, db = slice(par, par + 64), 2 * d + blk
                                mm = pe.matmul(sps[ch, n % 2, db * CH:db * CH + CH], r.mt[ch, db, c * CH:c * CH + CH],
                                               xs[ch, db, c, :], start=True, stop=True)
                    mm.then_inc(moved, 1)
                    if n < NT:
                        if n == 0:
                            pe.wait_ge(loaded, 32)
                        if n >= 2:
                            pe.wait_ge(gate_kept, n - 1)
                        pe.matmul(gps[:, n % 2, 0:B_W], g.fm[:, 6, n * P:(n + 1) * P], gup[:, :], start=True, stop=True).then_inc(gated, 1)
                pe.wait_ge(stepped, 2 * (NCH - 1))
                for t in range(NT):
                    if t >= 2:
                        pe.wait_ge(added, t - 1)
                    for h in range(B_HEADS):
                        for ck in range(2):
                            for d in range(2):
                                ch, db, c = slice((h % 2) * 64, (h % 2) * 64 + 64), 2 * d + h // 2, 2 * t + ck
                                mm = pe.matmul(yps[ck * 64:ck * 64 + 64, t % 2, h % 2, (h // 2) * HD:(h // 2) * HD + HD],
                                               r.pt[ch, db, c * CH:c * CH + CH], xs[ch, db, c, :], start=(d == 0), stop=(d == 1))
                    mm.then_inc(read, 1)
                for t in range(NT):
                    pe.wait_ge(done, 1)
                    if t >= 2:
                        pe.wait_ge(kept, t - 1)
                    for j in range(2):
                        mm = pe.transpose(tps[:, t % 2, j * P:(j + 1) * P], r.yl[:, t, j * P:(j + 1) * P], g.ident)
                    mm.then_inc(turned, 1)

            @block.gpsimd
            def _(pool):
                pool.tensor_tensor(g.vb[:, :, :].rearrange("p t (h n) -> p (t h) n", h=B_HEADS),
                                   g.vb[:, :, :].rearrange("p t (h n) -> p (t h) n", h=B_HEADS),
                                   spread(r.bonus[:, :, :].rearrange("p t h -> p (t h)"), 2, HD), ALU.mult).then_inc(vbon, 1)

            @block.scalar
            def _(act):
                for t in range(NT):
                    act.wait_ge(gated, t + 1)
                    act.activation(gate[:, t, :], gps[:, t % 2, 0:B_W], ACT.Copy).then_inc(gate_kept, 1)
                act.wait_ge(var, 1)
                act.activation(st[:, 2, :], st[:, 1, :], ACT.Sqrt).then_inc(root, 1)
                for t in range(NT):
                    act.wait_ge(turned, t + 1)
                    act.activation(g.mixT[:, 4:6, t * P:(t + 1) * P], tps[:, t % 2, 0:2 * P].rearrange("p (j n) -> p j n", j=2),
                                   ACT.Copy).then_inc(kept, 1)

            @block.vector
            def _(dve):
                link = Link(dve, chain)
                for d in range(2):
                    dve.memset(xs[:, 2 * d:2 * d + 2, order[d][0], :], 0.0).then_inc(zeroed, 1)
                for n in range(NCH - 1):
                    dve.wait_ge(moved, n + 1)
                    for d in range(2):
                        c, nxt, q = order[d][n], order[d][n + 1], slice(2 * d, 2 * d + 2)
                        dve.tensor_tensor(xs[:, q, nxt, :], sps[:, n % 2, 128 * d:128 * d + 128].rearrange("p (b n) -> p b n", b=2),
                                          r.hh[:, q, c * CH:c * CH + CH], ALU.add).then_inc(stepped, 1)
                for t in range(NT):
                    dve.wait_ge(read, t + 1)
                    yt = r.yl[:, t, :].rearrange("p (b a n) -> p a b n", b=2, a=2)
                    dve.tensor_tensor(yt, yt, yps[:, t % 2, :, 0:P].rearrange("p a (b n) -> p a b n", b=2),
                                      ALU.add).then_inc(added, 1)
                dve.wait_ge(added, NT)
                link(dve.tensor_reduce(st[:, 0, :], yh, AX_X, ALU.add))
                link(dve.tensor_scalar(st[:, 0, :], st[:, 0, :], 1.0 / HD, None, ALU.mult))
                link(dve.tensor_tensor(yh, yh, spread(st[:, 0, :], 2, HD), ALU.subtract))
                link(dve.tensor_tensor(tmp[:, :, :], yh, yh, ALU.mult))
                link(dve.tensor_reduce(st[:, 1, :], tmp[:, :, :], AX_X, ALU.add))
                dve.tensor_scalar(st[:, 1, :], st[:, 1, :], 1.0 / HD, LNX_EPS, ALU.mult, ALU.add).then_inc(var, 1)
                dve.wait_ge(root, 1)
                link(dve.reciprocal(st[:, 3, :], st[:, 2, :]))
                link(dve.tensor_tensor(yh, yh, spread(st[:, 3, :], 2, HD), ALU.mult))
                dve.wait_ge(loaded, 32)
                link(dve.tensor_tensor(yf, yf, spread(ln[:, 0, :], 1, NT), ALU.mult))
                link(dve.tensor_tensor(yf, yf, spread(ln[:, 1, :], 1, NT), ALU.add))
                dve.wait_ge(vbon, 1)
                link(dve.tensor_tensor(yf, yf, g.vb[:, :, :], ALU.add))
                dve.wait_ge(gate_kept, NT)
                dve.tensor_tensor(yf, yf, gate[:, :, :], ALU.mult).then_inc(done, 1)


def rwkv(nc, g, layer):
    with ExitStack() as stack:
        a, r = Scope(nc, stack), Buffers()
        r.cs = g.fm[:, 7:11, :]
        r.yl = a.sb("rk_yl", [P, NT, B_W])
        r.bonus = a.sb("rk_bonus", [P, NT, B_HEADS])
        r.pt, r.mt, r.hh = (a.sb("rk_" + n, [P, 4, T]) for n in ("pt", "mt", "hh"))
        with ExitStack() as chunks:
            c = Scope(nc, chunks)
            r.xc, r.b, r.kd = (c.sb("rk_" + n, [P, 4, T]) for n in ("xc", "b", "kd"))
            r.nkk = c.sb("rk_nkk", [P, 2, T])
            rwkv_gates(nc, g, r, layer)
            rwkv_chunks(nc, g, r, layer)
        rwkv_readout(nc, g, r, layer)




def mix_out(nc, g, layer):
    with ExitStack() as stack:
        a = Scope(nc, stack)
        x, z = a.sb("mo_x", [P, NT, D]), a.sb("mo_z", [P, 2, D])
        w, gate = a.sb("mo_w", [P, KD, D]), a.sb("mo_gate", [P, 2, D])
        junk, st = a.sb("mo_junk", [P, D]), a.sb("mo_st", [P, 4, NT])
        ps = a.ps("mo_ps", [P, 3, D])
        names = ("w_loaded", "rows_loaded", "made", "squared", "var", "root", "inv", "scaled", "added", "stored")
        s = Buffers()
        (s.w_loaded, s.rows_loaded, s.made, s.squared, s.var, s.root, s.inv, s.scaled, s.added, s.stored) = (g.sem("mo_" + n) for n in names)
        x_loaded = [g.sem(f"mo_x_loaded{t}") for t in range(NT)]
        with nc.Block(no_gpsimd_drain=True) as block:

            @block.sync
            def _(sync):
                sync.dma_start(w[:, :, :], at(g.w_out, layer).rearrange("(k p) n -> p k n", p=P)).then_inc(s.w_loaded, 16)
                load_mod_rows(sync, g, gate, 2, s.rows_loaded)
                for t in range(NT):
                    sync.dma_start(x[:, t, :], g.stream[t * P:(t + 1) * P, :]).then_inc(x_loaded[t], 16)
                for t in range(NT):
                    sync.wait_ge(s.added, t + 1)
                    sync.dma_start(g.stream[t * P:(t + 1) * P, :], x[:, t, :]).then_inc(s.stored, 16)
                sync.wait_ge(s.stored, 16 * NT)

            @block.tensor
            def _(pe):
                pe.wait_ge(s.w_loaded, 16)
                for t in range(NT):
                    if t >= 3:
                        pe.wait_ge(s.scaled, t - 2)
                    for half in range(2):
                        for k in range(KD):
                            mm = pe.matmul(ps[:, t % 3, half * 512:half * 512 + 512], g.mixT[:, k, t * P:(t + 1) * P],
                                           w[:, k, half * 512:half * 512 + 512], start=(k == 0), stop=(k == KD - 1))
                    mm.then_inc(s.made, 1)

            @block.scalar
            def _(act):
                for t in range(NT):
                    act.wait_ge(s.made, t + 1)
                    act.wait_ge(s.squared, t)
                    act.activation(junk[:, :], ps[:, t % 3, :], ACT.Square, accum_out=st[:, 0, t:t + 1]).then_inc(s.squared, 1)
                    act.wait_ge(s.var, t + 1)
                    act.activation(st[:, 2, t:t + 1], st[:, 1, t:t + 1], ACT.Sqrt).then_inc(s.root, 1)

            @block.vector
            def _(dve):
                for t in range(NT):
                    dve.wait_ge(s.squared, t + 1)
                    dve.tensor_scalar(st[:, 1, t:t + 1], st[:, 0, t:t + 1], 1.0 / D, EPS, ALU.mult, ALU.add).then_inc(s.var, 1)
                    dve.wait_ge(s.root, t + 1)
                    dve.reciprocal(st[:, 3, t:t + 1], st[:, 2, t:t + 1]).then_inc(s.inv, 1)
                    dve.wait_ge(s.inv, t + 1)
                    if t == 0:
                        dve.wait_ge(s.rows_loaded, 32)
                    if t >= 2:
                        dve.wait_ge(s.added, t - 1)
                    dve.scalar_tensor_tensor(z[:, t % 2, :], ps[:, t % 3, :], st[:, 3, t:t + 1], gate[:, int(t >= NTC), :],
                                             ALU.mult, ALU.mult).then_inc(s.scaled, 1)

            @block.gpsimd
            def _(pool):
                for t in range(NT):
                    pool.wait_ge(s.scaled, t + 1)
                    pool.wait_ge(x_loaded[t], 16)
                    pool.tensor_tensor(x[:, t, :], x[:, t, :], z[:, t % 2, :], ALU.add).then_inc(s.added, 1)



RAW_SLOTS, HI_SLOTS = 4, 4
PARTS = 24


def expert_part(g, layer, pair, n):
    kind, e = ((g.w_gate_e, 0), (g.w_up_e, 0), (g.w_gate_e, 1), (g.w_up_e, 1), (g.w_down_e, 0), (g.w_down_e, 1))[n // 4]
    q = n % 4
    return at(at(kind, layer), pair * 2 + e).rearrange("(p k) n -> p k n", k=KD)[:, 2 * q:2 * q + 2, :]


def routing(nc, g, f, layer):
    with ExitStack() as stack:
        a = Scope(nc, stack)
        gain, shift = a.sb("rt_gain", [P, 2, D]), a.sb("rt_shift", [P, 2, D])
        junk, st = a.sb("rt_junk", [P, D]), a.sb("rt_st", [P, 24])
        hT, wr = a.sb("rt_hT", [P, 2, KD, P]), a.sb("rt_wr", [P, KD, NE])
        lg, sm = a.sb("rt_lg", [P, NT, NE]), a.sb("rt_sm", [P, 3, NT])
        affT, work, sel, rank = (a.sb("rt_" + n, [NE, T]) for n in ("affT", "work", "sel", "rank"))
        ones, best = a.sb("rt_ones", [NE, SEQ]), a.sb("rt_best", [NE, 8])
        tp = a.ps("rt_tp", [P, 2, 4, P])
        lps = a.ps("rt_lps", [P, NT, NE])
        aps = a.ps("rt_aps", [NE, 1024])
        sps = a.ps("rt_sps", [P, NT, NE])
        norm = PreNorm(g, "rt", f.h, f.h, gain, shift, junk[:, :], st)
        x_loaded = [g.sem(f"rt_x_loaded{t}") for t in range(NT)]
        rows_loaded, turned, hT_ready = g.sem("rt_rows_loaded"), g.sem("rt_turned"), g.sem("rt_hT_ready")
        routed, chain, centred, exped = g.sem("rt_routed"), g.sem("rt_chain"), g.sem("rt_centred"), g.sem("rt_exped")
        zeroed = g.sem("rt_zeroed")
        aff_ready, aff_turned = g.sem("rt_aff_ready"), g.sem("rt_aff_turned")
        slots_ready, slots_turned = g.sem("rt_slots_ready"), g.sem("rt_slots_turned")
        lgf = lg[:, :, :]
        with nc.Block(no_gpsimd_drain=True) as block:

            @block.sync
            def _(sync):
                for t in range(NT):
                    sync.dma_start(f.h[:, t, :], g.stream[t * P:(t + 1) * P, :]).then_inc(x_loaded[t], 16)
                load_mod_rows(sync, g, gain, 4, rows_loaded)
                load_mod_rows(sync, g, shift, 3, rows_loaded)
                sync.dma_start(wr[:, :, :], at(g.w_router, layer).rearrange("(k p) n -> p k n", p=P)).then_inc(rows_loaded, 16)
                for n in range(RAW_SLOTS):
                    sync.dma_start(f.w_raw[:, n, :, :], expert_part(g, layer, 0, n)).then_inc(f.w_loaded[n], 16)

            @block.scalar
            def _(act):
                norm.scalar(act, lambda e, t: e.wait_ge(x_loaded[t], 16))
                for n in range(2 * NT):
                    act.wait_ge(turned, n + 1)
                    t, half = n // 2, n % 2
                    if t >= 2:
                        act.wait_ge(routed, t - 1)
                    act.activation(hT[:, t % 2, 4 * half:4 * half + 4, :], tp[:, half, :, :], ACT.Copy).then_inc(hT_ready, 1)
                act.wait_ge(centred, 1)
                act.activation(lgf, lgf, ACT.Exp).then_inc(exped, 1)

            @block.gpsimd
            def _(pool):
                norm.gpsimd(pool)
                pool.memset(f.acc[:, :, :], 0.0).then_inc(zeroed, 1)
                pool.wait_ge(zeroed, 1)

            @block.tensor
            def _(pe):
                def route(t):
                    pe.wait_ge(hT_ready, 2 * t + 2)
                    for k in range(KD):
                        mm = pe.matmul(lps[:, t, :], hT[:, t % 2, k, :], wr[:, k, :], start=(k == 0), stop=(k == KD - 1))
                    mm.then_inc(routed, 1)

                pe.wait_ge(rows_loaded, 80)
                for t in range(NT):
                    pe.wait_ge(norm.shifted, t + 1)
                    for half in range(2):
                        if t:
                            pe.wait_ge(hT_ready, 2 * t - 1 + half)
                        for j in range(4):
                            k = 4 * half + j
                            mm = pe.transpose(tp[:, half, j, :], f.h[:, t, k * P:(k + 1) * P], g.ident)
                        mm.then_inc(turned, 1)
                    if t:
                        route(t - 1)
                route(NT - 1)
                pe.wait_ge(aff_ready, 1)
                for t in range(NT):
                    mm = pe.transpose(aps[:, t * P:(t + 1) * P], f.aff[:, t, 0:NE], g.ident)
                mm.then_inc(aff_turned, 1)
                pe.wait_ge(slots_ready, 1)
                for t in range(NT):
                    mm = pe.transpose(sps[:, t, :], rank[:, t * P:(t + 1) * P], g.cst[0:NE, O_ID:O_ID + NE])
                mm.then_inc(slots_turned, 1)

            @block.vector
            def _(dve):
                link = Link(dve, chain)
                norm.roots(dve)
                norm.vector(dve, lambda e: e.wait_ge(rows_loaded, 80))
                link(dve.memset(ones[:, :], 1.0))
                dve.wait_ge(routed, NT)
                link(dve.tensor_reduce(sm[:, 0, :], lps[:, :, :], AX_X, ALU.max))
                dve.tensor_tensor(lgf, lps[:, :, :], spread(sm[:, 0, :], 2, NE), ALU.subtract).then_inc(centred, 1)
                dve.wait_ge(exped, 1)
                link(dve.tensor_reduce(sm[:, 1, :], lgf, AX_X, ALU.add))
                link(dve.reciprocal(sm[:, 2, :], sm[:, 1, :]))
                dve.tensor_tensor(f.aff[:, :, 0:NE], lgf, spread(sm[:, 2, :], 2, NE), ALU.mult).then_inc(aff_ready, 1)
                dve.wait_ge(aff_turned, 1)
                link(dve.tensor_copy(work[:, :], aps[:, 0:T]))
                for lo, hi, cap in ((0, CTX, CAP_C), (CTX, T, CAP_L)):
                    for _ in range(cap // 8):
                        link(dve.max(best[:, :], work[:, lo:hi]))
                        link(dve.match_replace(work[:, lo:hi], best[:, :], work[:, lo:hi], -1.0))
                link(dve.tensor_scalar(sel[:, :], work[:, :], 0.0, None, ALU.is_lt))
                for lo, hi in ((0, CTX), (CTX, T)):
                    link(dve.tensor_tensor_scan(rank[:, lo:hi], ones[:, 0:hi - lo], sel[:, lo:hi], 0.0, ALU.mult, ALU.add))
                link(dve.tensor_tensor(rank[:, :], rank[:, :], sel[:, :], ALU.mult))
                dve.tensor_scalar(rank[:, :], rank[:, :], 1.0, None, ALU.subtract).then_inc(slots_ready, 1)
                link(dve.memset(f.slot[:, :, NE:NE + 2], -1.0))
                link(dve.memset(f.aff[:, :, NE:NE + 2], 0.0))
                dve.wait_ge(slots_turned, 1)
                dve.tensor_copy(f.slot[:, :, 0:NE], sps[:, :, :])



U_GATHER, U_PICK, U_HID, U_SCATTER = 4, 2, 2, 12
NTL = NT - NTC


def experts(nc, g, f, layer):
    first_uses = U_GATHER + U_PICK + 2 * U_HID + U_GATHER
    uses = U_SCATTER + U_PICK + 2 * U_HID + U_GATHER
    with ExitStack() as stack:
        a = Scope(nc, stack)
        pick_l, pick_c = a.sb("ex_pick_l", [P, NTL, 2, CAP_L]), a.sb("ex_pick_c", [P, NTC, 2, CAP_C])
        pickT_l, pickT_c = a.sb("ex_pickT_l", [P, NTL * P], F32R), a.sb("ex_pickT_c", [2 * CAP_C, NTC * P], F32R)
        aff_now = a.sb("ex_aff_now", [P, NT, 2])
        weight = a.sb("ex_weight", [CAP, 4])
        xe_hi, xe_lo = a.sb("ex_xe_hi", [P, KD, 2, CAP], F32R), a.sb("ex_xe_lo", [P, KD, 2, CAP], F32R)
        sg, hid = a.sb("ex_sg", [CAP, DE]), a.sb("ex_hid", [CAP, DE])
        hidT_hi, hidT_lo = a.sb("ex_hidT_hi", [P, KD, CAP], F32R), a.sb("ex_hidT_lo", [P, KD, CAP], F32R)
        ye_l, ye_c = a.sb("ex_ye_l", [P, D]), a.sb("ex_ye_c", [2 * CAP_C, D])
        ye_hi_l, ye_hi_c = a.sb("ex_ye_hi_l", [P, D], F32R), a.sb("ex_ye_hi_c", [2 * CAP_C, D], F32R)
        ye_lo_l, ye_lo_c = a.sb("ex_ye_lo_l", [P, D], F32R), a.sb("ex_ye_lo_c", [2 * CAP_C, D], F32R)
        misc = a.ps("ex_misc", [P, 2, 512])
        gp, up, yp = (a.ps("ex_" + n, [CAP, 2, 512]) for n in ("gp", "up", "yp"))
        names = ("picked", "used", "free", "hi", "lo_v", "lo_p", "w_used", "silu", "hid", "kept", "ye_hi", "ye_lo")
        s = Buffers()
        (s.picked, s.used, s.free, s.hi, s.lo_v, s.lo_p, s.w_used, s.silu, s.hid, s.kept, s.ye_hi,
         s.ye_lo) = (g.sem("ex_" + n) for n in names)

        def start(j, peeled):
            return U_GATHER if peeled else (j - 1) * uses + first_uses

        def layout_uses(peeled):
            at_, order = {}, ([] if peeled else ["scatter"] * U_SCATTER) + ["pick"] * U_PICK + ["hid0"] * U_HID + \
                ["hid1"] * U_HID + ["gather"] * U_GATHER
            for n, what in enumerate(order):
                at_.setdefault(what, n)
            return at_

        scatter_places = [(t, half) for t in range(NT) for half in range(2)]

        def both(eng, body):
            body(0, True)
            with eng.Fori(1, NE // 2) as j:
                body(j, False)

        def take(pe, m):
            if not (isinstance(m, int) and m < 2):
                pe.wait_ge(s.free, m - 1)

        with nc.Block(no_gpsimd_drain=True) as block:

            @block.sync
            def _(sync):
                def body(j, peeled):
                    for n in range(PARTS):
                        if peeled and n < RAW_SLOTS:
                            continue
                        if n % 4 == 3:
                            sync.wait_ge(s.lo_p, j * (PARTS // 4) + (n - RAW_SLOTS) // 4 + 1)
                        else:
                            m = n - RAW_SLOTS
                            sync.wait_ge(s.lo_v, j * (PARTS - PARTS // 4) + m - m // 4 + 1)
                        sync.dma_start(f.w_raw[:, n % RAW_SLOTS, :, :],
                                       expert_part(g, layer, j, n)).then_inc(f.w_loaded[n % RAW_SLOTS], 16)

                both(sync, body)

            @block.tensor
            def _(pe):
                def part(j, peeled, n, hi, lo, out):
                    pe.wait_ge(s.hi, j * PARTS + n + 1)
                    w_hi, w_lo = f.w_hi[:, n % HI_SLOTS, :, :], f.w_lo[:, n % HI_SLOTS, :, :]
                    q = n % 4
                    for i in range(2):
                        for half in range(2):
                            cols = slice(half * 512, half * 512 + 512)
                            pe.matmul(out[:, half, :], hi(2 * q + i), w_hi[:, i, cols], start=(q == 0 and i == 0), stop=False)
                            pe.matmul(out[:, half, :], lo(2 * q + i), w_hi[:, i, cols], start=False, stop=False)
                    if n % 4 == 3:
                        pe.wait_ge(s.lo_p, j * (PARTS // 4) + n // 4 + 1)
                    else:
                        pe.wait_ge(s.lo_v, j * (PARTS - PARTS // 4) + n - n // 4 + 1)
                    for i in range(2):
                        for half in range(2):
                            cols = slice(half * 512, half * 512 + 512)
                            mm = pe.matmul(out[:, half, :], hi(2 * q + i), w_lo[:, i, cols], start=False, stop=(q == 3 and i == 1))
                    mm.then_inc(s.w_used, 1)

                def gate_up(j, peeled, n):
                    e, out, read = n // 8, *((gp, s.silu), (up, s.hid))[n // 4 % 2]
                    if n % 4 == 0 and not (peeled and e == 0):
                        pe.wait_ge(read, j * 4 + e * 2)
                    part(j, peeled, n, lambda k: xe_hi[:, k, e, :], lambda k: xe_lo[:, k, e, :], out)

                def down(j, peeled, e, hidT_free):
                    pe.wait_ge(s.free, hidT_free)
                    if not (peeled and e == 0):
                        pe.wait_ge(s.kept, j * 4 + e * 2)
                    for n in range(16 + 4 * e, 20 + 4 * e):
                        part(j, peeled, n, lambda k: hidT_hi[:, k, :], lambda k: hidT_lo[:, k, :], yp)

                def turn_hid(j, e, m0):
                    pe.wait_ge(s.hid, j * 4 + e * 2 + 2)
                    for n in range(2):
                        take(pe, m0 + n)
                        for i in range(4):
                            k = 4 * n + i
                            mm = pe.transpose(misc[:, n, i * CAP:(i + 1) * CAP], hid[:, k:DE:KD], g.cst[0:CAP, O_ID:O_ID + CAP])
                        mm.then_inc(s.used, 1)

                def gather(picked, m0):
                    pe.wait_ge(s.picked, picked)
                    for n in range(U_GATHER):
                        take(pe, m0 + n)
                        for i in range(2):
                            o = misc[:, n % 2, i * 2 * CAP:(i + 1) * 2 * CAP].rearrange("p (e c) -> p e c", e=2)
                            k = 2 * n + i
                            for t in range(NTL):
                                pe.matmul(o[:, :, 0:CAP_L], f.h[:, NTC + t, k:D:KD], pick_l[:, t, :, :],
                                          start=(t == 0), stop=(t == NTL - 1))
                            for t in range(NTC):
                                mm = pe.matmul(o[:, :, CAP_L:CAP], f.h[:, t, k:D:KD], pick_c[:, t, :, :],
                                               start=(t == 0), stop=(t == NTC - 1))
                        mm.then_inc(s.used, 1)

                def scatter(m0, places):
                    for n in places:
                        t, half = scatter_places[n]
                        take(pe, m0 + n)
                        cols = slice(half * 512, half * 512 + 512)
                        if t < NTC:
                            pick, hi, lo = pickT_c[:, t * P:(t + 1) * P], ye_hi_c, ye_lo_c
                        else:
                            pick, hi, lo = pickT_l[:, (t - NTC) * P:(t - NTC + 1) * P], ye_hi_l, ye_lo_l
                        pe.matmul(misc[:, n % 2, :], pick, hi[:, cols], start=True, stop=False)
                        pe.matmul(misc[:, n % 2, :], pick, lo[:, cols], start=False, stop=True).then_inc(s.used, 1)

                def turn_picks(j, m0):
                    for n in range(2):
                        take(pe, m0 + n)
                    for t in range(NTL):
                        mm = pe.transpose(misc[:, 0, t * P:(t + 1) * P], pick_l[:, t, :, :].rearrange("p e c -> p (e c)"), g.ident)
                    mm.then_inc(s.used, 1)
                    for t in range(NTC):
                        pe.transpose(misc[0:2 * CAP_C, 1, t * P:(t + 1) * P], pick_c[:, t, :, :].rearrange("p e c -> p (e c)"), g.ident)
                    for e in range(2):
                        w0 = NTC * P + 2 * e
                        for pick, tiles, rows in ((pick_l, range(NTC, NT), slice(0, CAP_L)), (pick_c, range(NTC), slice(CAP_L, CAP))):
                            for t in tiles:
                                mm = pe.matmul(misc[rows, 1, w0:w0 + 2], pick[:, t - tiles[0], e, :], aff_now[:, t, :],
                                               start=(t == tiles[0]), stop=(t == tiles[-1]))
                    mm.then_inc(s.used, 1)

                gather(3, 0)
                pe.wait_ge(s.free, U_GATHER)

                def body(j, peeled):
                    m, where = start(j, peeled), layout_uses(peeled)
                    if not peeled:
                        pe.wait_ge(s.free, m)
                    for n in range(0, 4):
                        gate_up(j, peeled, n)
                    if not peeled:
                        pe.wait_ge(s.ye_lo, j * 2)
                    for n in range(4, 8):
                        if not peeled:
                            scatter(m + where["scatter"], range(3 * n - 12, 3 * n - 9))
                        gate_up(j, peeled, n)
                    turn_picks(j, m + where["pick"])
                    for n in range(8, 16):
                        if n == 10:
                            turn_hid(j, 0, m + where["hid0"])
                        gate_up(j, peeled, n)
                    down(j, peeled, 0, m + where["hid0"] + 2)
                    turn_hid(j, 1, m + where["hid1"])
                    gather(j * 3 + 6, m + where["gather"])
                    down(j, peeled, 1, m + where["hid1"] + 2)

                both(pe, body)
                pe.wait_ge(s.ye_lo, NE)
                scatter(start(NE // 2, False), range(U_SCATTER))

            @block.scalar
            def _(act):
                def high(j, peeled, ns):
                    for n in ns:
                        act.wait_ge(f.w_loaded[n % RAW_SLOTS], j * (16 * PARTS // RAW_SLOTS) + 16 * (n // RAW_SLOTS) + 16)
                        if not (peeled and n < HI_SLOTS):
                            act.wait_ge(s.w_used, j * PARTS + n - HI_SLOTS + 1)
                        act.activation(f.w_hi[:, n % HI_SLOTS, :, :], f.w_raw[:, n % RAW_SLOTS, :, :], ACT.Copy).then_inc(s.hi, 1)

                def silu(j, peeled, e):
                    act.wait_ge(s.w_used, j * PARTS + 8 * e + 4)
                    if not (peeled and e == 0):
                        act.wait_ge(s.hid, j * 4 + e * 2)
                    for half in range(2):
                        act.activation(sg[:, half * 512:half * 512 + 512], gp[:, half, :], ACT.Silu).then_inc(s.silu, 1)

                def keep(j, e):
                    act.wait_ge(s.w_used, j * PARTS + 20 + 4 * e)
                    for rows, dst, cap in ((slice(0, CAP_L), ye_l, CAP_L), (slice(CAP_L, CAP), ye_c, CAP_C)):
                        act.activation(dst[e * cap:(e + 1) * cap, :], yp[rows, :, :].rearrange("p h n -> p (h n)"),
                                       ACT.Copy, scale=weight[rows, 3 * e:3 * e + 1]).then_inc(s.kept, 1)

                def finish(j):
                    keep(j, 1)
                    act.wait_ge(s.kept, j * 4 + 4)
                    act.activation(ye_hi_l[:, :], ye_l[:, :], ACT.Copy).then_inc(s.ye_hi, 1)
                    act.activation(ye_hi_c[:, :], ye_c[:, :], ACT.Copy).then_inc(s.ye_hi, 1)

                def body(j, peeled):
                    high(j, peeled, range(0, 4))
                    if not peeled:
                        finish(j - 1)
                    high(j, peeled, range(4, 8))
                    silu(j, peeled, 0)
                    high(j, peeled, range(8, 16))
                    silu(j, peeled, 1)
                    high(j, peeled, range(16, 24))
                    act.wait_ge(s.free, start(j, peeled) + layout_uses(peeled)["pick"] + 2)
                    keep(j, 0)

                both(act, body)
                finish(NE // 2 - 1)

            def low(eng, j, ns, on_pool=False):
                for n in ns:
                    if (n % 4 == 3) != (on_pool):
                        continue
                    eng.wait_ge(s.hi, j * PARTS + n + 1)
                    eng.tensor_tensor(f.w_lo[:, n % HI_SLOTS, :, :], f.w_raw[:, n % RAW_SLOTS, :, :], f.w_hi[:, n % HI_SLOTS, :, :].bitcast(F32),
                                      ALU.subtract).then_inc(s.lo_p if n % 4 == 3 else s.lo_v, 1)

            @block.gpsimd
            def _(pool):
                with pool.Fori(0, NE // 2) as j:
                    low(pool, j, range(PARTS), True)
                pool.wait_ge(s.lo_p, NE // 2 * PARTS // 4)

            @block.vector
            def _(dve):
                def pick(j2):
                    iota = g.cst[:, O_IOTA:O_IOTA + CAP_L]
                    dve.tensor_copy(aff_now[:, :, :], f.aff[:, :, ds(j2, 2)]).then_inc(s.picked, 1)
                    for dst, tiles, cap, n in ((pick_l, slice(NTC, NT), CAP_L, NTL), (pick_c, slice(0, NTC), CAP_C, NTC)):
                        dve.tensor_tensor(dst[:, :, :, :], spread(f.slot[:, tiles, ds(j2, 2)], 3, cap),
                                          spread(spread(iota[:, 0:cap], 1, 2), 1, n), ALU.is_equal).then_inc(s.picked, 1)

                def split(hi, lo, src, count):
                    dve.tensor_copy(hi, src).then_inc(f.split, 1)
                    dve.wait_ge(f.split, count + 1)
                    dve.tensor_tensor(lo, src, hi.bitcast(F32), ALU.subtract).then_inc(s.free, 1)

                def gathered(m0, count):
                    for n in range(U_GATHER):
                        dve.wait_ge(s.used, m0 + n + 1)
                        split(*(x[:, 2 * n:2 * n + 2, :, :].rearrange("p k e c -> p (k e c)") for x in (xe_hi, xe_lo)),
                              misc[:, n % 2, 0:4 * CAP], count + n)

                def gated(j, e):
                    dve.wait_ge(s.w_used, j * PARTS + 8 * e + 8)
                    for half in range(2):
                        dve.wait_ge(s.silu, j * 4 + e * 2 + half + 1)
                        c = slice(half * 512, half * 512 + 512)
                        dve.tensor_tensor(hid[:, c], sg[:, c], up[:, half, :], ALU.mult).then_inc(s.hid, 1)

                def hid_turned(e, m0, count):
                    for n in range(2):
                        dve.wait_ge(s.used, m0 + n + 1)
                        split(*(x[:, 4 * n:4 * n + 4, :].rearrange("p k c -> p (k c)") for x in (hidT_hi, hidT_lo)),
                              misc[:, n, 0:4 * CAP], count + n)

                def ye_low(j):
                    for n, (lo, ye, hi) in enumerate(((ye_lo_l, ye_l, ye_hi_l), (ye_lo_c, ye_c, ye_hi_c))):
                        dve.wait_ge(s.ye_hi, j * 2 + n + 1)
                        dve.tensor_tensor(lo[:, :], ye[:, :], hi[:, :].bitcast(F32), ALU.subtract).then_inc(s.ye_lo, 1)

                def scattered(m0, places):
                    for n in places:
                        t, half = scatter_places[n]
                        dve.wait_ge(s.used, m0 + n + 1)
                        acc = f.acc[:, t, half * 512:half * 512 + 512]
                        dve.tensor_tensor(acc, acc, misc[:, n % 2, :], ALU.add).then_inc(s.free, 1)

                pick(0)
                gathered(0, 0)

                def body(j, peeled):
                    m, where = start(j, peeled), layout_uses(peeled)
                    low(dve, j, range(0, 4))
                    if peeled:
                        low(dve, j, range(4, 12))
                    else:
                        ye_low(j - 1)
                        low(dve, j, (4, 5))
                        for i, n in enumerate((6, 8, 9, 10)):
                            scattered(m + where["scatter"], range(3 * i, 3 * i + 3))
                            low(dve, j, (n,))
                    m0 = m + where["pick"]
                    dve.wait_ge(s.used, m0 + 1)
                    dve.tensor_copy(pickT_l[:, :], misc[:, 0, :]).then_inc(s.free, 1)
                    dve.wait_ge(s.used, m0 + 2)
                    dve.tensor_copy(pickT_c[:, :], misc[0:2 * CAP_C, 1, 0:NTC * P]).then_inc(f.split, 1)
                    dve.tensor_copy(weight[:, :], misc[0:CAP, 1, NTC * P:NTC * P + 4]).then_inc(s.free, 1)
                    gated(j, 0)
                    low(dve, j, (12,))
                    hid_turned(0, m + where["hid0"], j * 9 + U_GATHER + 1)
                    low(dve, j, (13,))
                    pick(j * 2 + 2)
                    low(dve, j, range(14, 20))
                    gated(j, 1)
                    low(dve, j, (20, 21))
                    hid_turned(1, m + where["hid1"], j * 9 + U_GATHER + 3)
                    gathered(m + where["gather"], j * 9 + U_GATHER + 5)
                    low(dve, j, (22,))

                both(dve, body)
                ye_low(NE // 2 - 1)
                scattered(start(NE // 2, False), range(U_SCATTER))


def ffn_out(nc, g, f, layer):
    with ExitStack() as stack:
        a = Scope(nc, stack)
        gate, junk, st = a.sb("fo_gate", [P, 2, D]), a.sb("fo_junk", [P, D]), a.sb("fo_st", [P, 4, NT])
        names = ("rows_loaded", "squared", "var", "root", "inv", "scaled", "added", "stored")
        s = Buffers()
        (s.rows_loaded, s.squared, s.var, s.root, s.inv, s.scaled, s.added, s.stored) = (g.sem("fo_" + n) for n in names)
        x_loaded = [g.sem(f"fo_x_loaded{t}") for t in range(NT)]
        with nc.Block(no_gpsimd_drain=True) as block:

            @block.sync
            def _(sync):
                load_mod_rows(sync, g, gate, 5, s.rows_loaded)
                for t in range(NT):
                    sync.dma_start(f.h[:, t, :], g.stream[t * P:(t + 1) * P, :]).then_inc(x_loaded[t], 16)
                for t in range(NT):
                    sync.wait_ge(s.added, t + 1)
                    sync.dma_start(g.stream[t * P:(t + 1) * P, :], f.h[:, t, :]).then_inc(s.stored, 16)
                sync.wait_ge(s.stored, 16 * NT)

            @block.scalar
            def _(act):
                for t in range(NT):
                    act.activation(junk[:, :], f.acc[:, t, :], ACT.Square, accum_out=st[:, 0, t:t + 1]).then_inc(s.squared, 1)
                    act.wait_ge(s.squared, t + 1)
                act.wait_ge(s.var, 1)
                act.activation(st[:, 2, :], st[:, 1, :], ACT.Sqrt).then_inc(s.root, 1)

            @block.vector
            def _(dve):
                dve.wait_ge(s.squared, NT)
                dve.tensor_scalar(st[:, 1, :], st[:, 0, :], 1.0 / D, EPS, ALU.mult, ALU.add).then_inc(s.var, 1)
                dve.wait_ge(s.root, 1)
                dve.reciprocal(st[:, 3, :], st[:, 2, :]).then_inc(s.inv, 1)
                dve.wait_ge(s.inv, 1)
                dve.wait_ge(s.rows_loaded, 32)
                for t in range(NT):
                    dve.scalar_tensor_tensor(f.acc[:, t, :], f.acc[:, t, :], st[:, 3, t:t + 1], gate[:, int(t >= NTC), :],
                                             ALU.mult, ALU.mult).then_inc(s.scaled, 1)

            @block.gpsimd
            def _(pool):
                for t in range(NT):
                    pool.wait_ge(s.scaled, t + 1)
                    pool.wait_ge(x_loaded[t], 16)
                    pool.tensor_tensor(f.h[:, t, :], f.h[:, t, :], f.acc[:, t, :], ALU.add).then_inc(s.added, 1)


def ffn(nc, g, layer):
    with ExitStack() as stack:
        a, f = Scope(nc, stack), Buffers()
        f.h, f.acc = a.sb("ff_h", [P, NT, D]), a.sb("ff_acc", [P, NT, D])
        f.aff, f.slot = a.sb("ff_aff", [P, NT, NE + 2]), a.sb("ff_slot", [P, NT, NE + 2])
        f.w_raw = a.sb("ff_w_raw", [P, RAW_SLOTS, 2, D])
        f.w_hi, f.w_lo = (a.sb("ff_w" + n, [P, HI_SLOTS, 2, D], F32R) for n in ("_hi", "_lo"))
        f.w_loaded = [g.sem(f"ff_w_loaded{i}") for i in range(RAW_SLOTS)]
        f.split = g.sem("ff_split")
        routing(nc, g, f, layer)
        experts(nc, g, f, layer)
        ffn_out(nc, g, f, layer)


class Shared:

    def __init__(self, nc, stack):
        self.nc, self.stack, self.nums = nc, stack, []

    def sem(self, name):
        s = self.stack.enter_context(self.nc.semaphore(name))
        self.nums.append(s.num)
        return s

    @contextmanager
    def semaphores(self):
        outer, nums = self.stack, self.nums
        with ExitStack() as stack:
            self.stack, self.nums = stack, []
            yield
            first, last = min(self.nums), max(self.nums)
            assert last - first + 1 == len(self.nums)
            self.nc.all_engine_barrier(sems_to_clear=range(first, last + 1))
        self.stack, self.nums = outer, nums


def load_constants(nc, g, c_cols, consts, stream_in):
    loaded, silu_done, copied = g.sem("const_loaded"), g.sem("silu_done"), g.sem("stream_copied")
    with nc.Block(no_gpsimd_drain=True) as block:

        @block.sync
        def _(sync):
            sync.dma_start(g.cst[:, :], consts).then_inc(loaded, 16)
            sync.dma_start(g.silu_c[:, :, :], c_cols).then_inc(loaded, 16)
            for i, src in enumerate(stream_in):
                sync.dma_start(g.stream[i * CTX:i * CTX + src.shape[0], :], src).then_inc(copied, 16)
            sync.wait_ge(copied, 32)

        @block.scalar
        def _(act):
            act.wait_ge(loaded, 32)
            act.activation(g.silu_c[:, :, :], g.silu_c[:, :, :], ACT.Silu).then_inc(silu_done, 1)
            act.wait_ge(silu_done, 1)


def mixing(nc, g, layer):
    with ExitStack() as stack, ExitStack() as right:
        m = Scope(nc, stack)
        g.vb = m.sb("vb", [P, NT, B_W])
        g.fm = m.sb("fm", [P, 11, T])
        with ExitStack() as attending:
            a = Scope(nc, attending)
            g.qkv = a.sb("qkv", [P, NT, A_W + 2 * A_KVW])
            g.vn = a.sb("vn", [P, NT, C_W])
            with ExitStack() as projecting:
                j = projection_buffers(g, Scope(nc, projecting, "right"))
                modulation(nc, g, j, layer)
                projection(nc, g, j, layer)
            g.mixT = Scope(nc, right, "right").sb("mixT", [P, KD, T])
            attention(nc, g, layer)
        rwkv(nc, g, layer)
        mix_out(nc, g, layer)


def build(nc, c_cols, consts, rope, x, ctx, w_mod, b_mod, gains, w_in, w_out, cols, rows, bias, w_up, a_up, g_up,
          w_router, w_e_gate, w_e_up, w_e_down, out):
    with ExitStack() as stack:
        g = Shared(nc, stack)
        g.w_mod, g.b_mod, g.gains, g.w_in, g.w_out, g.cols_d, g.rows_d = w_mod, b_mod, gains, w_in, w_out, cols, rows
        g.rope_d, g.bias_d, g.w_up, g.a_up, g.g_up, g.w_router = rope, bias, w_up, a_up, g_up, w_router
        g.w_gate_e, g.w_up_e, g.w_down_e = w_e_gate, w_e_up, w_e_down
        g.stream = nc.dram_tensor("stream", [T, D], F32).ap()
        g.mod_rows = nc.dram_tensor("mod_rows", [2, 6 * D], F32).ap()
        a = Scope(nc, stack)
        g.cst = a.sb("cst", [P, N_CST])
        g.silu_c = a.sb("silu_c", [P, KD, 2])
        g.ident = g.cst[:, O_ID:O_ID + P]
        load_constants(nc, g, c_cols, consts, [ctx, x])
        with nc.Fori(0, DEPTH) as layer:
            with g.semaphores():
                mixing(nc, g, layer)
            with g.semaphores():
                ffn(nc, g, layer)
        store_out(nc, g, out)


def store_out(nc, g, out):
    stored = g.sem("out_stored")
    with nc.Block(no_gpsimd_drain=True) as block:

        @block.sync
        def _(sync):
            sync.dma_start(out[0, :, :], g.stream[CTX:T, :]).then_inc(stored, 16)
            sync.wait_ge(stored, 16)


def constants():
    cst = np.zeros((P, N_CST), np.float32)
    p, r, c = np.arange(P), np.arange(P) % 64, np.arange(64)
    cst[:, O_ID:O_ID + P] = np.eye(P)
    tri = [r[:, None] < c, r[:, None] <= c, r[:, None] > c, r[:, None] >= c]
    cst[:, O_TRI:O_TRI + 256] = np.concatenate(tri, 1)
    for lv in range(6):
        same = (r[:, None] >> (lv + 1)) == (c >> (lv + 1))
        cst[:, O_LM + 64 * lv:O_LM + 64 * lv + 64] = same & ((r[:, None] >> lv) != (c >> lv))
    cst[:, O_HB:O_HB + P] = (p[:, None] // 64) == (p[None, :] // 64)
    cst[:, O_HS:O_HS + 2] = (p[:, None] // 64) == np.arange(2)
    cst[:, O_IOTA:O_IOTA + 64] = c
    cst[:, O_I64:O_I64 + 64] = r[:, None] == c
    rope = np.zeros((T, 2, HD), np.float32)
    rope[:CTX, 0] = 1.0
    inv = (np.float32(10000.0) ** (-np.arange(16, dtype=np.float32) / np.float32(16))).astype(np.float32)
    for i, pos in enumerate((np.arange(SEQ) // GRID, np.arange(SEQ) % GRID)):
        ang = pos.astype(np.float32)[:, None] * inv[None, :]
        cos, sin = np.cos(ang), np.sin(ang)
        rope[CTX:, 0, 32 * i:32 * i + 32] = np.concatenate([cos, cos], 1)
        rope[CTX:, 1, 32 * i:32 * i + 32] = np.concatenate([-sin, sin], 1)
    return cst, np.ascontiguousarray(rope.reshape(NT, P, 2 * HD).transpose(1, 0, 2))


def bias_layout(rpb):
    rp, c = np.arange(P) // GRID, np.arange(P) % GRID
    m, kc = np.arange(1, RPB_M + 1), np.arange(GRID)
    start = np.clip(c - WIN_COLS // 2, 0, GRID - WIN_COLS)
    row = m[None, :] - rp[:, None]
    col = kc[None, :] - c[:, None] + WIN_COLS - 1
    inside = (kc[None, :] >= start[:, None]) & (kc[None, :] < start[:, None] + WIN_COLS)
    padded = np.full((*rpb.shape[:3], 2 * WIN_COLS), np.float32(NEG))
    padded[..., :2 * WIN_COLS - 1] = rpb
    col = np.where(inside, col, 2 * WIN_COLS - 1)
    laid = padded[:, :, row[:, :, None], col[:, None, :]]
    return np.ascontiguousarray(laid.transpose(0, 2, 1, 3, 4)).reshape(DEPTH, P, C_HEADS * RPB_M * GRID)


def layout(inputs):
    f = {k: np.asarray(v) for k, v in inputs.items()}
    cst, rope = constants()

    def columns(v):
        return v.reshape(DEPTH, -1, P).transpose(0, 2, 1)

    both = np.stack([f["c_ctx"], f["c"][0]], axis=-1)
    arrays = {
        "c_cols": both.reshape(KD, P, 2).transpose(1, 0, 2),
        "consts": cst,
        "rope": rope,
        "x": f["x"][0],
        "ctx": f["ctx"][0],
        "w_mod": f["w_mod"],
        "b_mod": f["b_mod"],
        "gains": np.concatenate([f[n] for n in ("g_pre_mix", "g_post_mix", "g_pre_ffn", "g_post_ffn")], 1),
        "w_in": f["w_in"],
        "w_out": f["w_out"],
        "cols": np.concatenate([columns(f[n]) for n in ("rk_w0", "rk_a0", "rk_k_k", "rk_k_a", "rk_r_k")], 2),
        "rows": np.concatenate([np.tile(f["q_gain"], (1, A_HEADS)), np.tile(f["k_gain"], (1, A_KV)),
                                f["rk_lnx_w"], f["rk_lnx_b"]], 1),
        "bias": bias_layout(f["rpb"]),
        "w_up": f["rk_w_up"].reshape(DEPTH, P, B_W),
        "a_up": f["rk_a_up"].reshape(DEPTH, P, B_W),
        "g_up": f["rk_g_up"],
        "w_router": f["w_router"],
        "w_e_gate": f["w_e_gate"],
        "w_e_up": f["w_e_up"],
        "w_e_down": f["w_e_down"],
    }
    return {k: np.ascontiguousarray(v) for k, v in arrays.items()}


def kernel(**inputs):
    import concourse.bacc as bacc
    from concourse.bass_utils import run_bass_kernel_spmd

    nc = bacc.Bacc("TRN2", target_bir_lowering=False, num_devices=1)
    arrays = layout(inputs)
    args = {n: nc.dram_tensor(n, v.shape, mybir.dt.from_np(v.dtype), kind="ExternalInput").ap() for n, v in arrays.items()}
    out = nc.dram_tensor("out", (1, SEQ, D), F32, kind="ExternalOutput").ap()
    build(nc, **args, out=out)
    r = run_bass_kernel_spmd(nc, [arrays], core_ids=[0])
    return r.results[0]["out"]
```

```python
from contextlib import ExitStack, contextmanager, nullcontext

import numpy as np

import concourse.bass as bass
from concourse import mybir

F32 = mybir.dt.float32
F32R = mybir.dt.float32r
ACT = mybir.ActivationFunctionType
ALU = mybir.AluOpType
AX_X = mybir.AxisListType.X
ds = bass.ds

P = 128
D = 1024
KD = D // P
SEQ, CTX = 512, 256
T = SEQ + CTX
NT, NTC = T // P, CTX // P
DEPTH = 2
HD = 64
A_HEADS, A_KV = 8, 2
A_GROUP = A_HEADS // A_KV
A_W, A_KVW = A_HEADS * HD, A_KV * HD
B_HEADS, B_W = 4, 256
C_HEADS, C_W = 4, 256
N_IN = A_W + 2 * A_KVW + 3 * B_W + 3 * P + 3 * C_W
GRID = 64
WIN_ROWS, WIN_COLS = 8, 16
RPB_M = 14
NE, DE = 16, 1024
CAP_L, CAP_C = 2 * SEQ // NE, 2 * CTX // NE
CAP = CAP_L + CAP_C
EPS, LNX_EPS = 1e-6, 64e-5
SCALE = HD ** -0.5
CH = 64
NCH = T // CH
NCC = CTX // CH
KAPPA = -float(np.exp(-0.5))
NEG = -1e30

O_ID, O_TRI, O_LM, O_HB, O_HS, O_IOTA, O_I64 = 0, 128, 384, 768, 896, 898, 962
N_CST = 1026
TRI_LT, TRI_LE, TRI_GT, TRI_GE = range(4)
C_W0, C_A0, C_KK, C_KA, C_RK, N_COL = 0, 4, 8, 10, 12, 14
R_GAIN, R_LNW, R_LNB, N_ROW = 0, 640, 896, 1152


class Scope:

    def __init__(self, nc, stack, side="left"):
        self.nc, self.stack, self.side = nc, stack, side

    def sb(self, name, shape, dtype=F32):
        return self.stack.enter_context(self.nc.sbuf_tensor(name, shape, dtype, side=self.side))

    def ps(self, name, shape):
        return self.stack.enter_context(self.nc.psum_tensor(name, shape, F32))


class Link:

    def __init__(self, eng, sem, base=0):
        self.eng, self.sem, self.n, self.base = eng, sem, 0, base

    def __call__(self, ins):
        ins.then_inc(self.sem, 1)
        self.n += 1
        self.eng.wait_ge(self.sem, self.base + self.n)


def at(ap, i):
    return ap[ds(i, 1)].squeeze(0)


def spread(ap, axis, n):
    v = ap.unsqueeze(axis)
    shape = list(v.shape)
    shape[axis] = n
    return v.to_broadcast(shape)




def modulation(nc, g, j, layer):
    NCHUNK, SLOTS, W, HW, SPLITS = 6 * D // 512, 3, 512, 256, 3
    with ExitStack() as stack:
        a = Scope(nc, stack)
        fm, qkv = (v.rearrange("p a b -> p (a b)") for v in (g.fm[:, :, :], g.qkv[:, :, :]))
        wm = [v.rearrange("p (k n) -> p k n", k=KD) for v in (fm[:, 0:KD * W], fm[:, KD * W:2 * KD * W], qkv[:, 0:KD * W])]
        w_hi, w_lo = (a.sb("mod_w" + n, [P, SPLITS, KD, HW], F32R) for n in ("_hi", "_lo"))
        rows = a.sb("mod_rows_sb", [2, 6, D])
        gains = a.sb("mod_gains", [2, 4, D])
        rowsf = rows[:, :, :].rearrange("s a b -> s (a b)")
        ps = a.ps("mod_ps", [2, 2, 512])
        w_loaded = [g.sem(f"mod_w_loaded{s}") for s in range(SLOTS)]
        w_high, w_low = g.sem("mod_w_high"), g.sem("mod_w_low")
        rows_loaded = g.sem("mod_rows_loaded")
        prod = g.sem("mod_product")
        biased = g.sem("mod_biased")
        folded = g.sem("mod_folded")
        stored = g.sem("mod_stored")
        wv = at(g.w_mod, layer).rearrange("(k p) n -> p k n", p=P)
        with nc.Block(no_gpsimd_drain=True) as block:

            @block.sync
            def _(sync):
                def load(c, s):
                    sync.dma_start(wm[s], wv[:, :, ds(c * W, W)]).then_inc(w_loaded[s], 16)

                load(0, 0)
                sync.dma_start(rowsf, at(g.b_mod, layer).partition_broadcast(2)).then_inc(rows_loaded, 16)
                sync.dma_start(gains[:, :, :].rearrange("s a b -> s (a b)"),
                               at(g.gains, layer).partition_broadcast(2)).then_inc(rows_loaded, 16)
                load(1, 1)
                load(2, 2)
                sync.wait_ge(g.stream_copied, 32)
                for t in range(NT):
                    sync.dma_start(j.x[:, t, :], g.stream[t * P:(t + 1) * P, :]).then_inc(j.x_loaded[t], 16)
                with sync.Fori(1, NCHUNK // SLOTS) as i:
                    for s in range(SLOTS):
                        sync.wait_ge(w_low, (i - 1) * 2 * SLOTS + 2 * s + 2)
                        load(i * SLOTS + s, s)
                for c in range(PJ_RAW):
                    load_w_in(sync, g, j, layer, c)
                sync.wait_ge(folded, 4)
                sync.dma_start(g.mod_rows[:, :], rowsf).then_inc(stored, 16)
                sync.wait_ge(stored, 16)

            @block.scalar
            def _(act):
                def body(i, last):
                    for s in range(SLOTS):
                        act.wait_ge(w_loaded[s], i * 16 + 16)
                        for half in range(2):
                            n = 2 * s + half
                            act.wait_ge(prod, i * 2 * SLOTS + n + 1)
                            act.activation(w_hi[:, n % SPLITS, :, :], wm[s][:, :, half * HW:half * HW + HW], ACT.Copy).then_inc(w_high, 1)
                            if last:
                                j.norm.square(act, n, lambda e, t: e.wait_ge(j.x_loaded[t], 16))

                assert 2 * SLOTS == NT
                with act.Fori(0, NCHUNK // SLOTS - 1) as i:
                    body(i, False)
                body(NCHUNK // SLOTS - 1, True)
                j.norm.sqrt(act)

            @block.tensor
            def _(pe):
                pe.sem_inc(prod, SPLITS)
                pe.sem_inc(biased, 2)
                with pe.Fori(0, NCHUNK // SLOTS) as i:
                    for n in range(2 * SLOTS):
                        pe.wait_ge(w_low, i * 2 * SLOTS + n + 1)
                        pe.wait_ge(biased, i * 2 * SLOTS + n + 1)
                        for k in range(KD):
                            for m, (c, wk) in enumerate(((g.silu_hi, w_hi), (g.silu_lo, w_hi), (g.silu_hi, w_lo))):
                                mm = pe.matmul(ps[:, n % 2, 0:HW], c[:, k, :], wk[:, n % SPLITS, k, :],
                                               start=(k == 0 and m == 0), stop=(k == KD - 1 and m == 2))
                        mm.then_inc(prod, 1)

            @block.vector
            def _(dve):
                dve.wait_ge(rows_loaded, 32)
                with dve.Fori(0, NCHUNK // SLOTS) as i:
                    def low(n):
                        s, half = n // 2, n % 2
                        dve.wait_ge(w_high, i * 2 * SLOTS + n + 1)
                        dve.tensor_tensor(w_lo[:, n % SPLITS, :, :], wm[s][:, :, half * HW:half * HW + HW],
                                          w_hi[:, n % SPLITS, :, :].bitcast(F32), ALU.subtract).then_inc(w_low, 1)

                    def bias(n):
                        dve.wait_ge(prod, i * 2 * SLOTS + n + 1 + SPLITS)
                        c = i * SLOTS * W + n * HW
                        dve.tensor_tensor(rowsf[:, ds(c, HW)], ps[:, n % 2, 0:HW], rowsf[:, ds(c, HW)],
                                          ALU.add).then_inc(biased, 1)

                    low(0)
                    for n in range(1, 2 * SLOTS):
                        low(n)
                        bias(n - 1)
                    bias(2 * SLOTS - 1)
                dve.wait_ge(biased, 2 + 2 * NCHUNK)
                for sec, gain, pre in ((1, 0, True), (2, 1, False), (4, 2, True), (5, 3, False)):
                    dve.scalar_tensor_tensor(rows[:, sec, :], rows[:, sec, :], 1.0 if pre else 0.0, gains[:, gain, :],
                                             ALU.add, ALU.mult).then_inc(folded, 1)
                j.norm.roots(dve)




class PreNorm:

    def __init__(self, g, name, x, h, gain, shift, junk, stats):
        self.x, self.h, self.gain, self.shift, self.junk, self.st = x, h, gain, shift, junk, stats
        if junk is not None:
            self.squares, self.var, self.root, self.inv = (g.sem(f"{name}_{n}") for n in ("squares", "var", "root", "inv"))
        self.scaled, self.shifted = (g.sem(f"{name}_{n}") for n in ("scaled", "shifted"))

    def square(self, act, t, x_ready):
        x_ready(act, t)
        if t:
            act.wait_ge(self.squares, t)
        act.activation(self.junk, self.x[:, t, :], ACT.Square,
                       accum_out=self.st[:, t:t + 1]).then_inc(self.squares, 1)

    def sqrt(self, act):
        act.wait_ge(self.var, 1)
        act.activation(self.st[:, 8:8 + NT], self.st[:, 8:8 + NT], ACT.Sqrt).then_inc(self.root, 1)

    def roots(self, dve):
        dve.wait_ge(self.squares, NT)
        dve.tensor_scalar(self.st[:, 8:8 + NT], self.st[:, 0:NT], 1.0 / D, EPS, ALU.mult, ALU.add).then_inc(self.var, 1)
        dve.wait_ge(self.root, 1)
        dve.reciprocal(self.st[:, 16:16 + NT], self.st[:, 8:8 + NT]).then_inc(self.inv, 1)
        dve.wait_ge(self.inv, 1)

    def vector(self, dve, tiles=range(NT)):
        for t in tiles:
            dve.scalar_tensor_tensor(self.h[:, t, :], self.x[:, t, :], self.st[:, 16 + t:17 + t],
                                     self.gain[:, int(t >= NTC), :], ALU.mult, ALU.mult).then_inc(self.scaled, 1)

    def gpsimd(self, pool):
        for t in range(NT):
            pool.wait_ge(self.scaled, t + 1)
            pool.tensor_tensor(self.h[:, t, :], self.h[:, t, :], self.shift[:, int(t >= NTC), :],
                               ALU.add).then_inc(self.shifted, 1)


def load_mod_rows(eng, g, dst, section, sem):
    for s in range(2):
        load_mod_row(eng, g, dst, section, s, sem)


def load_mod_row(eng, g, dst, section, s, sem):
    eng.dma_start(dst[:, s, :], g.mod_rows[s, section * D:(section + 1) * D].partition_broadcast(P)).then_inc(sem, 16)



FM_OF = {768: 0, 896: 1, 1024: 2, 1152: 3, 1536: 4, 1664: 5, 1792: 6, 1920: 7, 2048: 8, 2176: 9, 2304: 10}


def proj_jobs():
    jobs = []
    for c in range(11):
        base = c * 256
        if base < 768:
            jobs.append((c, "qkv", 0, 256, base))
        elif base == 1280:
            jobs.append((c, "vb", 0, 256, 0))
        else:
            for off in (0, 128):
                col = base + off
                if col in FM_OF:
                    jobs.append((c, "fm", off, 128, FM_OF[col]))
                elif col < N_IN:
                    jobs.append((c, "vn", off, 128, col - 2432))
    return jobs


PJ_RAW, PJ_HI, PJ_W = 2, 2, 256


def load_w_in(sync, g, j, layer, c):
    width = min(PJ_W, N_IN - c * PJ_W)
    sync.dma_start(j.w[:, c % PJ_RAW, :, 0:width],
                   at(g.w_in, layer).rearrange("(k p) n -> p k n", p=P)[:, :, c * PJ_W:c * PJ_W + width]
                   ).then_inc(j.w_loaded[c % PJ_RAW], 16)


def projection_buffers(g, a):
    j = Buffers()
    j.x, j.stats = a.sb("pj_x", [P, NT, D]), a.sb("pj_stats", [P, 24])
    j.w = a.sb("pj_w", [P, PJ_RAW, KD, PJ_W])
    j.x_loaded = [g.sem(f"pj_x_loaded{t}") for t in range(NT)]
    j.w_loaded = [g.sem(f"pj_w_loaded{s}") for s in range(PJ_RAW)]
    j.norm = PreNorm(g, "pj", j.x, j.x, None, None, g.vb[:, :, :].rearrange("p t n -> p (t n)")[:, 0:D], j.stats)
    return j


class Rotary:
    NH = A_HEADS + A_KV
    W = NH * HD

    def __init__(self, g, a, x):
        NH, W = self.NH, self.W
        self.g = g
        self.rope = x[:, 0, 0:NT * 2 * HD].rearrange("p (t n) -> p t n", t=NT)
        self.gain = x[:, 1, 0:W]
        self.tmp, self.tmp2 = x[:, 2:4, 0:W], x[:, 4:6, 0:W]
        self.ss = a.sb("qk_ss", [P, 3, NT, NH])
        self.ssf = self.ss[:, :, :, :].rearrange("p a t h -> p a (t h)")
        (self.tables, self.squared, self.summed, self.var, self.root, self.inv, self.scaled, self.gained, self.cosed,
         self.sined, self.rotated) = (g.sem("qk_" + n) for n in (
             "tables", "squared", "summed", "var", "root", "inv", "scaled", "gained", "cosed", "sined", "rotated"))

    def heads(self, v):
        return v.rearrange("p (h d) -> p h d", h=self.NH)

    def qk(self, t):
        return self.g.qkv[:, t, 0:self.W]

    def parts(self, v):
        return v.rearrange("p (h r s e) -> p h r s e", h=self.NH, r=2, s=2)

    def load(self, sync, layer):
        sync.dma_start(self.rope, self.g.rope_d).then_inc(self.tables, 16)
        sync.dma_start(self.gain, at(self.g.rows_d, layer)[R_GAIN:R_GAIN + self.W].partition_broadcast(P)).then_inc(self.tables, 16)

    def sum_squares(self, dve, t):
        if t >= 2:
            dve.wait_ge(self.summed, t - 1)
        dve.tensor_tensor(self.tmp[:, t % 2, :], self.qk(t), self.qk(t), ALU.mult).then_inc(self.squared, 1)
        dve.wait_ge(self.squared, t + 1)
        dve.tensor_reduce(self.ss[:, 0, t, :], self.heads(self.tmp[:, t % 2, :]), AX_X, ALU.add).then_inc(self.summed, 1)

    def variance(self, dve):
        dve.wait_ge(self.summed, NT)
        dve.tensor_scalar(self.ssf[:, 1, :], self.ssf[:, 0, :], 1.0 / HD, EPS, ALU.mult, ALU.add).then_inc(self.var, 1)

    def sqrt(self, act):
        act.wait_ge(self.var, 1)
        act.activation(self.ssf[:, 2, :], self.ssf[:, 1, :], ACT.Sqrt).then_inc(self.root, 1)

    def inverse(self, dve):
        dve.wait_ge(self.root, 1)
        dve.reciprocal(self.ssf[:, 0, :], self.ssf[:, 2, :]).then_inc(self.inv, 1)
        dve.wait_ge(self.inv, 1)

    def scale(self, dve, t):
        dve.tensor_tensor(self.heads(self.qk(t)), self.heads(self.qk(t)), spread(self.ss[:, 0, t, :], 2, HD),
                          ALU.mult).then_inc(self.scaled, 1)

    def rotate(self, dve, t):
        i = t % 2
        dve.wait_ge(self.gained, t + 1)
        if t >= 2:
            dve.wait_ge(self.rotated, 2 * t - 2)
        dve.tensor_tensor(self.heads(self.tmp[:, i, :]), self.heads(self.qk(t)), spread(self.rope[:, t, 0:HD], 1, self.NH),
                          ALU.mult).then_inc(self.cosed, 1)
        dve.wait_ge(self.cosed, t + 1)
        dve.wait_ge(self.sined, 2 * t + 2)
        q, k = slice(0, A_W), slice(A_W, self.W)
        dve.tensor_tensor(self.qk(t)[:, q].rearrange("p (g v d) -> p v g d", v=A_KV, d=HD),
                          self.tmp[:, i, q].rearrange("p (v g d) -> p v g d", v=A_KV, d=HD),
                          self.tmp2[:, i, q].rearrange("p (v g d) -> p v g d", v=A_KV, d=HD), ALU.add).then_inc(self.rotated, 1)
        dve.tensor_tensor(self.qk(t)[:, k], self.tmp[:, i, k], self.tmp2[:, i, k], ALU.add).then_inc(self.rotated, 1)

    def gpsimd(self, pool):
        pool.wait_ge(self.tables, 32)
        for t in range(NT):
            i = t % 2
            pool.wait_ge(self.scaled, t + 1)
            pool.tensor_tensor(self.qk(t), self.qk(t), self.gain, ALU.mult).then_inc(self.gained, 1)
            pool.wait_ge(self.gained, t + 1)
            if t >= 2:
                pool.wait_ge(self.rotated, 2 * t - 2)
            for s in range(2):
                sin = self.rope[:, t, HD:2 * HD].rearrange("p (r s e) -> p r s e", r=2, s=2)[:, :, s, :]
                pool.tensor_tensor(self.parts(self.tmp2[:, i, :])[:, :, :, s, :], self.parts(self.qk(t))[:, :, :, 1 - s, :],
                                   spread(sin, 1, self.NH), ALU.mult).then_inc(self.sined, 1)
        pool.wait_ge(self.sined, 2 * NT)


def projection(nc, g, j, layer):
    BANKS = 6
    NC = (N_IN + PJ_W - 1) // PJ_W
    jobs = proj_jobs()
    groups = [(job, t) for t in range(NT) for job in jobs[0:2]]
    for job in jobs[2:]:
        groups += [(job, i) for i in range(2 if job[1] == "fm" else NT)]
    last_group = {}
    for n, (job, _) in enumerate(groups):
        last_group[job[0]] = n
    with ExitStack() as stack:
        a = Scope(nc, stack)
        h, w, w_loaded, norm = j.x, j.w, j.w_loaded, j.norm
        hT_hi, hT_lo = (a.sb("pj_hT" + n, [P, KD, T], F32R) for n in ("_hi", "_lo"))
        w_hi, w_lo = (a.sb("pj_w" + n, [P, PJ_HI, KD, PJ_W], F32R) for n in ("_hi", "_lo"))
        gain, shift = a.sb("pj_gain", [P, 2, D]), a.sb("pj_shift", [P, 2, D])
        norm.gain, norm.shift = gain, shift
        tp = a.ps("pj_tp", [P, 2, 4, P])
        ps = a.ps("pj_ps", [P, BANKS, 512])
        rows_loaded = [g.sem(f"pj_rows_loaded{s}") for s in range(2)]
        turned = g.sem("pj_turned")
        hi_ready, lo_ready = g.sem("pj_hT_hi_ready"), g.sem("pj_hT_lo_ready")
        w_hi_ready, w_lo_ready = g.sem("pj_w_hi_ready"), g.sem("pj_w_lo_ready")
        group_done = g.sem("pj_group_done")
        out_s = g.sem("pj_copied_scalar")
        out_v = g.sem("pj_copied_vector")
        rotary = Rotary(g, a, j.x)
        first = 3 * NT + 1
        norms, scales, rotations = 2 * NT, 2 * NT + 2, 3 * NT + 2

        def dest(n):
            (c, kind, off, width, place), i = groups[n]
            src = ps[:, n % BANKS, 0:(T // 2 if kind == "fm" else width)]
            if kind == "fm":
                return g.fm[:, place, i * (T // 2):(i + 1) * (T // 2)], src
            buf = {"qkv": g.qkv, "vb": g.vb, "vn": g.vn}[kind]
            return buf[:, i, place:place + width], src

        def width_of(c):
            return min(PJ_W, N_IN - c * PJ_W)

        with nc.Block(no_gpsimd_drain=True) as block:

            @block.sync
            def _(sync):
                for s in range(2):
                    load_mod_row(sync, g, gain, 1, s, rows_loaded[s])
                    load_mod_row(sync, g, shift, 0, s, rows_loaded[s])
                for c in range(PJ_RAW, NC):
                    sync.wait_ge(w_lo_ready, c - PJ_RAW + 1)
                    load_w_in(sync, g, j, layer, c)
                    if c == PJ_RAW + 2:
                        sync.wait_ge(group_done, 2 * NT)
                        rotary.load(sync, layer)

            @block.scalar
            def _(act):
                def high(c):
                    act.wait_ge(w_loaded[c % PJ_RAW], 16 * (c // PJ_RAW + 1))
                    if c >= PJ_HI:
                        act.wait_ge(group_done, last_group[c - PJ_HI] + 1)
                    act.activation(w_hi[:, c % PJ_HI, :, 0:width_of(c)], w[:, c % PJ_RAW, :, 0:width_of(c)],
                                   ACT.Copy).then_inc(w_hi_ready, 1)

                def copies(begin, end):
                    for n in range(begin, end):
                        if n % 2 == 0:
                            act.wait_ge(group_done, n + 1)
                            act.activation(*dest(n), ACT.Copy).then_inc(out_s, 1)
                        for c in range(PJ_HI, NC):
                            if last_group[c - PJ_HI] == n:
                                high(c)
                        if n == first + norms + 1:
                            rotary.sqrt(act)

                high(0)
                high(1)
                for n in range(2 * NT):
                    act.wait_ge(turned, n + 1)
                    t, half = n // 2, n % 2
                    act.activation(hT_hi[:, 4 * half:4 * half + 4, t * P:(t + 1) * P], tp[:, half, :, :],
                                   ACT.Copy).then_inc(hi_ready, 1)
                    if half:
                        copies(2 * max(t - 1, 0), 2 * t)
                copies(2 * NT - 2, len(groups))

            @block.vector
            def _(dve):
                def low(c):
                    dve.wait_ge(w_hi_ready, c + 1)
                    lo, raw = w_lo[:, c % PJ_HI, :, 0:width_of(c)], w[:, c % PJ_RAW, :, 0:width_of(c)]
                    dve.tensor_tensor(lo, raw, w_hi[:, c % PJ_HI, :, 0:width_of(c)].bitcast(F32),
                                      ALU.subtract).then_inc(w_lo_ready, 1)

                def rotary_step(n):
                    k = n - first
                    if k < 0 or k % 2:
                        return
                    if k == 0:
                        dve.wait_ge(out_s, 3 * NT // 2)
                    if k < norms:
                        rotary.sum_squares(dve, k // 2)
                    elif k == norms:
                        rotary.variance(dve)
                    elif k < rotations:
                        if k == scales:
                            rotary.inverse(dve)
                        for t in (k - scales, k - scales + 1):
                            rotary.scale(dve, t)
                    elif k < rotations + 2 * NT:
                        rotary.rotate(dve, (k - rotations) // 2)

                def copies(begin, end):
                    for n in range(begin, end):
                        if n % 2 == 1:
                            dve.wait_ge(group_done, n + 1)
                            dve.tensor_copy(*dest(n)).then_inc(out_v, 1)
                        for c in range(PJ_HI, NC):
                            if last_group[c - PJ_HI] == n:
                                low(c)
                        rotary_step(n)

                dve.wait_ge(rows_loaded[0], 32)
                norm.vector(dve, range(0, NTC))
                low(0)
                for n in range(2 * NT):
                    dve.wait_ge(hi_ready, n + 1)
                    t, half = n // 2, n % 2
                    blocks, cols = slice(4 * half, 4 * half + 4), slice(t * P, (t + 1) * P)
                    dve.tensor_tensor(hT_lo[:, blocks, cols], tp[:, half, :, :], hT_hi[:, blocks, cols].bitcast(F32),
                                      ALU.subtract).then_inc(lo_ready, 1)
                    if n == 1:
                        low(1)
                        dve.wait_ge(rows_loaded[1], 32)
                    if half:
                        norm.vector(dve, range(t + NTC, min(t + NTC + 1, NT)))
                        copies(2 * max(t - 1, 0), 2 * t)
                copies(2 * NT - 2, len(groups))

            @block.gpsimd
            def _(pool):
                norm.gpsimd(pool)
                rotary.gpsimd(pool)

            @block.tensor
            def _(pe):
                def turn(t):
                    pe.wait_ge(norm.shifted, t + 1)
                    for half in range(2):
                        if t:
                            pe.wait_ge(lo_ready, 2 * t - 1 + half)
                        for i in range(4):
                            k = 4 * half + i
                            mm = pe.transpose(tp[:, half, i, :], h[:, t, k * P:(k + 1) * P], g.ident)
                        mm.then_inc(turned, 1)

                def group(n):
                    (c, kind, off, width, place), i = groups[n]
                    pe.wait_ge(w_lo_ready, c + 1)
                    if n >= BANKS:
                        pe.wait_ge(out_s if n % 2 == 0 else out_v, (n - BANKS) // 2 + 1)
                    out = ps[:, n % BANKS, 0:(T // 2 if kind == "fm" else width)]
                    cols = slice(i * (T // 2), (i + 1) * (T // 2)) if kind == "fm" else slice(i * P, (i + 1) * P)
                    for k in range(KD):
                        whk = w_hi[:, c % PJ_HI, k, off:off + width]
                        wlk = w_lo[:, c % PJ_HI, k, off:off + width]
                        hhk, hlk = hT_hi[:, k, cols], hT_lo[:, k, cols]
                        for last, wk, hk in ((False, whk, hhk), (False, whk, hlk), (True, wlk, hhk)):
                            stationary, moving = (wk, hk) if kind == "fm" else (hk, wk)
                            mm = pe.matmul(out, stationary, moving, start=(wk is whk and hk is hhk and k == 0),
                                           stop=(last and k == KD - 1))
                    mm.then_inc(group_done, 1)

                turn(0)
                for t in range(NT):
                    if t + 1 < NT:
                        turn(t + 1)
                    pe.wait_ge(lo_ready, 2 * t + 2)
                    group(2 * t)
                    group(2 * t + 1)
                for n in range(2 * NT, len(groups)):
                    group(n)



N_ITEM = A_HEADS + C_HEADS
Q_BLOCKS = A_GROUP + 2


def attention_prepare(nc, g, b, layer):
    bias_loaded, turned, stored, keys_hi = (g.sem(n) for n in ("bias_loaded", "qk_turned", "qk_stored", "qk_keys_hi"))
    b.qk_ready, b.bias_ready = stored, bias_loaded

    def sync(sync):
        sync.dma_start(b.bias[:, :, :].rearrange("p h n -> p (h n)"), at(g.bias_d, layer)).then_inc(bias_loaded, 16)

    def tensor(pe):
        for t in range(NT):
            if t >= 2:
                pe.wait_ge(stored, t - 1)
            for j in range(5):
                mm = pe.transpose(b.prep_ps[:, t % 2, j, :], g.qkv[:, t, j * P:(j + 1) * P], g.ident)
            mm.then_inc(turned, 1)

    def scalar(act):
        act.activation(b.k_hi[:, 1:3, :], g.fm[:, 9:11, :], ACT.Copy).then_inc(keys_hi, 1)
        for t in range(NT):
            act.wait_ge(turned, t + 1)
            act.activation(b.qkT[:, :, t * P:(t + 1) * P], b.prep_ps[:, t % 2, :, :], ACT.Copy).then_inc(stored, 1)
        act.wait_ge(stored, NT)
        act.activation(b.k_hi[:, 0, :], b.qkT[:, A_GROUP, :], ACT.Copy).then_inc(keys_hi, 1)

    def vector(dve):
        dve.wait_ge(keys_hi, 1)
        dve.tensor_tensor(b.k_lo[:, 1:3, :], g.fm[:, 9:11, :], b.k_hi[:, 1:3, :].bitcast(F32), ALU.subtract)
        dve.wait_ge(keys_hi, 2)
        dve.tensor_tensor(b.k_lo[:, 0, :], b.qkT[:, A_GROUP, :], b.k_hi[:, 0, :].bitcast(F32), ALU.subtract)

    return sync, scalar, vector, tensor


def attend(nc, g, b, block, name, tiles, first, key_tiles, local_bias, when):
    TURN = 2
    items, groups = TURN * N_ITEM, TURN * N_ITEM // 4
    keys = key_tiles * P
    ka = (key_tiles + 1) // 2
    kb = key_tiles - ka
    staged, staged_lo = g.sem(name + "_staged"), g.sem(name + "_staged_lo")
    scored, maxed = g.sem(name + "_scored"), g.sem(name + "_maxed")
    link_sem = g.sem(name + "_dve_chain")
    exped, turned = g.sem(name + "_exped"), g.sem(name + "_turned")
    copied_a, copied_b = g.sem(name + "_copied_scalar"), g.sem(name + "_copied_vector")
    inverted, valued, rows_kept, normed = (g.sem(f"{name}_{n}") for n in ("inverted", "valued", "rows_kept", "normed"))

    def is_local(m):
        return local_bias and m % N_ITEM >= A_HEADS

    def head(m):
        n = m % N_ITEM
        if n < A_HEADS:
            v = n // A_GROUP
            return n % A_GROUP, v * HD, 0, lambda kt: g.qkv[:, kt, A_W + A_KVW + v * HD:A_W + A_KVW + (v + 1) * HD]
        h = n - A_HEADS
        return A_GROUP + h // 2, (h % 2) * HD, 1 + h // 2, lambda kt: g.vn[:, kt, h * HD:(h + 1) * HD]

    @block.tensor
    def _(pe):
        with when(pe):
            pe.sem_inc(normed, 4)
            with pe.Fori(0, tiles // TURN) as i:
                def scores(m):
                    q, part, kblk, _ = head(m)
                    rows = slice(part, part + HD)
                    for c in range(0, keys, 512):
                        cols = slice(c, min(c + 512, keys))
                        for n, (qs, ks) in enumerate(((b.q_hi, b.k_hi), (b.q_lo, b.k_hi), (b.q_hi, b.k_lo))):
                            mm = pe.matmul(b.sc_ps[:, m % 2, cols], qs[rows, m // N_ITEM, q, :], ks[rows, kblk, cols],
                                           start=(n == 0), stop=(n == 2))
                    mm.then_inc(scored, 1)

                def turns(m):
                    pe.wait_ge(exped, i * items + m + 1)
                    for kt in range(key_tiles):
                        if kt == 0 and m > 0:
                            pe.wait_ge(copied_a, i * items + m)
                        if kt == ka and m > 0:
                            pe.wait_ge(copied_b, i * items + m)
                        half, j = (0, kt) if kt < ka else (1, kt - ka)
                        mm = pe.transpose(b.pt_ps[:, half, j, :], b.e[:, m % 2, kt * P:(kt + 1) * P], g.ident)
                        if kt in (ka - 1, key_tiles - 1):
                            mm.then_inc(turned, 1)

                def values(m):
                    pe.wait_ge(copied_a, i * items + m + 1)
                    pe.wait_ge(copied_b, i * items + m + 1)
                    if m % 4 == 0:
                        pe.wait_ge(normed, (i * groups + m // 4) * 2 + 2)
                    for kt in range(key_tiles):
                        pe.matmul(b.o_ps[0:HD, m // 4 % 2, m % 4, :], head(m)[3](kt), b.pT[:, m % 2, kt, :],
                                  start=(kt == 0), stop=(kt == key_tiles - 1))
                    pe.wait_ge(inverted, i * items + m + 1)
                    mm = pe.matmul(b.o_ps[HD:P, m // 4 % 2, m % 4, :], b.inv[:, m:m + 1].to_broadcast([P, HD]), g.ident,
                                   start=True, stop=True)
                    if m % 4 == 3:
                        mm.then_inc(valued, 1)

                pe.wait_ge(staged_lo, i * 2 * TURN + 2)
                scores(0)
                scores(1)
                for m in range(items):
                    turns(m)
                    if m >= 1:
                        values(m - 1)
                    if m + 2 == N_ITEM:
                        pe.wait_ge(staged_lo, i * 2 * TURN + 4)
                    if m + 2 < items:
                        scores(m + 2)
                values(items - 1)

    @block.scalar
    def _(act):
        with when(act):
            act.wait_ge(b.qk_ready, NT)
            with act.Fori(0, tiles // TURN) as i:
                def exp(m):
                    act.wait_ge(maxed, i * items + m + 1)
                    src, scale = (b.s[:, m % 2, 0:keys], 1.0) if is_local(m) else (b.sc_ps[:, m % 2, 0:keys], SCALE)
                    act.activation(b.e[:, m % 2, 0:keys], src, ACT.Exp, bias=b.negmax[:, m:m + 1], scale=scale,
                                   accum_out=b.total[:, m:m + 1]).then_inc(exped, 1)

                def keep_rows(k):
                    act.wait_ge(valued, i * groups + k + 1)
                    act.activation(b.inv_rows[:, k % 2, :, :], b.o_ps[HD:P, k % 2, :, :], ACT.Copy).then_inc(rows_kept, 1)

                def stage(u):
                    col = (i * TURN + first + u) * P
                    act.activation(b.q_hi[:, u, 0:A_GROUP, :], b.qkT[:, 0:A_GROUP, ds(col, P)], ACT.Copy).then_inc(staged, 1)
                    act.activation(b.q_hi[:, u, A_GROUP:, :], g.fm[:, 7:9, ds(col, P)], ACT.Copy).then_inc(staged, 1)

                stage(0)
                exp(0)
                stage(1)
                for m in range(items):
                    act.wait_ge(turned, i * 2 * items + 2 * m + 1)
                    act.activation(b.pT[:, m % 2, 0:ka, :], b.pt_ps[:, 0, 0:ka, :], ACT.Copy).then_inc(copied_a, 1)
                    if m + 1 < items:
                        exp(m + 1)
                    if m >= 4 and m % 4 == 0:
                        keep_rows(m // 4 - 1)
                keep_rows(groups - 1)

    @block.vector
    def _(dve):
        with when(dve):
            n_local = TURN * C_HEADS if local_bias else 0
            per = (items - n_local) + 3 * n_local
            if local_bias:
                dve.wait_ge(b.bias_ready, 16)
            with dve.Fori(0, tiles // TURN) as i:
                link = Link(dve, link_sem, i * per)

                def maximum(m):
                    dve.wait_ge(scored, i * items + m + 1)
                    if not is_local(m):
                        link(dve.tensor_reduce(b.mx[:, m:m + 1], b.sc_ps[:, m % 2, 0:keys], AX_X, ALU.max))
                        scale = -SCALE
                    else:
                        tile = i * TURN + m // N_ITEM
                        dve.scalar_tensor_tensor(b.s[:, m % 2, CTX:keys], b.sc_ps[:, m % 2, CTX:keys], SCALE,
                                                 b.bias[:, m % N_ITEM - A_HEADS,
                                                        ds((RPB_M - WIN_ROWS) * GRID - tile * 2 * GRID, WIN_ROWS * GRID)],
                                                 ALU.mult, ALU.add).then_inc(link_sem, 1)
                        link.n += 1
                        link(dve.tensor_scalar(b.s[:, m % 2, 0:CTX], b.sc_ps[:, m % 2, 0:CTX], SCALE, None, ALU.mult))
                        link(dve.tensor_reduce(b.mx[:, m:m + 1], b.s[:, m % 2, 0:keys], AX_X, ALU.max))
                        scale = -1.0
                    dve.tensor_scalar(b.negmax[:, m:m + 1], b.mx[:, m:m + 1], scale, None, ALU.mult).then_inc(maxed, 1)

                def normalise(k):
                    tile, blk = i * TURN + first + k * 4 // N_ITEM, (0, 2, 6)[k % (N_ITEM // 4)]
                    dve.wait_ge(rows_kept, i * groups + k + 1)
                    for par in range(2):
                        dve.tensor_tensor(g.mixT[par * HD:par * HD + HD, blk:blk + 2, ds(tile * P, P)],
                                          b.o_ps[0:HD, k % 2, par:4:2, :], b.inv_rows[:, k % 2, par:4:2, :],
                                          ALU.mult).then_inc(normed, 1)

                def stage(u):
                    col = (i * TURN + first + u) * P
                    for n, (blocks, src) in enumerate(((slice(0, A_GROUP), b.qkT[:, 0:A_GROUP, ds(col, P)]),
                                                       (slice(A_GROUP, Q_BLOCKS), g.fm[:, 7:9, ds(col, P)]))):
                        dve.wait_ge(staged, i * 2 * TURN + 2 * u + n + 1)
                        dve.tensor_tensor(b.q_lo[:, u, blocks, :], src, b.q_hi[:, u, blocks, :].bitcast(F32),
                                          ALU.subtract).then_inc(staged_lo, 1)

                stage(0)
                maximum(0)
                stage(1)
                for m in range(items):
                    if m + 1 < items:
                        maximum(m + 1)
                    dve.wait_ge(turned, i * 2 * items + 2 * m + 2)
                    dve.tensor_copy(b.pT[:, m % 2, ka:key_tiles, :], b.pt_ps[:, 1, 0:kb, :]).then_inc(copied_b, 1)
                    dve.reciprocal(b.inv[:, m:m + 1], b.total[:, m:m + 1]).then_inc(inverted, 1)
                    if m >= 5 and m % 4 == 1:
                        normalise(m // 4 - 1)
                normalise(groups - 1)
                assert link.n == per, (link.n, per)


class Buffers:
    pass


def attention(nc, g, layer):
    with ExitStack() as stack:
        a, b = Scope(nc, stack), Buffers()
        b.bias = a.sb("at_bias", [P, C_HEADS, RPB_M * GRID])
        b.qkT = a.sb("at_qkT", [P, A_GROUP + 1, T])
        b.k_hi, b.k_lo = (a.sb("at_k" + n, [P, 3, T], F32R) for n in ("_hi", "_lo"))
        with ExitStack() as first:
            f = Scope(nc, first)
            b.prep_ps = f.ps("at_prep_ps", [P, 2, 8, P])[:, :, 0:5, :]
            sync, scalar, vector, tensor = attention_prepare(nc, g, b, layer)
            with nc.Block(no_gpsimd_drain=True) as block:
                block.sync(sync)
                block.scalar(scalar)
                block.vector(vector)
                block.tensor(tensor)
        b.q_hi, b.q_lo = (a.sb("at_q" + n, [P, 2, Q_BLOCKS, P], F32R) for n in ("_hi", "_lo"))
        b.e = a.sb("at_e", [P, 2, T])
        b.s = a.sb("at_s", [P, 2, T])
        b.pT = a.sb("at_pT", [P, 2, NT, P])
        b.mx, b.negmax = (a.sb("at_" + n, [P, 2 * N_ITEM]) for n in ("mx", "negmax"))
        b.total, b.inv = (a.sb("at_" + n, [P, 2 * N_ITEM]) for n in ("total", "inv"))
        b.inv_rows = a.sb("at_inv_rows", [HD, 2, 4, P])
        b.sc_ps = a.ps("at_sc_ps", [P, 2, 1024])
        b.pt_ps = a.ps("at_pt_ps", [P, 2, 4, P])
        b.o_ps = a.ps("at_o_ps", [P, 2, 4, P])
        with nc.Block(no_gpsimd_drain=True) as block:
            attend(nc, g, b, block, "lat", NT - NTC, NTC, NT, True, lambda eng: nullcontext())
        with nc.Block(no_gpsimd_drain=True) as block:
            attend(nc, g, b, block, "ctx", NTC, 0, NTC, False, lambda eng: eng.If(layer < DEPTH - 1))



HALF = T // 2


def rwkv_gates(nc, g, r, layer):
    fm = g.fm
    rT, kT, wl, al, gl = fm[:, 0:2, :], fm[:, 2:4, :], fm[:, 4, :], fm[:, 5, :], fm[:, 6, :]
    with ExitStack() as stack:
        a = Scope(nc, stack)
        tmp, tmp2 = a.sb("rg_tmp", [P, 2, T]), a.sb("rg_tmp2", [P, 2, T])
        restart = a.sb("rg_restart", [P, T])
        cols, wu, au = a.sb("rg_cols", [P, N_COL]), a.sb("rg_wu", [P, B_W]), a.sb("rg_au", [P, B_W])
        z = a.ps("rg_z", [P, 4, 512])
        ns = a.ps("rg_ns", [P, 2, 2, 512])
        bon = z[:, 0, 0:NT * B_HEADS].rearrange("p (t h) -> p t h", h=B_HEADS)
        loaded, acted, looked, gated = g.sem("rg_loaded"), g.sem("rg_acted"), g.sem("rg_looked"), g.sem("rg_gated")
        squared, summed, rooted, chain = g.sem("rg_squared"), g.sem("rg_summed"), g.sem("rg_rooted"), g.sem("rg_chain")
        bonus_in, bonus_out = g.sem("rg_bonus_in"), g.sem("rg_bonus_out")
        scanned, excluded = g.sem("rg_scanned"), g.sem("rg_excluded")
        NORM_AT = 4
        with nc.Block(no_gpsimd_drain=True) as block:

            @block.sync
            def _(sync):
                sync.dma_start(cols[:, :], at(g.cols_d, layer)).then_inc(loaded, 16)
                sync.dma_start(wu[:, :], at(g.w_up, layer)).then_inc(loaded, 16)
                sync.dma_start(au[:, :], at(g.a_up, layer)).then_inc(loaded, 16)

            @block.scalar
            def _(act):
                act.activation(wl, wl, ACT.Tanh).then_inc(acted, 1)
                act.activation(gl, gl, ACT.Sigmoid).then_inc(acted, 1)
                act.wait_ge(loaded, 48)
                for n in range(16):
                    if n == NORM_AT:
                        act.wait_ge(summed, 1)
                        act.activation(tmp2[:, :, :].rearrange("p b (h n) -> p b h n", h=2), ns[:, :, :, 0:HALF],
                                       ACT.Sqrt).then_inc(rooted, 1)
                    d, blk, half = (n % 8) // 4, (n % 4) // 2, n % 2
                    dst, col = (r.xc, C_W0) if n < 8 else (r.b, C_A0)
                    act.wait_ge(looked, n + 1)
                    act.activation(dst[:, 2 * d + blk, half * HALF:(half + 1) * HALF], z[:, n % 4, 0:HALF], ACT.Sigmoid,
                                   bias=cols[:, col + 2 * d + blk:col + 2 * d + blk + 1]).then_inc(gated, 1)

            @block.tensor
            def _(pe):
                pe.wait_ge(loaded, 48)
                pe.wait_ge(acted, 1)
                for n in range(16):
                    if n == NORM_AT:
                        pe.wait_ge(squared, 1)
                        for blk in range(2):
                            for half in range(2):
                                mm = pe.matmul(ns[:, blk, half, 0:HALF], g.cst[:, O_HB:O_HB + P],
                                               tmp[:, blk, half * HALF:(half + 1) * HALF], start=True, stop=True)
                        mm.then_inc(summed, 1)
                    d, blk, half = (n % 8) // 4, (n % 4) // 2, n % 2
                    wt, src = (wu, wl) if n < 8 else (au, al)
                    if n >= 4:
                        pe.wait_ge(gated, n - 3)
                    pe.matmul(z[:, n % 4, 0:HALF], wt[d * 64:d * 64 + 64, blk * P:(blk + 1) * P],
                              src[d * 64:d * 64 + 64, half * HALF:(half + 1) * HALF], start=True, stop=True).then_inc(looked, 1)
                pe.wait_ge(bonus_in, 2)
                for t in range(NT):
                    for blk in range(2):
                        mm = pe.matmul(bon[:, t, 2 * blk:2 * blk + 2], tmp[:, blk, t * P:(t + 1) * P],
                                       g.cst[:, O_HS:O_HS + 2], start=True, stop=True)
                mm.then_inc(bonus_out, 1)

            @block.vector
            def _(dve):
                link = Link(dve, chain)
                dve.wait_ge(loaded, 48)
                for blk in range(2):
                    link(dve.tensor_scalar(r.nkk[:, blk, :], kT[:, blk, :], cols[:, C_KK + blk:C_KK + blk + 1], None, ALU.mult))
                dve.tensor_tensor(tmp[:, :, :], r.nkk[:, :, :], r.nkk[:, :, :], ALU.mult).then_inc(squared, 1)
                link(dve.memset(restart[:, :], 1.0))
                link(dve.memset(restart[:, 0:T:CH], 0.0))
                dve.wait_ge(rooted, 1)
                link(dve.tensor_scalar(tmp2[:, :, :], tmp2[:, :, :], 1e-12, None, ALU.max))
                link(dve.reciprocal(tmp2[:, :, :], tmp2[:, :, :]))
                link(dve.scalar_tensor_tensor(r.nkk[:, :, :], r.nkk[:, :, :], -1.0, tmp2[:, :, :], ALU.mult, ALU.mult))
                dve.wait_ge(gated, 8)
                for db in range(4):
                    way = slice(None) if db < 2 else slice(None, None, -1)
                    dve.tensor_tensor_scan(r.cs[:, db, way], restart[:, :], r.xc[:, db, way], 0.0, ALU.mult,
                                           ALU.add).then_inc(scanned, 1)
                dve.wait_ge(gated, 16)
                for db in range(4):
                    blk = db % 2
                    link(dve.tensor_scalar(r.kd[:, db, :], r.b[:, db, :], 1.0, cols[:, C_KA + blk:C_KA + blk + 1],
                                           ALU.subtract, ALU.mult))
                for d in range(2):
                    link(dve.scalar_tensor_tensor(r.kd[:, 2 * d:2 * d + 2, :], r.kd[:, 2 * d:2 * d + 2, :], 1.0, kT,
                                                  ALU.add, ALU.mult))
                link(dve.tensor_tensor(tmp[:, :, :], r.kd[:, 0:2, :], r.kd[:, 2:4, :], ALU.add))
                for blk in range(2):
                    dve.scalar_tensor_tensor(tmp[:, blk, :], tmp[:, blk, :], cols[:, C_RK + blk:C_RK + blk + 1],
                                             rT[:, blk, :], ALU.mult, ALU.mult).then_inc(bonus_in, 1)
                for d in range(2):
                    link(dve.scalar_tensor_tensor(r.b[:, 2 * d:2 * d + 2, :], r.b[:, 2 * d:2 * d + 2, :], -1.0, r.nkk[:, :, :],
                                                  ALU.mult, ALU.mult))
                dve.wait_ge(bonus_out, 1)
                dve.tensor_copy(r.bonus[:, :, :], bon)

            @block.gpsimd
            def _(pool):
                for db in range(4):
                    pool.wait_ge(scanned, db + 1)
                    pool.tensor_tensor(r.xc[:, db, :], r.cs[:, db, :], r.xc[:, db, :], ALU.subtract).then_inc(excluded, 1)
                pool.wait_ge(excluded, 4)


def rwkv_chunks(nc, g, r, layer):
    with ExitStack() as stack:
        a = Scope(nc, stack)
        e = a.sb("rc_e", [P, 3, 4, P])
        bh, kh = e[:, 0, :, :], e[:, 1, :, :]
        wend = a.sb("rc_wend", [P, 8])
        ar = a.sb("rc_ar", [P, 2, 4, P])
        bt, kt = a.sb("rc_bt", [P, 4, P]), a.sb("rc_kt", [P, 4, P])
        vt = a.sb("rc_vt", [P, B_W])
        ag = a.sb("rc_ag", [P, 8, 2, CH])
        bht, kht = a.sb("rc_bht", [P, 8, CH]), a.sb("rc_kht", [P, 8, CH])
        lb, lk = a.sb("rc_lb", [P, 8, 2 * CH]), a.sb("rc_lk", [P, 8, 2 * CH])
        nl = a.sb("rc_nl", [P, 5, 8, CH])
        tu = a.sb("rc_tu", [P, 2, 2, 4, CH])
        y = a.sb("rc_y", [P, 8, CH])
        tag = a.sb("rc_tag", [P, 8, 2 * CH])
        mk = a.sb("rc_mk", [P, 2, 2 * CH])
        m0 = a.sb("rc_m0", [P, 2, CH])
        ps = a.ps("rc_ps", [P, 8, 512])
        names = ("masks", "decays", "tildes", "hats", "v_staged", "products", "turned", "turned_kept", "masked",
                 "levels", "y_made", "y_kept", "step_made", "inverse", "g0_made", "g0_kept", "tag_made",
                 "tag_kept_v", "tag_kept_s", "results", "kept_v", "kept_s", "passed")
        s = Buffers()
        (s.masks, s.decays, s.tildes, s.hats, s.v_staged, s.products, s.turned, s.turned_kept, s.masked,
         s.levels, s.y_made, s.y_kept, s.step_made, s.inverse, s.g0_made, s.g0_kept, s.tag_made,
         s.tag_kept_v, s.tag_kept_s, s.results, s.kept_v, s.kept_s, s.passed) = (g.sem("rc_" + n) for n in names)
        lm = [g.cst[:, O_LM + 64 * lv:O_LM + 64 * lv + 64] for lv in range(6)]
        tri = [g.cst[:, O_TRI + 64 * i:O_TRI + 64 * i + 64] for i in range(4)]
        i64 = g.cst[:, O_I64:O_I64 + CH]
        units = [(par, db, ck) for par in range(2) for db in range(4) for ck in range(2)]
        half = [slice(0, 64), slice(64, 128)]

        def value(par, db):
            h = (db % 2) * 2 + par
            return slice(h * HD, h * HD + HD)

        def by_ck(v, col):
            return v[:, :, ds(col, P)].rearrange("p b (c n) -> p b c n", c=2)

        def from_ck(bank, c):
            return ps[:, bank:bank + 2, c:c + 256].rearrange("p c (b n) -> p b c n", b=4)

        def by_db(v, groups=4):
            return v.rearrange("p (b n) -> p b n", b=groups)

        def tiles(eng, body):
            with eng.Fori(0, NT - 1) as i:
                body(i, False)
            body(NT - 1, True)

        with nc.Block(no_gpsimd_drain=True) as block:

            @block.scalar
            def _(act):
                def decays(i, n):
                    src, scale = ((r.cs, KAPPA), (r.xc, KAPPA), (r.cs, -KAPPA))[n]
                    act.activation(e[:, n, :, :], src[:, :, ds(i * P, P)], ACT.Exp, scale=scale).then_inc(s.decays, 1)

                def body(i, last):
                    col = i * P
                    for n, (dst, bank) in enumerate(((ag[:, :, 0, :], 6), (bht[:, :, :], 7), (kht[:, :, :], 6))):
                        act.wait_ge(s.turned, i * 3 + n + 1)
                        act.activation(dst, by_db(ps[:, bank, :], 8), ACT.Copy).then_inc(s.turned_kept, 1)
                    act.wait_ge(s.g0_made, i + 1)
                    act.activation(ag[:, :, 1, :], ps[:, 7, :].rearrange("p (u n) -> p u n", u=8), ACT.Copy).then_inc(s.g0_kept, 1)
                    for lv in range(5):
                        for d in range(2):
                            act.wait_ge(s.y_made, i * 10 + lv * 2 + d + 1)
                            act.activation(y[:, d:8:2, :], by_db(ps[:, 4 + d, 0:256]),
                                           ACT.Copy).then_inc(s.y_kept, 1)
                        if lv < 3 and not last:
                            decays(i + 1, lv)
                    act.wait_ge(s.tag_made, i * 2 + 2)
                    act.activation(tag[:, 1:8:2, :], by_db(ps[:, 3, :]), ACT.Copy).then_inc(s.tag_kept_s, 1)
                    act.wait_ge(s.results, i * 4 + 3)
                    act.activation(r.yl[:, ds(i, 1), :].squeeze(1), ps[:, 2, 0:256], ACT.Copy).then_inc(s.kept_s, 1)
                    act.wait_ge(s.results, i * 4 + 4)
                    act.activation(by_ck(r.hh, col), from_ck(5, 0), ACT.Copy).then_inc(s.kept_s, 1)

                for n in range(3):
                    decays(0, n)
                tiles(act, body)

            @block.vector
            def _(dve):
                for d in range(2):
                    strict, incl, other = (TRI_LT, TRI_LE, TRI_GT) if d == 0 else (TRI_GT, TRI_GE, TRI_LT)
                    dve.tensor_copy(mk[:, d, 0:CH], tri[strict]).then_inc(s.masks, 1)
                    dve.tensor_copy(mk[:, d, CH:], tri[incl]).then_inc(s.masks, 1)
                    dve.tensor_tensor(m0[:, d, :], tri[other], lm[0], ALU.mult).then_inc(s.masks, 1)
                dve.wait_ge(s.masks, 6)

                def tildes_1(i):
                    dve.wait_ge(s.decays, i * 3 + 3)
                    dve.tensor_copy(wend[:, 0:4].rearrange("p (b c) -> p b c", b=2), e[:, 0, 0:2, CH - 1:P:CH]).then_inc(s.tildes, 1)
                    dve.tensor_copy(wend[:, 4:8].rearrange("p (b c) -> p b c", b=2), e[:, 0, 2:4, 0:P:CH]).then_inc(s.tildes, 1)
                    for d in range(2):
                        for n, (decay, src) in enumerate(((1, r.nkk), (0, g.fm[:, 0:2, :]))):
                            dve.tensor_tensor(ar[:, n, 2 * d:2 * d + 2, :], e[:, decay, 2 * d:2 * d + 2, :],
                                              src[:, :, ds(i * P, P)], ALU.mult).then_inc(s.tildes, 1)

                def tildes_2(i):
                    dve.tensor_tensor(bt[:, :, :], e[:, 2, :, :], r.b[:, :, ds(i * P, P)], ALU.mult).then_inc(s.tildes, 1)
                    dve.tensor_tensor(kt[:, :, :], e[:, 2, :, :], r.kd[:, :, ds(i * P, P)], ALU.mult).then_inc(s.tildes, 1)

                def body(i, last):
                    col = i * P
                    for par in range(2):
                        dve.wait_ge(s.products, i * 2 + par + 1)

                        def by_d(v):
                            return v.rearrange("p (d b) n -> p d b n", d=2)

                        for dst, bank in ((lb, par), (lk, 2 + par)):
                            dve.tensor_tensor(by_d(dst[:, par:8:2, :]), by_d(by_db(ps[:, bank, :])),
                                              spread(mk[:, :, :], 2, 2), ALU.mult).then_inc(s.masked, 1)
                        dve.tensor_tensor(by_d(tu[:, par, 0, :, :]), by_d(by_db(ps[:, 4 + par, 0:256])),
                                          spread(m0[:, :, :], 2, 2), ALU.mult).then_inc(s.masked, 1)
                        dve.wait_ge(s.masked, i * 8 + par * 4 + 3)
                        dve.tensor_tensor(tu[:, par, 1, :, :], lb[:, par:8:2, 0:CH], spread(lm[0], 1, 4), ALU.mult).then_inc(s.masked, 1)
                        dve.wait_ge(s.masked, i * 8 + par * 4 + 4)
                        tud = tu[:, par, :, :, :].rearrange("p a h n -> p (a h) n")
                        dve.tensor_tensor(tud, tud, spread(i64, 1, 8), ALU.add).then_inc(s.inverse, 1)
                    for lv in range(5):
                        for d in range(2):
                            n = lv * 2 + d
                            dve.wait_ge(s.step_made, i * 10 + n + 1)
                            dve.wait_ge(s.inverse, i * 12 + n + 1)
                            if lv < 4:
                                dst, src = tu[:, d, :, :, :].rearrange("p a h n -> p (a h n)"), ps[:, d, :]
                            else:
                                dst, src = tu[:, d, 1, :, :].rearrange("p h n -> p (h n)"), ps[:, d, 256:512]
                            dve.tensor_tensor(dst, dst, src, ALU.add).then_inc(s.inverse, 1)
                        if lv == 2 and not last:
                            dve.wait_ge(s.hats, i * 4 + 4)
                            tildes_1(i + 1)
                        if lv == 3 and not last:
                            tildes_2(i + 1)
                    dve.wait_ge(s.tag_made, i * 2 + 1)
                    dve.tensor_copy(tag[:, 0:8:2, :], by_db(ps[:, 2, :])).then_inc(s.tag_kept_v, 1)
                    dve.wait_ge(s.results, i * 4 + 2)
                    dve.wait_ge(s.hats, i * 4 + 4)
                    dve.tensor_tensor(by_ck(r.pt, col), by_ck(r.pt, col), from_ck(0, 0), ALU.add).then_inc(s.kept_v, 1)
                    dve.tensor_tensor(by_ck(r.mt, col), by_ck(r.mt, col), from_ck(0, 256), ALU.add).then_inc(s.kept_v, 1)

                tildes_1(0)
                tildes_2(0)
                tiles(dve, body)

            @block.gpsimd
            def _(pool):
                def stage_v(i):
                    pool.tensor_copy(vt[:, :], g.vb[:, ds(i, 1), :].squeeze(1)).then_inc(s.v_staged, 1)

                def body(i, last):
                    pool.wait_ge(s.tildes, i * 8 + 8)
                    w8 = spread(wend[:, :], 2, CH)
                    for dst, src in ((bh, bt), (kh, kt)):
                        pool.tensor_tensor(dst.rearrange("p b (c n) -> p (b c) n", c=2),
                                           src[:, :, :].rearrange("p b (c n) -> p (b c) n", c=2), w8, ALU.mult).then_inc(s.hats, 1)
                    pool.tensor_tensor(by_ck(r.mt, i * P), spread(spread(i64, 1, 2), 1, 4),
                                       spread(wend[:, :].rearrange("p (b c) -> p b c", c=2), 3, CH), ALU.mult).then_inc(s.hats, 1)
                    pool.tensor_copy(r.pt[:, :, ds(i * P, P)], ar[:, 1, :, :]).then_inc(s.hats, 1)
                    for d in range(2):
                        pool.wait_ge(s.masked, i * 8 + d * 4 + 1)
                        for lv in range(5):
                            pool.tensor_tensor(nl[:, lv, d:8:2, :], lb[:, d:8:2, 0:CH],
                                               spread(lm[lv + 1], 1, 4), ALU.mult).then_inc(s.levels, 1)
                    if not last:
                        pool.wait_ge(s.results, i * 4 + 4)
                        stage_v(i + 1)

                stage_v(0)
                tiles(pool, body)

            @block.tensor
            def _(pe):
                def pe_wait(sem, value):
                    pe.wait_ge(sem, value)
                    pe.sem_inc(s.passed, 1)

                def body(i, last):
                    pe_wait(s.tildes, i * 8 + 8)
                    for par in range(2):
                        ch = half[par]
                        for db in range(4):
                            for ck in range(2):
                                st, steps = half[ck], slice(ck * CH, ck * CH + CH)
                                for bank, lhs in ((par, bt), (2 + par, kt)):
                                    pe.matmul(ps[st, bank, db * 128:db * 128 + 128].rearrange("p (a n) -> p a n", a=2),
                                              lhs[ch, db, steps], ar[ch, :, db, steps], start=True, stop=True)
                                mm = pe.matmul(ps[st, 4 + par, db * CH:db * CH + CH], ar[ch, 0, db, steps], bt[ch, db, steps],
                                               start=True, stop=True)
                        mm.then_inc(s.products, 1)
                    for n, (src, bank) in enumerate(((ar[:, 0, :, :], 6), (bh, 7), (kh, 6))):
                        if n:
                            pe_wait(s.hats, i * 4 + n)
                        if n == 2:
                            pe_wait(s.turned_kept, i * 3 + 1)
                        for db in range(4):
                            mm = pe.transpose(ps[:, bank, db * P:db * P + P], src[:, db, :], g.ident)
                        mm.then_inc(s.turned, 1)
                    pe_wait(s.turned_kept, i * 3 + 3)
                    pe_wait(s.masked, i * 8 + 7)
                    pe_wait(s.v_staged, i + 1)
                    for par, db, ck in units:
                        st, u = half[ck], 2 * db + par
                        mm = pe.matmul(ps[st, 7, u * CH:u * CH + CH], lk[st, u, 0:CH], vt[st, value(par, db)], start=True, stop=True)
                    mm.then_inc(s.g0_made, 1)
                    for lv in range(5):
                        for par in range(2):
                            pe_wait(s.levels, i * 10 + par * 5 + lv + 1)
                            pe_wait(s.inverse, i * 12 + lv * 2 + par + 1)
                            for db in range(4):
                                for st in half:
                                    mm = pe.matmul(ps[st, 4 + par, db * CH:db * CH + CH], nl[st, lv, 2 * db + par, :],
                                                   tu[st, par, 0, db, :], start=True, stop=True)
                            mm.then_inc(s.y_made, 1)
                        for par in range(2):
                            pe_wait(s.y_kept, i * 10 + lv * 2 + par + 1)
                            for db in range(4):
                                for st in half:
                                    t_, y_, c = tu[st, par, 1, db, :], y[st, 2 * db + par, :], db * CH
                                    if lv < 4:
                                        pe.matmul(ps[st, par, c:c + CH], t_, y_, start=True, stop=True)
                                    mm = pe.matmul(ps[st, par, 256 + c:256 + c + CH], y_, t_, start=True, stop=True)
                            mm.then_inc(s.step_made, 1)
                    pe_wait(s.g0_kept, i + 1)
                    for par in range(2):
                        pe_wait(s.inverse, i * 12 + 11 + par)
                        for db in range(4):
                            for st in half:
                                mm = pe.matmul(ps[st, 2 + par, db * 128:db * 128 + 128], tu[st, par, 1, db, :],
                                               ag[st, 2 * db + par, :, :].rearrange("p a n -> p (a n)"), start=True, stop=True)
                        mm.then_inc(s.tag_made, 1)
                    pe_wait(s.tag_kept_v, i + 1)
                    pe_wait(s.tag_kept_s, i + 1)
                    for base, rhs in ((0, lambda st, u: lb[st, u, CH:]), (256, lambda st, u: bht[st, u, :])):
                        for par, db, ck in units:
                            u, st, ch, c = 2 * db + par, half[ck], half[par], base + db * CH
                            mm = pe.matmul(ps[ch, ck, c:c + CH], tag[st, u, 0:CH], rhs(st, u), start=True, stop=True)
                        mm.then_inc(s.results, 1)
                    for h in range(4):
                        for st in half:
                            for d in range(2):
                                u, o = d * 4 + h, ps[st, 2, h * HD:h * HD + HD]
                                pe.matmul(o, lb[st, u, CH:], tag[st, u, CH:], start=(d == 0), stop=False)
                                mm = pe.matmul(o, lk[st, u, CH:], vt[st, h * HD:h * HD + HD], start=False, stop=(d == 1))
                    mm.then_inc(s.results, 1)
                    for par, db, ck in units:
                        u, st, ch = 2 * db + par, half[ck], half[par]
                        o = ps[ch, 5 + ck, db * CH:db * CH + CH]
                        pe.matmul(o, bht[st, u, :], tag[st, u, CH:], start=True, stop=False)
                        mm = pe.matmul(o, kht[st, u, :], vt[st, value(par, db)], start=False, stop=True)
                    mm.then_inc(s.results, 1)
                    if not last:
                        pe_wait(s.kept_v, i * 2 + 2)
                        pe_wait(s.kept_s, i * 2 + 2)

                tiles(pe, body)


def rwkv_readout(nc, g, r, layer):
    order = [list(range(NCH)), list(range(NCC - 1, -1, -1)) + list(range(NCH - 1, NCC - 1, -1))]
    with ExitStack() as stack:
        a = Scope(nc, stack)
        xs = a.sb("ro_xs", [P, 4, NCH, CH])
        gate = a.sb("ro_gate", [P, NT, B_W])
        gup, ln = a.sb("ro_gup", [P, B_W]), a.sb("ro_ln", [P, 2, B_W])
        tmp = a.sb("ro_tmp", [P, NT * B_HEADS, HD])
        st = a.sb("ro_st", [P, 4, NT * B_HEADS])
        sps = a.ps("ro_sps", [P, 2, B_W])
        yps = a.ps("ro_yps", [P, 2, 2, 512])
        gps = a.ps("ro_gps", [P, 2, 512])
        tps = gps
        loaded, zeroed, moved, stepped = g.sem("ro_loaded"), g.sem("ro_zeroed"), g.sem("ro_moved"), g.sem("ro_stepped")
        read, added, gated, gate_kept = g.sem("ro_read"), g.sem("ro_added"), g.sem("ro_gated"), g.sem("ro_gate_kept")
        chain, var, root, done = g.sem("ro_chain"), g.sem("ro_var"), g.sem("ro_root"), g.sem("ro_done")
        folds, turned, kept = g.sem("ro_folds"), g.sem("ro_turned"), g.sem("ro_kept")
        mo_rows_loaded = g.sem("mo_gate_loaded")
        yh = r.yl[:, :, :].rearrange("p t (h n) -> p (t h) n", h=B_HEADS)
        yf = r.yl[:, :, :]
        with nc.Block(no_gpsimd_drain=True) as block:

            @block.sync
            def _(sync):
                sync.dma_start(gup[:, :], at(g.g_up, layer)).then_inc(loaded, 16)
                sync.dma_start(ln[:, :, :].rearrange("p a n -> p (a n)"),
                               at(g.rows_d, layer)[R_LNW:R_LNW + 2 * B_W].partition_broadcast(P)).then_inc(loaded, 16)
                load_mod_rows(sync, g, g.mo_gate, 2, mo_rows_loaded)
                sync.dma_start(g.w_out_sb[:, :, :], at(g.w_out, layer).rearrange("(k p) n -> p k n", p=P)).then_inc(g.w_out_loaded, 16)
                sync.wait_ge(mo_rows_loaded, 32)

            @block.tensor
            def _(pe):
                pe.wait_ge(zeroed, 2)
                for n in range(NCH - 1):
                    if n:
                        pe.wait_ge(stepped, 2 * n)
                    for d in range(2):
                        c = order[d][n]
                        for blk in range(2):
                            for par in (0, 64):
                                ch, db = slice(par, par + 64), 2 * d + blk
                                mm = pe.matmul(sps[ch, n % 2, db * CH:db * CH + CH], r.mt[ch, db, c * CH:c * CH + CH],
                                               xs[ch, db, c, :], start=True, stop=True)
                    mm.then_inc(moved, 1)
                    if n < NT:
                        if n == 0:
                            pe.wait_ge(loaded, 32)
                        if n >= 2:
                            pe.wait_ge(gate_kept, n - 1)
                        pe.matmul(gps[:, n % 2, 0:B_W], g.fm[:, 6, n * P:(n + 1) * P], gup[:, :], start=True, stop=True).then_inc(gated, 1)
                pe.wait_ge(stepped, 2 * (NCH - 1))
                for t in range(NT):
                    if t >= 2:
                        pe.wait_ge(added, t - 1)
                    for h in range(B_HEADS):
                        for ck in range(2):
                            for d in range(2):
                                ch, db, c = slice((h % 2) * 64, (h % 2) * 64 + 64), 2 * d + h // 2, 2 * t + ck
                                mm = pe.matmul(yps[ck * 64:ck * 64 + 64, t % 2, h % 2, (h // 2) * HD:(h // 2) * HD + HD],
                                               r.pt[ch, db, c * CH:c * CH + CH], xs[ch, db, c, :], start=(d == 0), stop=(d == 1))
                    mm.then_inc(read, 1)
                for t in range(NT):
                    pe.wait_ge(done, t + 1)
                    if t >= 2:
                        pe.wait_ge(kept, t - 1)
                    for j in range(2):
                        mm = pe.transpose(tps[:, t % 2, j * P:(j + 1) * P], r.yl[:, t, j * P:(j + 1) * P], g.ident)
                    mm.then_inc(turned, 1)

            @block.gpsimd
            def _(pool):
                vbf = g.vb[:, :, :]
                vbh = vbf.rearrange("p t (h n) -> p (t h) n", h=B_HEADS)
                link = Link(pool, folds)
                link(pool.tensor_tensor(vbh, vbh, spread(r.bonus[:, :, :].rearrange("p t h -> p (t h)"), 2, HD), ALU.mult))
                pool.wait_ge(loaded, 32)
                link(pool.tensor_tensor(vbf, vbf, spread(ln[:, 1, :], 1, NT), ALU.add))
                pool.wait_ge(gate_kept, NT)
                link(pool.tensor_tensor(vbf, vbf, gate[:, :, :], ALU.mult))
                link(pool.tensor_tensor(gate[:, :, :], gate[:, :, :], spread(ln[:, 0, :], 1, NT), ALU.mult))

            @block.scalar
            def _(act):
                for t in range(NT):
                    act.wait_ge(gated, t + 1)
                    act.activation(gate[:, t, :], gps[:, t % 2, 0:B_W], ACT.Copy).then_inc(gate_kept, 1)
                act.wait_ge(var, 1)
                act.activation(st[:, 2, :], st[:, 1, :], ACT.Sqrt).then_inc(root, 1)
                for t in range(NT):
                    act.wait_ge(turned, t + 1)
                    act.activation(g.mixT[:, 4:6, t * P:(t + 1) * P], tps[:, t % 2, 0:2 * P].rearrange("p (j n) -> p j n", j=2),
                                   ACT.Copy).then_inc(kept, 1)

            @block.vector
            def _(dve):
                link = Link(dve, chain)
                for d in range(2):
                    dve.memset(xs[:, 2 * d:2 * d + 2, order[d][0], :], 0.0).then_inc(zeroed, 1)
                for n in range(NCH - 1):
                    dve.wait_ge(moved, n + 1)
                    for d in range(2):
                        c, nxt, q = order[d][n], order[d][n + 1], slice(2 * d, 2 * d + 2)
                        dve.tensor_tensor(xs[:, q, nxt, :], sps[:, n % 2, 128 * d:128 * d + 128].rearrange("p (b n) -> p b n", b=2),
                                          r.hh[:, q, c * CH:c * CH + CH], ALU.add).then_inc(stepped, 1)
                def heads(v, t):
                    return v[:, t * B_HEADS:(t + 1) * B_HEADS]

                for t in range(NT):
                    dve.wait_ge(read, t + 1)
                    yt = r.yl[:, t, :].rearrange("p (b a n) -> p a b n", b=2, a=2)
                    dve.tensor_tensor(yt, yt, yps[:, t % 2, :, 0:P].rearrange("p a (b n) -> p a b n", b=2),
                                      ALU.add).then_inc(added, 1)
                    dve.wait_ge(added, t + 1)
                    mean, var_t = heads(st[:, 0, :], t), heads(st[:, 1, :], t)
                    yth, sq = yh[:, t * B_HEADS:(t + 1) * B_HEADS, :], tmp[:, t * B_HEADS:(t + 1) * B_HEADS, :]
                    link(dve.tensor_reduce(mean, yth, AX_X, ALU.add))
                    link(dve.tensor_scalar(mean, mean, 1.0 / HD, None, ALU.mult))
                    link(dve.tensor_tensor(yth, yth, spread(mean, 2, HD), ALU.subtract))
                    link(dve.tensor_tensor(sq, yth, yth, ALU.mult))
                    link(dve.tensor_reduce(var_t, sq, AX_X, ALU.add))
                dve.tensor_scalar(st[:, 1, :], st[:, 1, :], 1.0 / HD, LNX_EPS, ALU.mult, ALU.add).then_inc(var, 1)
                dve.wait_ge(root, 1)
                link(dve.reciprocal(st[:, 3, :], st[:, 2, :]))
                dve.wait_ge(folds, 4)
                for t in range(NT):
                    yth = yh[:, t * B_HEADS:(t + 1) * B_HEADS, :]
                    link(dve.tensor_tensor(yth, yth, spread(heads(st[:, 3, :], t), 2, HD), ALU.mult))
                    link(dve.tensor_tensor(yf[:, t, :], yf[:, t, :], gate[:, t, :], ALU.mult))
                    dve.tensor_tensor(yf[:, t, :], yf[:, t, :], g.vb[:, t, :], ALU.add).then_inc(done, 1)


def rwkv(nc, g, right, layer):
    with ExitStack() as stack:
        a, r = Scope(nc, stack), Buffers()
        r.cs = g.fm[:, 7:11, :]
        r.yl = a.sb("rk_yl", [P, NT, B_W])
        r.bonus = a.sb("rk_bonus", [P, NT, B_HEADS])
        r.pt, r.mt, r.hh = (a.sb("rk_" + n, [P, 4, T]) for n in ("pt", "mt", "hh"))
        with ExitStack() as chunks:
            c = Scope(nc, chunks)
            r.xc, r.b, r.kd = (c.sb("rk_" + n, [P, 4, T]) for n in ("xc", "b", "kd"))
            r.nkk = c.sb("rk_nkk", [P, 2, T])
            rwkv_gates(nc, g, r, layer)
            rwkv_chunks(nc, g, r, layer)
        g.w_out_sb, g.mo_gate = right.sb("mo_w", [P, KD, D]), right.sb("mo_gate", [P, 2, D])
        g.w_out_loaded = g.sem("mo_w_loaded")
        rwkv_readout(nc, g, r, layer)




def mix_out(nc, g, f, layer):
    order = list(range(NTC, NT)) + list(range(NTC))
    nl = NT - NTC
    w, gate = g.w_out_sb, g.mo_gate
    with ExitStack() as stack:
        a = Scope(nc, stack)
        x, z = f.h, a.sb("mo_z", [P, 2, D])
        w_hi, w_lo = (a.sb("mo_w" + n, [P, KD, D], F32R) for n in ("_hi", "_lo"))
        m_hi, m_lo = (a.sb("mo_mix" + n, [P, 2, KD, P], F32R) for n in ("_hi", "_lo"))
        junk, junk2, st = a.sb("mo_junk", [P, D]), a.sb("mo_junk2", [P, D]), a.sb("mo_st", [P, 4, NT])
        ps = a.ps("mo_ps", [P, 3, D])
        names = ("m_hi", "m_lo", "w_hi", "w_lo", "made", "squared", "var", "root", "inv", "scaled", "added", "stored",
                 "stored_ctx", "next_squared", "next_var", "next_root", "rows_loaded")
        s = Buffers()
        (s.m_hi, s.m_lo, s.w_hi, s.w_lo, s.made, s.squared, s.var, s.root, s.inv, s.scaled, s.added, s.stored,
         s.stored_ctx, s.next_squared, s.next_var, s.next_root,
         s.rows_loaded) = (g.sem("mo_" + n) for n in names)
        x_loaded = [g.sem(f"mo_x_loaded{t}") for t in range(NT)]

        def tiles(eng, body, begin=0):
            for n in range(begin, nl):
                body(n, order[n])
            with eng.If(layer < DEPTH - 1):
                for n in range(nl, NT):
                    body(n, order[n])

        with nc.Block(no_gpsimd_drain=True) as block:

            @block.sync
            def _(sync):
                for t in order:
                    sync.dma_start(x[:, t, :], g.stream[t * P:(t + 1) * P, :]).then_inc(x_loaded[t], 16)

                def body(n, t):
                    sync.wait_ge(s.added, n + 1)
                    sync.dma_start(g.stream[t * P:(t + 1) * P, :], x[:, t, :]).then_inc(s.stored if n < nl else s.stored_ctx, 16)

                load_mod_rows(sync, g, f.gain, 4, s.rows_loaded)
                load_mod_rows(sync, g, f.shift, 3, s.rows_loaded)
                sync.dma_start(f.wr[:, :, :], at(g.w_router, layer).rearrange("(k p) n -> p k n", p=P)).then_inc(s.rows_loaded, 16)
                tiles(sync, body)
                sync.wait_ge(s.rows_loaded, 80)
                sync.wait_ge(s.stored, 16 * nl)
                with sync.If(layer < DEPTH - 1):
                    sync.wait_ge(s.stored_ctx, 16 * NTC)

            @block.tensor
            def _(pe):
                def part(n, k):
                    for half in range(2):
                        cols = slice(half * 512, half * 512 + 512)
                        for i, (m, wk) in enumerate(((m_hi, w_hi), (m_lo, w_hi), (m_hi, w_lo))):
                            mm = pe.matmul(ps[:, n % 3, cols], m[:, n % 2, k, :], wk[:, k, cols],
                                           start=(k == 0 and i == 0), stop=(k == KD - 1 and i == 2))
                    if k == KD - 1:
                        mm.then_inc(s.made, 1)

                pe.wait_ge(s.m_lo, 2)
                for q in range(4):
                    pe.wait_ge(s.w_lo, q + 1)
                    for n in range(2):
                        part(n, 2 * q)
                        part(n, 2 * q + 1)

                def body(n, t):
                    pe.wait_ge(s.m_lo, n + 1)
                    if n >= 3:
                        pe.wait_ge(s.scaled, n - 2)
                    for k in range(KD):
                        part(n, k)

                tiles(pe, body, 2)

            @block.scalar
            def _(act):
                def high(n):
                    t = order[n]
                    act.activation(m_hi[:, n % 2, :, :], g.mixT[:, :, t * P:(t + 1) * P], ACT.Copy).then_inc(s.m_hi, 1)

                high(0)
                act.wait_ge(g.w_out_loaded, 16)
                act.activation(w_hi[:, 0:2, :], w[:, 0:2, :], ACT.Copy).then_inc(s.w_hi, 1)
                high(1)
                for q in range(1, 4):
                    act.activation(w_hi[:, 2 * q:2 * q + 2, :], w[:, 2 * q:2 * q + 2, :], ACT.Copy).then_inc(s.w_hi, 1)

                def body(n, t):
                    act.wait_ge(s.made, n + 1)
                    if n + 2 < nl:
                        high(n + 2)
                    if n:
                        act.wait_ge(s.squared, n)
                    act.activation(junk[:, :], ps[:, n % 3, :], ACT.Square, accum_out=st[:, 0, n:n + 1]).then_inc(s.squared, 1)
                    act.wait_ge(s.var, n + 1)
                    act.activation(st[:, 2, n:n + 1], st[:, 1, n:n + 1], ACT.Sqrt).then_inc(s.root, 1)
                    if 1 <= n < nl:
                        square_next(n - 1)

                def square_next(n):
                    t = order[n]
                    act.wait_ge(x_loaded[t], 16)
                    if n < nl:
                        act.wait_ge(s.added, n + 1)
                    if n:
                        act.wait_ge(s.next_squared, n)
                    act.activation(junk2[:, :], x[:, t, :], ACT.Square, accum_out=f.st[:, t:t + 1]).then_inc(s.next_squared, 1)

                for n in range(nl):
                    body(n, order[n])
                with act.If(layer < DEPTH - 1):
                    high(nl)
                    high(nl + 1)
                    body(nl, order[nl])
                    body(nl + 1, order[nl + 1])
                    act.wait_ge(s.added, NT)
                for n in range(nl - 1, NT):
                    square_next(n)
                act.wait_ge(s.next_var, 1)
                act.activation(f.st[:, 8:8 + NT], f.st[:, 8:8 + NT], ACT.Sqrt).then_inc(s.next_root, 1)

            @block.vector
            def _(dve):
                def low(n):
                    t = order[n]
                    dve.wait_ge(s.m_hi, n + 1)
                    dve.tensor_tensor(m_lo[:, n % 2, :, :], g.mixT[:, :, t * P:(t + 1) * P],
                                      m_hi[:, n % 2, :, :].bitcast(F32), ALU.subtract).then_inc(s.m_lo, 1)

                def low_w(q):
                    dve.wait_ge(s.w_hi, q + 1)
                    k = slice(2 * q, 2 * q + 2)
                    dve.tensor_tensor(w_lo[:, k, :], w[:, k, :], w_hi[:, k, :].bitcast(F32), ALU.subtract).then_inc(s.w_lo, 1)

                low(0)
                low_w(0)
                low(1)
                for q in range(1, 4):
                    low_w(q)

                def body(n, t):
                    if n + 2 < nl:
                        low(n + 2)
                    elif n == nl:
                        low(nl)
                        low(nl + 1)
                    dve.wait_ge(s.squared, n + 1)
                    dve.tensor_scalar(st[:, 1, n:n + 1], st[:, 0, n:n + 1], 1.0 / D, EPS, ALU.mult, ALU.add).then_inc(s.var, 1)
                    dve.wait_ge(s.root, n + 1)
                    dve.reciprocal(st[:, 3, n:n + 1], st[:, 2, n:n + 1]).then_inc(s.inv, 1)
                    dve.wait_ge(s.inv, n + 1)
                    if n >= 2:
                        dve.wait_ge(s.added, n - 1)
                    dve.scalar_tensor_tensor(z[:, n % 2, :], ps[:, n % 3, :], st[:, 3, n:n + 1], gate[:, int(t >= NTC), :],
                                             ALU.mult, ALU.mult).then_inc(s.scaled, 1)

                tiles(dve, body)
                dve.wait_ge(s.next_squared, NT)
                dve.tensor_scalar(f.st[:, 8:8 + NT], f.st[:, 0:NT], 1.0 / D, EPS, ALU.mult, ALU.add).then_inc(s.next_var, 1)
                dve.wait_ge(s.next_root, 1)
                dve.reciprocal(f.st[:, 16:16 + NT], f.st[:, 8:8 + NT])

            @block.gpsimd
            def _(pool):
                def body(n, t):
                    pool.wait_ge(s.scaled, n + 1)
                    pool.wait_ge(x_loaded[t], 16)
                    pool.tensor_tensor(x[:, t, :], x[:, t, :], z[:, n % 2, :], ALU.add).then_inc(s.added, 1)

                tiles(pool, body)



RAW_SLOTS, HI_SLOTS = 4, 4
PARTS = 24
POOLED = (3, 5, 7, 11, 15, 19, 23)


def expert_part(g, layer, pair, n):
    kind, e = ((g.w_gate_e, 0), (g.w_up_e, 0), (g.w_gate_e, 1), (g.w_up_e, 1), (g.w_down_e, 0), (g.w_down_e, 1))[n // 4]
    q = n % 4
    return at(at(kind, layer), pair * 2 + e).rearrange("(p k) n -> p k n", k=KD)[:, 2 * q:2 * q + 2, :]


def routing(nc, g, f, layer):
    with ExitStack() as stack:
        a = Scope(nc, stack)
        hT, wr = a.sb("rt_hT", [P, 2, KD, P]), f.wr
        lg, sm = a.sb("rt_lg", [P, NT, NE]), a.sb("rt_sm", [P, 3, NT])
        affT, work, sel, rank = (a.sb("rt_" + n, [NE, T]) for n in ("affT", "work", "sel", "rank"))
        ones, best = a.sb("rt_ones", [NE, SEQ]), a.sb("rt_best", [NE, 8])
        tp = a.ps("rt_tp", [P, 2, 4, P])
        lps = a.ps("rt_lps", [P, NT, NE])
        aps = a.ps("rt_aps", [NE, 1024])
        sps = a.ps("rt_sps", [P, NT, NE])
        norm = PreNorm(g, "rt", f.h, f.h, f.gain, f.shift, None, f.st)
        turned, hT_ready = g.sem("rt_turned"), g.sem("rt_hT_ready")
        routed, chain, centred, exped = g.sem("rt_routed"), g.sem("rt_chain"), g.sem("rt_centred"), g.sem("rt_exped")
        zeroed = g.sem("rt_zeroed")
        aff_ready, aff_turned = g.sem("rt_aff_ready"), g.sem("rt_aff_turned")
        slots_ready, slots_turned = g.sem("rt_slots_ready"), g.sem("rt_slots_turned")
        lgf = lg[:, :, :]
        with nc.Block(no_gpsimd_drain=True) as block:

            @block.sync
            def _(sync):
                for n in range(RAW_SLOTS):
                    sync.dma_start(f.w_raw[:, n, :, :], expert_part(g, layer, 0, n)).then_inc(f.w_loaded[n], 16)

            @block.scalar
            def _(act):
                for n in range(2 * NT):
                    act.wait_ge(turned, n + 1)
                    t, half = n // 2, n % 2
                    if t >= 2:
                        act.wait_ge(routed, t - 1)
                    act.activation(hT[:, t % 2, 4 * half:4 * half + 4, :], tp[:, half, :, :], ACT.Copy).then_inc(hT_ready, 1)
                act.wait_ge(centred, 1)
                act.activation(lgf, lgf, ACT.Exp).then_inc(exped, 1)

            @block.gpsimd
            def _(pool):
                norm.gpsimd(pool)
                pool.memset(f.acc[:, :, :], 0.0).then_inc(zeroed, 1)
                pool.wait_ge(zeroed, 1)

            @block.tensor
            def _(pe):
                def route(t):
                    pe.wait_ge(hT_ready, 2 * t + 2)
                    for k in range(KD):
                        mm = pe.matmul(lps[:, t, :], hT[:, t % 2, k, :], wr[:, k, :], start=(k == 0), stop=(k == KD - 1))
                    mm.then_inc(routed, 1)

                for t in range(NT):
                    pe.wait_ge(norm.shifted, t + 1)
                    for half in range(2):
                        if t:
                            pe.wait_ge(hT_ready, 2 * t - 1 + half)
                        for j in range(4):
                            k = 4 * half + j
                            mm = pe.transpose(tp[:, half, j, :], f.h[:, t, k * P:(k + 1) * P], g.ident)
                        mm.then_inc(turned, 1)
                    if t:
                        route(t - 1)
                route(NT - 1)
                pe.wait_ge(aff_ready, 1)
                for t in range(NT):
                    mm = pe.transpose(aps[:, t * P:(t + 1) * P], f.aff[:, t, 0:NE], g.ident)
                mm.then_inc(aff_turned, 1)
                pe.wait_ge(slots_ready, 1)
                for t in range(NT):
                    mm = pe.transpose(sps[:, t, :], rank[:, t * P:(t + 1) * P], g.cst[0:NE, O_ID:O_ID + NE])
                mm.then_inc(slots_turned, 1)

            @block.vector
            def _(dve):
                link = Link(dve, chain)
                norm.vector(dve)
                link(dve.memset(ones[:, :], 1.0))
                dve.wait_ge(routed, NT)
                link(dve.tensor_reduce(sm[:, 0, :], lps[:, :, :], AX_X, ALU.max))
                dve.tensor_tensor(lgf, lps[:, :, :], spread(sm[:, 0, :], 2, NE), ALU.subtract).then_inc(centred, 1)
                dve.wait_ge(exped, 1)
                link(dve.tensor_reduce(sm[:, 1, :], lgf, AX_X, ALU.add))
                link(dve.reciprocal(sm[:, 2, :], sm[:, 1, :]))
                dve.tensor_tensor(f.aff[:, :, 0:NE], lgf, spread(sm[:, 2, :], 2, NE), ALU.mult).then_inc(aff_ready, 1)
                dve.wait_ge(aff_turned, 1)
                link(dve.tensor_copy(work[:, :], aps[:, 0:T]))
                for lo, hi, cap in ((0, CTX, CAP_C), (CTX, T, CAP_L)):
                    for _ in range(cap // 8):
                        link(dve.max(best[:, :], work[:, lo:hi]))
                        link(dve.match_replace(work[:, lo:hi], best[:, :], work[:, lo:hi], -1.0))
                link(dve.tensor_scalar(sel[:, :], work[:, :], 0.0, None, ALU.is_lt))
                for lo, hi in ((0, CTX), (CTX, T)):
                    link(dve.tensor_tensor_scan(rank[:, lo:hi], ones[:, 0:hi - lo], sel[:, lo:hi], 0.0, ALU.mult, ALU.add))
                link(dve.tensor_tensor(rank[:, :], rank[:, :], sel[:, :], ALU.mult))
                dve.tensor_scalar(rank[:, :], rank[:, :], 1.0, None, ALU.subtract).then_inc(slots_ready, 1)
                link(dve.memset(f.slot[:, :, NE:NE + 2], -1.0))
                link(dve.memset(f.aff[:, :, NE:NE + 2], 0.0))
                dve.wait_ge(slots_turned, 1)
                dve.tensor_copy(f.slot[:, :, 0:NE], sps[:, :, :])



U_GATHER, U_PICK, U_HID, U_SCATTER = 4, 2, 2, 12
NTL = NT - NTC


def experts(nc, g, f, layer):
    first_uses = U_GATHER + U_PICK + 2 * U_HID + U_GATHER
    uses = U_SCATTER + U_PICK + 2 * U_HID + U_GATHER
    with ExitStack() as stack:
        a = Scope(nc, stack)
        pick_l, pick_c = a.sb("ex_pick_l", [P, NTL, 2, CAP_L]), a.sb("ex_pick_c", [P, NTC, 2, CAP_C])
        pickT_l, pickT_c = a.sb("ex_pickT_l", [P, NTL * P], F32R), a.sb("ex_pickT_c", [2 * CAP_C, NTC * P], F32R)
        aff_now = a.sb("ex_aff_now", [P, NT, 2])
        weight = a.sb("ex_weight", [CAP, 4])
        xe_hi, xe_lo = a.sb("ex_xe_hi", [P, KD, 2, CAP], F32R), a.sb("ex_xe_lo", [P, KD, 2, CAP], F32R)
        sg, hid = a.sb("ex_sg", [CAP, DE]), a.sb("ex_hid", [CAP, DE])
        hidT_hi, hidT_lo = a.sb("ex_hidT_hi", [P, KD, CAP], F32R), a.sb("ex_hidT_lo", [P, KD, CAP], F32R)
        ye_l, ye_c = a.sb("ex_ye_l", [P, D]), a.sb("ex_ye_c", [2 * CAP_C, D])
        ye_hi_l, ye_hi_c = a.sb("ex_ye_hi_l", [P, D], F32R), a.sb("ex_ye_hi_c", [2 * CAP_C, D], F32R)
        ye_lo_l, ye_lo_c = a.sb("ex_ye_lo_l", [P, D], F32R), a.sb("ex_ye_lo_c", [2 * CAP_C, D], F32R)
        misc = a.ps("ex_misc", [P, 2, 512])
        gp, up, yp = (a.ps("ex_" + n, [CAP, 2, 512]) for n in ("gp", "up", "yp"))
        names = ("picked", "used", "free", "hi", "lo_v", "lo_p", "w_used", "silu", "hid", "kept", "ye_hi", "ye_lo")
        s = Buffers()
        (s.picked, s.used, s.free, s.hi, s.lo_v, s.lo_p, s.w_used, s.silu, s.hid, s.kept, s.ye_hi,
         s.ye_lo) = (g.sem("ex_" + n) for n in names)

        def start(j, peeled):
            return U_GATHER if peeled else (j - 1) * uses + first_uses

        def layout_uses(peeled):
            at_, order = {}, ([] if peeled else ["scatter"] * U_SCATTER) + ["pick"] * U_PICK + ["hid0"] * U_HID + \
                ["hid1"] * U_HID + ["gather"] * U_GATHER
            for n, what in enumerate(order):
                at_.setdefault(what, n)
            return at_

        scatter_places = [(t, half) for t in range(NT) for half in range(2)]

        def both(eng, body):
            body(0, True)
            with eng.Fori(1, NE // 2) as j:
                body(j, False)

        def low_made(eng, j, n):
            pooled = sum(m in POOLED for m in range(n + 1))
            if n in POOLED:
                eng.wait_ge(s.lo_p, j * len(POOLED) + pooled)
            else:
                eng.wait_ge(s.lo_v, j * (PARTS - len(POOLED)) + n + 1 - pooled)

        def take(pe, m):
            if not (isinstance(m, int) and m < 2):
                pe.wait_ge(s.free, m - 1)

        with nc.Block(no_gpsimd_drain=True) as block:

            @block.sync
            def _(sync):
                def body(j, peeled):
                    for n in range(PARTS):
                        if peeled and n < RAW_SLOTS:
                            continue
                        if n >= RAW_SLOTS:
                            low_made(sync, j, n - RAW_SLOTS)
                        else:
                            low_made(sync, j - 1, n - RAW_SLOTS + PARTS)
                        sync.dma_start(f.w_raw[:, n % RAW_SLOTS, :, :],
                                       expert_part(g, layer, j, n)).then_inc(f.w_loaded[n % RAW_SLOTS], 16)

                both(sync, body)
                sync.wait_ge(s.used, start(NE // 2, False))
                for t in range(NT):
                    sync.dma_start(f.h[:, t, :], g.stream[t * P:(t + 1) * P, :]).then_inc(f.x_loaded[t], 16)

            @block.tensor
            def _(pe):
                def part(j, peeled, n, hi, lo, out):
                    pe.wait_ge(s.hi, j * PARTS + n + 1)
                    w_hi, w_lo = f.w_hi[:, n % HI_SLOTS, :, :], f.w_lo[:, n % HI_SLOTS, :, :]
                    q = n % 4
                    for i in range(2):
                        for half in range(2):
                            cols = slice(half * 512, half * 512 + 512)
                            pe.matmul(out[:, half, :], hi(2 * q + i), w_hi[:, i, cols], start=(q == 0 and i == 0), stop=False)
                            pe.matmul(out[:, half, :], lo(2 * q + i), w_hi[:, i, cols], start=False, stop=False)
                    low_made(pe, j, n)
                    for i in range(2):
                        for half in range(2):
                            cols = slice(half * 512, half * 512 + 512)
                            mm = pe.matmul(out[:, half, :], hi(2 * q + i), w_lo[:, i, cols], start=False, stop=(q == 3 and i == 1))
                    mm.then_inc(s.w_used, 1)

                def gate_up(j, peeled, n):
                    e, out, read = n // 8, *((gp, s.silu), (up, s.hid))[n // 4 % 2]
                    if n % 4 == 0 and not (peeled and e == 0):
                        pe.wait_ge(read, j * 4 + e * 2)
                    part(j, peeled, n, lambda k: xe_hi[:, k, e, :], lambda k: xe_lo[:, k, e, :], out)

                def down(j, peeled, e, hidT_free):
                    pe.wait_ge(s.free, hidT_free)
                    if not (peeled and e == 0):
                        pe.wait_ge(s.kept, j * 4 + e * 2)
                    for n in range(16 + 4 * e, 20 + 4 * e):
                        part(j, peeled, n, lambda k: hidT_hi[:, k, :], lambda k: hidT_lo[:, k, :], yp)

                def turn_hid(j, e, m0):
                    pe.wait_ge(s.hid, j * 4 + e * 2 + 2)
                    for n in range(2):
                        take(pe, m0 + n)
                        for i in range(4):
                            k = 4 * n + i
                            mm = pe.transpose(misc[:, n, i * CAP:(i + 1) * CAP], hid[:, k:DE:KD], g.cst[0:CAP, O_ID:O_ID + CAP])
                        mm.then_inc(s.used, 1)

                def gather(picked, m0):
                    pe.wait_ge(s.picked, picked)
                    for n in range(U_GATHER):
                        take(pe, m0 + n)
                        for i in range(2):
                            o = misc[:, n % 2, i * 2 * CAP:(i + 1) * 2 * CAP].rearrange("p (e c) -> p e c", e=2)
                            k = 2 * n + i
                            for t in range(NTL):
                                pe.matmul(o[:, :, 0:CAP_L], f.h[:, NTC + t, k:D:KD], pick_l[:, t, :, :],
                                          start=(t == 0), stop=(t == NTL - 1))
                            for t in range(NTC):
                                mm = pe.matmul(o[:, :, CAP_L:CAP], f.h[:, t, k:D:KD], pick_c[:, t, :, :],
                                               start=(t == 0), stop=(t == NTC - 1))
                        mm.then_inc(s.used, 1)

                def scatter(m0, places):
                    for n in places:
                        t, half = scatter_places[n]
                        take(pe, m0 + n)
                        cols = slice(half * 512, half * 512 + 512)
                        if t < NTC:
                            pick, hi, lo = pickT_c[:, t * P:(t + 1) * P], ye_hi_c, ye_lo_c
                        else:
                            pick, hi, lo = pickT_l[:, (t - NTC) * P:(t - NTC + 1) * P], ye_hi_l, ye_lo_l
                        pe.matmul(misc[:, n % 2, :], pick, hi[:, cols], start=True, stop=False)
                        pe.matmul(misc[:, n % 2, :], pick, lo[:, cols], start=False, stop=True).then_inc(s.used, 1)

                def turn_picks(j, m0):
                    for n in range(2):
                        take(pe, m0 + n)
                    for t in range(NTL):
                        mm = pe.transpose(misc[:, 0, t * P:(t + 1) * P], pick_l[:, t, :, :].rearrange("p e c -> p (e c)"), g.ident)
                    mm.then_inc(s.used, 1)
                    for t in range(NTC):
                        pe.transpose(misc[0:2 * CAP_C, 1, t * P:(t + 1) * P], pick_c[:, t, :, :].rearrange("p e c -> p (e c)"), g.ident)
                    for e in range(2):
                        w0 = NTC * P + 2 * e
                        for pick, tiles, rows in ((pick_l, range(NTC, NT), slice(0, CAP_L)), (pick_c, range(NTC), slice(CAP_L, CAP))):
                            for t in tiles:
                                mm = pe.matmul(misc[rows, 1, w0:w0 + 2], pick[:, t - tiles[0], e, :], aff_now[:, t, :],
                                               start=(t == tiles[0]), stop=(t == tiles[-1]))
                    mm.then_inc(s.used, 1)

                gather(3, 0)
                pe.wait_ge(s.free, U_GATHER)

                def body(j, peeled):
                    m, where = start(j, peeled), layout_uses(peeled)
                    if not peeled:
                        pe.wait_ge(s.free, m)
                    for n in range(0, 4):
                        gate_up(j, peeled, n)
                    if not peeled:
                        pe.wait_ge(s.ye_lo, j * 2)
                    for n in range(4, 8):
                        if not peeled:
                            scatter(m + where["scatter"], range(3 * n - 12, 3 * n - 9))
                        gate_up(j, peeled, n)
                    turn_picks(j, m + where["pick"])
                    for n in range(8, 16):
                        if n == 10:
                            turn_hid(j, 0, m + where["hid0"])
                        gate_up(j, peeled, n)
                    down(j, peeled, 0, m + where["hid0"] + 2)
                    turn_hid(j, 1, m + where["hid1"])
                    gather(j * 3 + 6, m + where["gather"])
                    down(j, peeled, 1, m + where["hid1"] + 2)

                both(pe, body)
                pe.wait_ge(s.ye_lo, NE)
                scatter(start(NE // 2, False), range(U_SCATTER))

            @block.scalar
            def _(act):
                def high(j, peeled, ns):
                    for n in ns:
                        act.wait_ge(f.w_loaded[n % RAW_SLOTS], j * (16 * PARTS // RAW_SLOTS) + 16 * (n // RAW_SLOTS) + 16)
                        if not (peeled and n < HI_SLOTS):
                            act.wait_ge(s.w_used, j * PARTS + n - HI_SLOTS + 1)
                        act.activation(f.w_hi[:, n % HI_SLOTS, :, :], f.w_raw[:, n % RAW_SLOTS, :, :], ACT.Copy).then_inc(s.hi, 1)

                def silu(j, peeled, e):
                    act.wait_ge(s.w_used, j * PARTS + 8 * e + 4)
                    if not (peeled and e == 0):
                        act.wait_ge(s.hid, j * 4 + e * 2)
                    for half in range(2):
                        act.activation(sg[:, half * 512:half * 512 + 512], gp[:, half, :], ACT.Silu).then_inc(s.silu, 1)

                def keep(j, e):
                    act.wait_ge(s.w_used, j * PARTS + 20 + 4 * e)
                    for rows, dst, cap in ((slice(0, CAP_L), ye_l, CAP_L), (slice(CAP_L, CAP), ye_c, CAP_C)):
                        act.activation(dst[e * cap:(e + 1) * cap, :], yp[rows, :, :].rearrange("p h n -> p (h n)"),
                                       ACT.Copy, scale=weight[rows, 3 * e:3 * e + 1]).then_inc(s.kept, 1)

                def finish(j):
                    keep(j, 1)
                    act.wait_ge(s.kept, j * 4 + 4)
                    act.activation(ye_hi_l[:, :], ye_l[:, :], ACT.Copy).then_inc(s.ye_hi, 1)
                    act.activation(ye_hi_c[:, :], ye_c[:, :], ACT.Copy).then_inc(s.ye_hi, 1)

                def body(j, peeled):
                    high(j, peeled, range(0, 4))
                    if not peeled:
                        finish(j - 1)
                    high(j, peeled, range(4, 8))
                    silu(j, peeled, 0)
                    high(j, peeled, range(8, 16))
                    silu(j, peeled, 1)
                    high(j, peeled, range(16, 24))
                    act.wait_ge(s.free, start(j, peeled) + layout_uses(peeled)["pick"] + 2)
                    keep(j, 0)

                both(act, body)
                finish(NE // 2 - 1)
                for t in range(NT):
                    act.wait_ge(s.free, start(NE // 2, False) + 2 * t + 2)
                    if t:
                        act.wait_ge(f.squared, t)
                    act.activation(ye_l[:, :], f.acc[:, t, :], ACT.Square, accum_out=f.st[:, t:t + 1]).then_inc(f.squared, 1)

            def low(eng, j, ns, on_pool=False):
                for n in ns:
                    if (n in POOLED) != on_pool:
                        continue
                    eng.wait_ge(s.hi, j * PARTS + n + 1)
                    eng.tensor_tensor(f.w_lo[:, n % HI_SLOTS, :, :], f.w_raw[:, n % RAW_SLOTS, :, :], f.w_hi[:, n % HI_SLOTS, :, :].bitcast(F32),
                                      ALU.subtract).then_inc(s.lo_p if on_pool else s.lo_v, 1)

            @block.gpsimd
            def _(pool):
                with pool.Fori(0, NE // 2) as j:
                    low(pool, j, range(PARTS), True)
                pool.wait_ge(s.lo_p, NE // 2 * len(POOLED))

            @block.vector
            def _(dve):
                def pick(j2):
                    iota = g.cst[:, O_IOTA:O_IOTA + CAP_L]
                    dve.tensor_copy(aff_now[:, :, :], f.aff[:, :, ds(j2, 2)]).then_inc(s.picked, 1)
                    for dst, tiles, cap, n in ((pick_l, slice(NTC, NT), CAP_L, NTL), (pick_c, slice(0, NTC), CAP_C, NTC)):
                        dve.tensor_tensor(dst[:, :, :, :], spread(f.slot[:, tiles, ds(j2, 2)], 3, cap),
                                          spread(spread(iota[:, 0:cap], 1, 2), 1, n), ALU.is_equal).then_inc(s.picked, 1)

                def split(hi, lo, src, count):
                    dve.tensor_copy(hi, src).then_inc(f.split, 1)
                    dve.wait_ge(f.split, count + 1)
                    dve.tensor_tensor(lo, src, hi.bitcast(F32), ALU.subtract).then_inc(s.free, 1)

                def gathered(m0, count):
                    for n in range(U_GATHER):
                        dve.wait_ge(s.used, m0 + n + 1)
                        split(*(x[:, 2 * n:2 * n + 2, :, :].rearrange("p k e c -> p (k e c)") for x in (xe_hi, xe_lo)),
                              misc[:, n % 2, 0:4 * CAP], count + n)

                def gated(j, e):
                    dve.wait_ge(s.w_used, j * PARTS + 8 * e + 8)
                    for half in range(2):
                        dve.wait_ge(s.silu, j * 4 + e * 2 + half + 1)
                        c = slice(half * 512, half * 512 + 512)
                        dve.tensor_tensor(hid[:, c], sg[:, c], up[:, half, :], ALU.mult).then_inc(s.hid, 1)

                def hid_turned(e, m0, count):
                    for n in range(2):
                        dve.wait_ge(s.used, m0 + n + 1)
                        split(*(x[:, 4 * n:4 * n + 4, :].rearrange("p k c -> p (k c)") for x in (hidT_hi, hidT_lo)),
                              misc[:, n, 0:4 * CAP], count + n)

                def ye_low(j):
                    for n, (lo, ye, hi) in enumerate(((ye_lo_l, ye_l, ye_hi_l), (ye_lo_c, ye_c, ye_hi_c))):
                        dve.wait_ge(s.ye_hi, j * 2 + n + 1)
                        dve.tensor_tensor(lo[:, :], ye[:, :], hi[:, :].bitcast(F32), ALU.subtract).then_inc(s.ye_lo, 1)

                def scattered(m0, places):
                    for n in places:
                        t, half = scatter_places[n]
                        dve.wait_ge(s.used, m0 + n + 1)
                        acc = f.acc[:, t, half * 512:half * 512 + 512]
                        dve.tensor_tensor(acc, acc, misc[:, n % 2, :], ALU.add).then_inc(s.free, 1)

                pick(0)
                gathered(0, 0)

                def body(j, peeled):
                    m, where = start(j, peeled), layout_uses(peeled)
                    low(dve, j, range(0, 4))
                    if peeled:
                        low(dve, j, range(4, 12))
                    else:
                        ye_low(j - 1)
                        low(dve, j, (4,))
                        for i, n in enumerate((6, 8, 9, 10)):
                            scattered(m + where["scatter"], range(3 * i, 3 * i + 3))
                            low(dve, j, (n,))
                    m0 = m + where["pick"]
                    dve.wait_ge(s.used, m0 + 1)
                    dve.tensor_copy(pickT_l[:, :], misc[:, 0, :]).then_inc(s.free, 1)
                    dve.wait_ge(s.used, m0 + 2)
                    dve.tensor_copy(pickT_c[:, :], misc[0:2 * CAP_C, 1, 0:NTC * P]).then_inc(f.split, 1)
                    dve.tensor_copy(weight[:, :], misc[0:CAP, 1, NTC * P:NTC * P + 4]).then_inc(s.free, 1)
                    gated(j, 0)
                    low(dve, j, (12,))
                    hid_turned(0, m + where["hid0"], j * 9 + U_GATHER + 1)
                    low(dve, j, (13,))
                    pick(j * 2 + 2)
                    low(dve, j, range(14, 20))
                    gated(j, 1)
                    low(dve, j, (20,))
                    hid_turned(1, m + where["hid1"], j * 9 + U_GATHER + 3)
                    low(dve, j, (21,))
                    gathered(m + where["gather"], j * 9 + U_GATHER + 5)
                    low(dve, j, (22,))

                both(dve, body)
                ye_low(NE // 2 - 1)
                scattered(start(NE // 2, False), range(U_SCATTER))


def ffn_out(nc, g, f, layer):
    by_vector = (3, 5)
    order = list(range(NTC, NT)) + list(range(NTC))
    with ExitStack() as stack:
        a = Scope(nc, stack)
        gate, st = a.sb("fo_gate", [P, 2, D]), a.sb("fo_st", [P, 3, NT])
        rows_loaded = [g.sem(f"fo_rows_loaded{s}") for s in range(2)]
        names = ("var", "root", "inv", "scaled", "added_v", "added_p", "stored")
        s = Buffers()
        (s.var, s.root, s.inv, s.scaled, s.added_v, s.added_p, s.stored) = (g.sem("fo_" + n) for n in names)
        with nc.Block(no_gpsimd_drain=True) as block:

            @block.sync
            def _(sync):
                def store(to, tiles):
                    done_v = done_p = 0
                    for t in tiles:
                        if t in by_vector:
                            done_v += 1
                            sync.wait_ge(s.added_v, done_v)
                        else:
                            done_p += 1
                            sync.wait_ge(s.added_p, done_p)
                        sync.dma_start(to(t), f.h[:, t, :]).then_inc(s.stored, 16)
                    sync.wait_ge(s.stored, 16 * len(tiles))

                for i in (1, 0):
                    load_mod_row(sync, g, gate, 5, i, rows_loaded[i])
                with sync.If(layer < DEPTH - 1):
                    store(lambda t: g.stream[t * P:(t + 1) * P, :], order)
                with sync.If(layer == DEPTH - 1):
                    store(lambda t: g.out[0, (t - NTC) * P:(t - NTC + 1) * P, :], order[:NT - NTC])

            @block.scalar
            def _(act):
                act.wait_ge(s.var, 1)
                act.activation(st[:, 1, :], st[:, 0, :], ACT.Sqrt).then_inc(s.root, 1)

            @block.vector
            def _(dve):
                dve.tensor_scalar(st[:, 0, :], f.st[:, 0:NT], 1.0 / D, EPS, ALU.mult, ALU.add).then_inc(s.var, 1)
                dve.wait_ge(s.root, 1)
                dve.reciprocal(st[:, 2, :], st[:, 1, :]).then_inc(s.inv, 1)
                dve.wait_ge(s.inv, 1)
                for n, t in enumerate(order):
                    if n in (0, NT - NTC):
                        dve.wait_ge(rows_loaded[int(t >= NTC)], 16)
                    dve.scalar_tensor_tensor(f.acc[:, t, :], f.acc[:, t, :], st[:, 2, t:t + 1], gate[:, int(t >= NTC), :],
                                             ALU.mult, ALU.mult).then_inc(s.scaled, 1)
                    if t in by_vector:
                        dve.wait_ge(s.scaled, n + 1)
                        dve.wait_ge(f.x_loaded[t], 16)
                        dve.tensor_tensor(f.h[:, t, :], f.h[:, t, :], f.acc[:, t, :], ALU.add).then_inc(s.added_v, 1)

            @block.gpsimd
            def _(pool):
                for n, t in enumerate(order):
                    if t in by_vector:
                        continue
                    pool.wait_ge(s.scaled, n + 1)
                    pool.wait_ge(f.x_loaded[t], 16)
                    pool.tensor_tensor(f.h[:, t, :], f.h[:, t, :], f.acc[:, t, :], ALU.add).then_inc(s.added_p, 1)
                pool.wait_ge(s.added_p, NT - len(by_vector))


def ffn_inputs(nc, a, right):
    f = Buffers()
    f.h, f.st = a.sb("ff_h", [P, NT, D]), a.sb("ff_st", [P, 24])
    f.gain, f.shift, f.wr = right.sb("rt_gain", [P, 2, D]), right.sb("rt_shift", [P, 2, D]), right.sb("rt_wr", [P, KD, NE])
    return f


def ffn(nc, g, f, rows, layer):
    with ExitStack() as stack:
        a = Scope(nc, stack, "right")
        f.acc = a.sb("ff_acc", [P, NT, D])
        f.aff, f.slot = a.sb("ff_aff", [P, NT, NE + 2]), a.sb("ff_slot", [P, NT, NE + 2])
        f.w_raw = a.sb("ff_w_raw", [P, RAW_SLOTS, 2, D])
        f.w_loaded = [g.sem(f"ff_w_loaded{i}") for i in range(RAW_SLOTS)]
        f.split, f.squared = g.sem("ff_split"), g.sem("ff_squared")
        f.x_loaded = [g.sem(f"ff_x_loaded{t}") for t in range(NT)]
        routing(nc, g, f, layer)
        rows.close()
        f.w_hi, f.w_lo = (a.sb("ff_w" + n, [P, HI_SLOTS, 2, D], F32R) for n in ("_hi", "_lo"))
        experts(nc, g, f, layer)
        ffn_out(nc, g, f, layer)


class Shared:

    def __init__(self, nc, stack):
        self.nc, self.stack, self.nums = nc, stack, []

    def sem(self, name):
        s = self.stack.enter_context(self.nc.semaphore(name))
        self.nums.append(s.num)
        return s

    @contextmanager
    def semaphores(self):
        outer, nums = self.stack, self.nums
        with ExitStack() as stack:
            self.stack, self.nums = stack, []
            yield
            first, last = min(self.nums), max(self.nums)
            assert last - first + 1 == len(self.nums)
            self.nc.all_engine_barrier(sems_to_clear=range(first, last + 1))
        self.stack, self.nums = outer, nums


def load_constants(nc, g, c_cols, consts, stream_in):
    loaded, silu_done, g.stream_copied = g.sem("const_loaded"), g.sem("silu_done"), g.sem("stream_copied")
    with nc.Block(no_gpsimd_drain=True) as block:

        @block.sync
        def _(sync):
            sync.dma_start(g.cst[:, :], consts).then_inc(loaded, 16)
            sync.dma_start(g.silu_c[:, :, :], c_cols).then_inc(loaded, 16)
            for i, src in enumerate(stream_in):
                sync.dma_start(g.stream[i * CTX:i * CTX + src.shape[0], :], src).then_inc(g.stream_copied, 16)

        @block.scalar
        def _(act):
            act.wait_ge(loaded, 32)
            act.activation(g.silu_c[:, :, :], g.silu_c[:, :, :], ACT.Silu).then_inc(silu_done, 1)
            act.wait_ge(silu_done, 1)
            act.activation(g.silu_hi[:, :, :], g.silu_c[:, :, :], ACT.Copy).then_inc(silu_done, 1)
            act.wait_ge(silu_done, 2)

        @block.vector
        def _(dve):
            dve.wait_ge(silu_done, 2)
            dve.tensor_tensor(g.silu_lo[:, :, :], g.silu_c[:, :, :], g.silu_hi[:, :, :].bitcast(F32), ALU.subtract)


def mixing(nc, g, right, layer):
    with ExitStack() as stack:
        m = Scope(nc, stack)
        g.vb = m.sb("vb", [P, NT, B_W])
        g.fm = m.sb("fm", [P, 11, T])
        with ExitStack() as attending:
            a = Scope(nc, attending)
            g.qkv = a.sb("qkv", [P, NT, A_W + 2 * A_KVW])
            g.vn = a.sb("vn", [P, NT, C_W])
            with ExitStack() as projecting:
                j = projection_buffers(g, Scope(nc, projecting, "right"))
                modulation(nc, g, j, layer)
                projection(nc, g, j, layer)
            g.mixT = right.sb("mixT", [P, KD, T])
            attention(nc, g, layer)
        rwkv(nc, g, right, layer)


def build(nc, c_cols, consts, rope, x, ctx, w_mod, b_mod, gains, w_in, w_out, cols, rows, bias, w_up, a_up, g_up,
          w_router, w_e_gate, w_e_up, w_e_down, out):
    with ExitStack() as stack:
        g = Shared(nc, stack)
        g.w_mod, g.b_mod, g.gains, g.w_in, g.w_out, g.cols_d, g.rows_d = w_mod, b_mod, gains, w_in, w_out, cols, rows
        g.rope_d, g.bias_d, g.w_up, g.a_up, g.g_up, g.w_router = rope, bias, w_up, a_up, g_up, w_router
        g.w_gate_e, g.w_up_e, g.w_down_e = w_e_gate, w_e_up, w_e_down
        g.out = out
        g.stream = nc.dram_tensor("stream", [T, D], F32).ap()
        g.mod_rows = nc.dram_tensor("mod_rows", [2, 6 * D], F32).ap()
        a = Scope(nc, stack)
        g.cst = a.sb("cst", [P, N_CST])
        g.silu_c = a.sb("silu_c", [P, KD, 2])
        g.silu_hi, g.silu_lo = (a.sb("silu" + n, [P, KD, 2], F32R) for n in ("_hi", "_lo"))
        g.ident = g.cst[:, O_ID:O_ID + P]
        load_constants(nc, g, c_cols, consts, [ctx, x])
        with nc.Fori(0, DEPTH) as layer:
            with ExitStack() as feeding, ExitStack() as rows:
                with g.semaphores(), ExitStack() as mixed:
                    right = Scope(nc, mixed, "right")
                    mixing(nc, g, right, layer)
                    f = ffn_inputs(nc, Scope(nc, feeding), Scope(nc, rows))
                    mix_out(nc, g, f, layer)
                with g.semaphores():
                    ffn(nc, g, f, rows, layer)


def constants():
    cst = np.zeros((P, N_CST), np.float32)
    p, r, c = np.arange(P), np.arange(P) % 64, np.arange(64)
    cst[:, O_ID:O_ID + P] = np.eye(P)
    tri = [r[:, None] < c, r[:, None] <= c, r[:, None] > c, r[:, None] >= c]
    cst[:, O_TRI:O_TRI + 256] = np.concatenate(tri, 1)
    for lv in range(6):
        same = (r[:, None] >> (lv + 1)) == (c >> (lv + 1))
        cst[:, O_LM + 64 * lv:O_LM + 64 * lv + 64] = same & ((r[:, None] >> lv) != (c >> lv))
    cst[:, O_HB:O_HB + P] = (p[:, None] // 64) == (p[None, :] // 64)
    cst[:, O_HS:O_HS + 2] = (p[:, None] // 64) == np.arange(2)
    cst[:, O_IOTA:O_IOTA + 64] = c
    cst[:, O_I64:O_I64 + 64] = r[:, None] == c
    rope = np.zeros((T, 2, HD), np.float32)
    rope[:CTX, 0] = 1.0
    inv = (np.float32(10000.0) ** (-np.arange(16, dtype=np.float32) / np.float32(16))).astype(np.float32)
    for i, pos in enumerate((np.arange(SEQ) // GRID, np.arange(SEQ) % GRID)):
        ang = pos.astype(np.float32)[:, None] * inv[None, :]
        cos, sin = np.cos(ang), np.sin(ang)
        rope[CTX:, 0, 32 * i:32 * i + 32] = np.concatenate([cos, cos], 1)
        rope[CTX:, 1, 32 * i:32 * i + 32] = np.concatenate([-sin, sin], 1)
    return cst, np.ascontiguousarray(rope.reshape(NT, P, 2 * HD).transpose(1, 0, 2))


def bias_layout(rpb):
    rp, c = np.arange(P) // GRID, np.arange(P) % GRID
    m, kc = np.arange(1, RPB_M + 1), np.arange(GRID)
    start = np.clip(c - WIN_COLS // 2, 0, GRID - WIN_COLS)
    row = m[None, :] - rp[:, None]
    col = kc[None, :] - c[:, None] + WIN_COLS - 1
    inside = (kc[None, :] >= start[:, None]) & (kc[None, :] < start[:, None] + WIN_COLS)
    padded = np.full((*rpb.shape[:3], 2 * WIN_COLS), np.float32(NEG))
    padded[..., :2 * WIN_COLS - 1] = rpb
    col = np.where(inside, col, 2 * WIN_COLS - 1)
    laid = padded[:, :, row[:, :, None], col[:, None, :]]
    return np.ascontiguousarray(laid.transpose(0, 2, 1, 3, 4)).reshape(DEPTH, P, C_HEADS * RPB_M * GRID)


def layout(inputs):
    f = {k: np.asarray(v) for k, v in inputs.items()}
    cst, rope = constants()

    def columns(v):
        return v.reshape(DEPTH, -1, P).transpose(0, 2, 1)

    both = np.stack([f["c_ctx"], f["c"][0]], axis=-1)
    arrays = {
        "c_cols": both.reshape(KD, P, 2).transpose(1, 0, 2),
        "consts": cst,
        "rope": rope,
        "x": f["x"][0],
        "ctx": f["ctx"][0],
        "w_mod": f["w_mod"],
        "b_mod": f["b_mod"],
        "gains": np.concatenate([f[n] for n in ("g_pre_mix", "g_post_mix", "g_pre_ffn", "g_post_ffn")], 1),
        "w_in": f["w_in"],
        "w_out": f["w_out"],
        "cols": np.concatenate([columns(f[n]) for n in ("rk_w0", "rk_a0", "rk_k_k", "rk_k_a", "rk_r_k")], 2),
        "rows": np.concatenate([np.tile(f["q_gain"], (1, A_HEADS)), np.tile(f["k_gain"], (1, A_KV)),
                                f["rk_lnx_w"], f["rk_lnx_b"]], 1),
        "bias": bias_layout(f["rpb"]),
        "w_up": f["rk_w_up"].reshape(DEPTH, P, B_W),
        "a_up": f["rk_a_up"].reshape(DEPTH, P, B_W),
        "g_up": f["rk_g_up"],
        "w_router": f["w_router"],
        "w_e_gate": f["w_e_gate"],
        "w_e_up": f["w_e_up"],
        "w_e_down": f["w_e_down"],
    }
    return {k: np.ascontiguousarray(v) for k, v in arrays.items()}


def kernel(**inputs):
    import concourse.bacc as bacc
    from concourse.bass_utils import run_bass_kernel_spmd

    nc = bacc.Bacc("TRN2", target_bir_lowering=False, num_devices=1)
    arrays = layout(inputs)
    args = {n: nc.dram_tensor(n, v.shape, mybir.dt.from_np(v.dtype), kind="ExternalInput").ap() for n, v in arrays.items()}
    out = nc.dram_tensor("out", (1, SEQ, D), F32, kind="ExternalOutput").ap()
    build(nc, **args, out=out)
    r = run_bass_kernel_spmd(nc, [arrays], core_ids=[0])
    return r.results[0]["out"]
```
